# Optimizing a Trainium2 kernel written in Bass

```python
import jax, jax.numpy as jnp
from jax import lax
import numpy as np

D_MODEL = 1024
BATCH = 1
SEQ = 256
DEPTH = 2

GRID_W = 64
CTX_LEN = 256
D_MIX = D_MODEL
EPS = 1e-6
LB_FLOOR = 1e-30
NEG_BIG = -1e4
A_HEADS = 4
A_HD = 64
A_WIDTH = A_HEADS * A_HD
CHUNK = 64
B_GROUPS = 4
B_WIDTH = D_MIX // 4
B_GW = B_WIDTH // B_GROUPS
POOL_WINDOWS = (2, 4, 8, 16)
C_HEADS = 8
C_KV_HEADS = 2
C_HD = 64
C_WIDTH = C_HEADS * C_HD
C_KV_WIDTH = C_KV_HEADS * C_HD
Q_BLOCK = 128
ROPE_THETA = 10000.0
N_EXPERTS = 16
N_GROUPS = 4
E_PER_GROUP = N_EXPERTS // N_GROUPS
TOP_K = 2
D_EXPERT = D_MODEL // 2
IN_SIZES = (A_WIDTH, A_WIDTH, A_WIDTH, A_WIDTH, A_WIDTH, B_WIDTH, C_WIDTH, C_KV_WIDTH, C_KV_WIDTH)
IN_COLS = 5 * A_WIDTH + B_WIDTH + C_WIDTH + 2 * C_KV_WIDTH

kernel_name = "hybrid_hgrn2_pool_gqa_grouped_moe_dit"

def rms_norm(x, g):
    xf = x.astype(jnp.float32)
    y = xf * lax.rsqrt(jnp.mean(xf * xf, axis=-1, keepdims=True) + EPS)
    return (y * g.astype(jnp.float32)).astype(x.dtype)

def modulate(h, shift, scale):
    return h * (1 + scale) + shift

def split_in(a):
    outs, off = [], 0
    for s in IN_SIZES:
        outs.append(a[..., off:off + s])
        off += s
    return outs

def axial_rope_tables(T):
    rows_n = T // GRID_W
    row = jnp.repeat(jnp.arange(rows_n), GRID_W).astype(jnp.float32)
    col = jnp.tile(jnp.arange(GRID_W), rows_n).astype(jnp.float32)
    n_freq = C_HD // 4
    inv = ROPE_THETA ** (-jnp.arange(n_freq, dtype=jnp.float32) / n_freq)
    ang = jnp.concatenate([row[:, None] * inv, col[:, None] * inv], axis=-1)
    return jnp.cos(ang), jnp.sin(ang)

def apply_rope(x, cos, sin):
    xf = x.astype(jnp.float32).reshape(*x.shape[:-1], C_HD // 2, 2)
    x1, x2 = xf[..., 0], xf[..., 1]
    cs, sn = cos[None, :, None, :], sin[None, :, None, :]
    out = jnp.stack([x1 * cs - x2 * sn, x1 * sn + x2 * cs], axis=-1)
    return out.reshape(x.shape).astype(x.dtype)

def to_heads(a):
    B, T, _ = a.shape
    return a.astype(jnp.float32).reshape(B, T, A_HEADS, A_HD).transpose(0, 2, 1, 3)

def log_forget(z, lb):
    lbf = jnp.maximum(lb, LB_FLOOR)
    return jnp.logaddexp(jnp.log(lbf), jnp.log1p(-lbf) + jax.nn.log_sigmoid(z))

def gated_chunk_scan(q, k, v, logf, s0):
    B, H, T, dk = q.shape
    n = T // CHUNK

    def chunks(a):
        return a.reshape(B, H, n, CHUNK, a.shape[-1]).transpose(2, 0, 1, 3, 4)

    causal_in_chunk = jnp.tril(jnp.ones((CHUNK, CHUNK), dtype=bool))[:, :, None]
    causal_f = causal_in_chunk.astype(jnp.float32)

    def step(S, inp):
        qc, kc, vc, lc = inp
        b = jnp.cumsum(lc, axis=2)
        o_inter = jnp.einsum('bhtk,bhkv->bhtv', qc * jnp.exp(b), S)
        diff = b[:, :, :, None, :] - b[:, :, None, :, :]
        decay = jnp.exp(jnp.where(causal_in_chunk, diff, 0.0)) * causal_f
        att = jnp.einsum('bhtk,bhtsk,bhsk->bhts', qc, decay, kc)
        o = o_inter + jnp.einsum('bhts,bhsv->bhtv', att, vc)
        b_last = b[:, :, -1:, :]
        S_new = jnp.exp(b_last[:, :, 0, :])[..., None] * S + jnp.einsum(
            'bhsk,bhsv->bhkv', kc * jnp.exp(b_last - b), vc)
        return S_new, o

    S, o = lax.scan(step, s0, (chunks(q), chunks(k), chunks(v), chunks(logf)))
    return o.transpose(1, 2, 0, 3, 4).reshape(B, H, T, v.shape[-1]), S

def flip_seq(a, rev):
    return a[:, :, ::-1] if rev else a

def hgrn2_mixer(lat, ctx, lb, norm_g, need_ctx):
    def prep(qz, ffz, fbz, iz):
        q = jax.nn.silu(to_heads(qz))
        v = to_heads(iz)
        logfs = [log_forget(to_heads(fz), lb[d].reshape(A_HEADS, 1, A_HD))
                 for d, fz in enumerate((ffz, fbz))]
        return q, v, logfs

    q, v, logfs = prep(*lat[:4])
    qc, vc, logfcs = prep(*ctx[:4])
    B, H, L, _ = qc.shape
    o, oc = 0.0, 0.0
    for d, rev in enumerate((False, True)):
        lf, lfc = logfs[d], logfcs[d]
        s0 = jnp.zeros((B, H, A_HD, A_HD), jnp.float32)
        oc_d, s_ctx = gated_chunk_scan(flip_seq(qc, rev), flip_seq(-jnp.expm1(lfc), rev),
                                       flip_seq(vc, rev), flip_seq(lfc, rev), s0)
        o_d, _ = gated_chunk_scan(flip_seq(q, rev), flip_seq(-jnp.expm1(lf), rev),
                                  flip_seq(v, rev), flip_seq(lf, rev), s_ctx)
        o = o + flip_seq(o_d, rev)
        oc = oc + flip_seq(oc_d, rev)

    def readout(o_, gz):
        Bq, T, _ = gz.shape
        g = jax.nn.silu(gz.astype(jnp.float32)).reshape(Bq, T, A_HEADS, A_HD)
        return (rms_norm(o_.transpose(0, 2, 1, 3), norm_g) * g).reshape(Bq, T, A_WIDTH).astype(gz.dtype)

    return readout(o, lat[4]), (readout(oc, ctx[4]) if need_ctx else None)

def pool_mixer(h, w, scale):
    B, T, _ = h.shape
    hf = h.astype(jnp.float32).reshape(B, T, B_GROUPS, B_GW)
    P = jnp.concatenate([jnp.zeros((B, 1, B_GROUPS, B_GW), jnp.float32), jnp.cumsum(hf, axis=1)], axis=1)
    t = jnp.arange(T)
    outs = []
    for gi, win in enumerate(POOL_WINDOWS):
        lo = jnp.maximum(t - win // 2, 0)
        hi = jnp.minimum(t + win // 2, T)
        cnt = (hi - lo).astype(jnp.float32)
        mean = (P[:, hi, gi] - P[:, lo, gi]) / cnt[None, :, None]
        outs.append(mean - hf[:, :, gi])
    d = jnp.stack(outs, axis=2)
    y = jnp.einsum('btgc,gce->btge', d, w.astype(jnp.float32)).reshape(B, T, B_WIDTH)
    return (y * scale.astype(jnp.float32)).astype(h.dtype)

def attend(qg, k, v):
    s = jnp.einsum('bhgqd,bhsd->bhgqs', qg, k).astype(jnp.float32) * (C_HD ** -0.5)
    p = jax.nn.softmax(s, axis=-1).astype(v.dtype)
    return jnp.einsum('bhgqs,bhsd->bhgqd', p, v)

def gqa_mixer(q, k, v, qc, kc, vc, qn, kn, cos, sin, need_ctx):
    B, T, _ = q.shape
    L = qc.shape[1]
    G = C_HEADS // C_KV_HEADS

    def heads(a, h):
        return a.reshape(a.shape[0], a.shape[1], h, C_HD)

    q = apply_rope(rms_norm(heads(q, C_HEADS), qn), cos, sin)
    k = apply_rope(rms_norm(heads(k, C_KV_HEADS), kn), cos, sin)
    v = heads(v, C_KV_HEADS)
    kc = rms_norm(heads(kc, C_KV_HEADS), kn)
    vc = heads(vc, C_KV_HEADS)
    keys = jnp.concatenate([kc, k], axis=1).transpose(0, 2, 1, 3)
    vals = jnp.concatenate([vc, v], axis=1).transpose(0, 2, 1, 3)
    nb = T // Q_BLOCK
    qb = q.reshape(B, nb, Q_BLOCK, C_KV_HEADS, G, C_HD).transpose(1, 0, 3, 4, 2, 5)
    ob = lax.map(lambda blk: attend(blk, keys, vals), qb)
    o = ob.transpose(1, 0, 4, 2, 3, 5).reshape(B, T, C_WIDTH)
    oc = None
    if need_ctx:
        qcg = rms_norm(heads(qc, C_HEADS), qn).reshape(B, L, C_KV_HEADS, G, C_HD).transpose(0, 2, 3, 1, 4)
        oc = attend(qcg, kc.transpose(0, 2, 1, 3), vc.transpose(0, 2, 1, 3))
        oc = oc.transpose(0, 3, 1, 2, 4).reshape(B, L, C_WIDTH)
    return o, oc

def grouped_moe(h, router_w, router_b, wg, wu, wd):
    N = h.shape[0]
    scores = jax.nn.sigmoid((h @ router_w).astype(jnp.float32))
    sel = scores + router_b.astype(jnp.float32)
    grp_score = lax.top_k(sel.reshape(N, N_GROUPS, E_PER_GROUP), 2)[0].sum(-1)
    best = jnp.argmax(grp_score, axis=-1)
    in_grp = (jnp.arange(N_EXPERTS) // E_PER_GROUP)[None, :] == best[:, None]
    _, idx = lax.top_k(jnp.where(in_grp, sel, NEG_BIG), TOP_K)
    w = jnp.take_along_axis(scores, idx, axis=-1)
    w = w / jnp.sum(w, axis=-1, keepdims=True)
    combine = jnp.sum(jax.nn.one_hot(idx, N_EXPERTS, dtype=jnp.float32) * w[..., None], axis=1)
    y = jnp.zeros((N, h.shape[1]), jnp.float32)
    for e in range(N_EXPERTS):
        a = jax.nn.silu(h @ wg[e]) * (h @ wu[e])
        y = y + combine[:, e:e + 1] * (a @ wd[e]).astype(jnp.float32)
    return y.astype(h.dtype)

def setup_inputs(seed: int = 0) -> dict:
    key = jax.random.key(seed)
    ks = jax.random.split(key, 21)

    def nrm(k, shape, s):
        return jax.random.normal(k, shape, jnp.float32) * s

    return {
        "x": nrm(ks[0], (BATCH, SEQ, D_MODEL), 1.0),
        "c": nrm(ks[1], (BATCH, D_MODEL), 1.0),
        "ctx": nrm(ks[2], (BATCH, CTX_LEN, D_MODEL), 1.0),
        "c_ctx": nrm(ks[3], (D_MODEL,), 1.0),
        "w_mod": nrm(ks[4], (DEPTH, D_MODEL, 6 * D_MODEL), 0.5 * D_MODEL ** -0.5),
        "b_mod": nrm(ks[5], (DEPTH, 6 * D_MODEL), 0.02),
        "norm1_g": 1.0 + nrm(ks[6], (DEPTH, D_MODEL), 0.05),
        "norm2_g": 1.0 + nrm(ks[7], (DEPTH, D_MODEL), 0.05),
        "w_in": nrm(ks[8], (DEPTH, D_MODEL, IN_COLS), D_MODEL ** -0.5),
        "w_out": nrm(ks[9], (DEPTH, D_MIX, D_MODEL), D_MIX ** -0.5),
        "hgrn_lb": nrm(ks[10], (DEPTH, 2, A_WIDTH), 1.0),
        "hgrn_norm_g": 1.0 + nrm(ks[11], (DEPTH, A_HD), 0.05),
        "pool_w": nrm(ks[12], (DEPTH, B_GROUPS, B_GW, B_GW), B_GW ** -0.5),
        "pool_scale": 1.0 + nrm(ks[13], (DEPTH, B_WIDTH), 0.05),
        "q_norm_g": 1.0 + nrm(ks[14], (DEPTH, C_HD), 0.05),
        "k_norm_g": 1.0 + nrm(ks[15], (DEPTH, C_HD), 0.05),
        "router_w": nrm(ks[16], (D_MODEL, N_EXPERTS), D_MODEL ** -0.5),
        "router_b": nrm(ks[17], (N_EXPERTS,), 0.01),
        "moe_w_gate": nrm(ks[18], (DEPTH, N_EXPERTS, D_MODEL, D_EXPERT), D_MODEL ** -0.5),
        "moe_w_up": nrm(ks[19], (DEPTH, N_EXPERTS, D_MODEL, D_EXPERT), D_MODEL ** -0.5),
        "moe_w_down": nrm(ks[20], (DEPTH, N_EXPERTS, D_EXPERT, D_MODEL), D_EXPERT ** -0.5),
    }

def reference(x, c, ctx, c_ctx, w_mod, b_mod, norm1_g, norm2_g, w_in, w_out, hgrn_lb, hgrn_norm_g,
              pool_w, pool_scale, q_norm_g, k_norm_g, router_w, router_b, moe_w_gate, moe_w_up, moe_w_down):
    B, T, D = x.shape
    L = ctx.shape[1]
    cos, sin = axial_rope_tables(T)
    c_act = jax.nn.silu(c)
    cc_act = jax.nn.silu(c_ctx)
    sm = jax.nn.softmax(hgrn_lb.astype(jnp.float32), axis=0)
    lower = jnp.cumsum(sm, axis=0) - sm[0:1]

    xl, xc = x, ctx
    for l in range(DEPTH):
        need_ctx = l < DEPTH - 1
        mod = c_act @ w_mod[l] + b_mod[l]
        sh1, sc1, ga1, sh2, sc2, ga2 = jnp.split(mod[:, None, :], 6, axis=-1)
        sh1c, sc1c, ga1c, sh2c, sc2c, ga2c = jnp.split(cc_act @ w_mod[l] + b_mod[l], 6)

        h = modulate(rms_norm(xl, norm1_g[l]), sh1, sc1)
        hc = modulate(rms_norm(xc, norm1_g[l]), sh1c, sc1c)
        aq, aff, afb, ai, ag, bp, cq, ck, cv = split_in(h @ w_in[l])
        aqc, affc, afbc, aic, agc, bpc, cqc, ckc, cvc = split_in(hc @ w_in[l])

        oa, oac = hgrn2_mixer((aq, aff, afb, ai, ag), (aqc, affc, afbc, aic, agc),
                              lower[l], hgrn_norm_g[l], need_ctx)
        ob = pool_mixer(bp, pool_w[l], pool_scale[l])
        oc, occ = gqa_mixer(cq, ck, cv, cqc, ckc, cvc, q_norm_g[l], k_norm_g[l], cos, sin, need_ctx)
        xl = xl + ga1 * (jnp.concatenate([oa, ob, oc], axis=-1) @ w_out[l])

        h2 = modulate(rms_norm(xl, norm2_g[l]), sh2, sc2)
        if need_ctx:
            obc = pool_mixer(bpc, pool_w[l], pool_scale[l])
            xc = xc + ga1c * (jnp.concatenate([oac, obc, occ], axis=-1) @ w_out[l])
            h2c = modulate(rms_norm(xc, norm2_g[l]), sh2c, sc2c)
            m = grouped_moe(jnp.concatenate([h2.reshape(B * T, D), h2c.reshape(B * L, D)], axis=0),
                            router_w, router_b, moe_w_gate[l], moe_w_up[l], moe_w_down[l])
            xl = xl + ga2 * m[:B * T].reshape(B, T, D)
            xc = xc + ga2c * m[B * T:].reshape(B, L, D)
        else:
            m = grouped_moe(h2.reshape(B * T, D), router_w, router_b,
                            moe_w_gate[l], moe_w_up[l], moe_w_down[l])
            xl = xl + ga2 * m.reshape(B, T, D)
    return xl


_drawn_inputs = setup_inputs


def setup_inputs(seed=0):
    import zlib

    import numpy as np

    out = dict(_drawn_inputs(seed))
    spreads = {}
    factors = {'q_norm_g': 3.849,
     'k_norm_g': 8.0,
     'hgrn_lb': 3.827,
     'hgrn_norm_g': 3.914,
     'pool_scale': 3.199}
    for name, (base, spread) in spreads.items():
        noise = np.random.default_rng([zlib.crc32(name.encode()), seed]).standard_normal(out[name].shape)
        drawn = base * np.exp(spread * noise) if base else spread * noise
        out[name] = __import__('jax').numpy.asarray(drawn.astype(out[name].dtype))
    for name, factor in factors.items():
        out[name] = (out[name] * factor).astype(out[name].dtype)
    return out
```

```python
def build(nc, T, debug=None):
    import concourse.bass as bass
    from concourse import mybir
    from concourse.alu_op_type import AluOpType as ALU
    from contextlib import ExitStack

    f32, i32, u32, u8 = mybir.dt.float32, mybir.dt.int32, mybir.dt.uint32, mybir.dt.uint8
    ACT, AX = mybir.ActivationFunctionType, mybir.AxisListType.X

    P = 128
    D = T["x"].shape[-1]
    SEQ, CTX = T["x"].shape[1], T["ctx"].shape[1]
    L = T["w_mod"].shape[0]
    KD = D // P
    HD = 64
    TT = SEQ + CTX
    NT = TT // P
    NE = T["router_w"].shape[1]
    NG = 4
    EG = NE // NG
    FE = T["moe_w_gate"].shape[-1]
    KF = FE // P
    CAP = TT
    EPS = 1e-6
    LEVELS = [1, 2, 4, 8, 16, 32, 64]
    SLAB = KD * 512
    NMOD, NIN, NWO = 6 * D // 512, 5, D // 512
    NSL = NMOD + NIN + NWO
    QK = 640
    NEG = -1e30

    ctx = ExitStack()
    with ctx:
        def sb(name, shape, dt=f32):
            return ctx.enter_context(nc.sbuf_tensor(name, shape, dt))

        def sem(name):
            return ctx.enter_context(nc.semaphore(name))

        x_sb = sb("x_sb", [P, NT, D])
        mod = sb("mod", [P, 6, D])
        ring = sb("ring", [P, 2, SLAB])
        actT = sb("actT", [P, KD, TT])
        rows = sb("rows", [P, NT, D])
        arena = sb("arena", [P, 22528])
        ident = sb("ident", [P, P])
        before = sb("before", [P, P])
        ones = sb("ones", [P, P])
        headsep = sb("headsep", [P, P])
        masks = sb("masks", [P, len(LEVELS), P], u8)
        rope = sb("rope", [P, SEQ // P, 2, HD])
        invcnt = sb("invcnt", [P, 2, SEQ])
        gain_qk = sb("gain_qk", [P, QK])
        gain_o = sb("gain_o", [P, HD])
        pool_bd = sb("pool_bd", [P, 2, P])
        pool_sc = sb("pool_sc", [P, 2])
        rw = sb("rw", [P, KD, NE])
        rb = sb("rb", [P, NE])
        small = sb("small", [P, 1024])
        idx = sb("idx", [P, 2, NT], u32)
        offs = sb("offs", [P, NE + 4], i32)

        ps = [ctx.enter_context(nc.psum_tensor(f"bank{i}", [P, 512], f32)) for i in range(8)]

        X_s = nc.dram_tensor("expert_in", [2 * TT + CAP, D], f32).ap()
        Y_s = nc.dram_tensor("expert_out", [2 * TT + CAP, D], f32).ap()

        def cut(tensor, start):
            at = [start]

            def take(n):
                at[0] += n
                return tensor[:, at[0] - n:at[0]]
            return take

        take = cut(arena, 0)
        q_t = take(1024).rearrange("p (c t) -> p c t", c=2)
        f_t = [take(1024), take(1024)]
        v_a = take(1024).rearrange("p (j c) -> p j c", j=NT)
        g_a = take(1024).rearrange("p (j c) -> p j c", j=NT)
        qkv = take(3072).rearrange("p (j c) -> p j c", j=NT)
        dpool = take(1024).rearrange("p (c t) -> p c t", c=2)
        hg0 = 9 * 1024
        KG = [take(1024), take(1024)]
        QF = [take(1024), take(1024)]
        ksum = take(1024)
        tots = [take(1024), take(1024)]
        pair_buf = take(4096).rearrange("p (b w n) -> p b w n", b=2, w=2)
        kg_tok = pair_buf.rearrange("p b w n -> p (b w n)")[:, 0:2048].rearrange("p (d c j k) -> p d c j k", d=2, c=2, j=NT)
        osb = pair_buf.rearrange("p b w n -> p (b w n)")[:, 2048:3072].rearrange("p (j c) -> p j c", j=NT)
        osq = pair_buf.rearrange("p b w n -> p (b w n)")[:, 3072:4096].rearrange("p (j c) -> p j c", j=NT)
        S_st = take(2048).rearrange("p (d c j v) -> p d c j v", d=2, c=2, j=NT)
        U_m = arena[:, hg0:hg0 + 1536].rearrange("p (s n) -> p s n", s=3)
        take = cut(arena, hg0 + 2048)
        qkr = take(2 * QK).rearrange("p (b c) -> p b c", b=2)
        swp = take(2 * QK).rearrange("p (b c) -> p b c", b=2)
        qT = take(2048).rearrange("p (c t) -> p c t", c=4)
        kT = take(512)
        Pb = take(1024).rearrange("p (b k) -> p b k", b=2)
        PT = take(1024).rearrange("p (b k) -> p b k", b=2)
        sqk = take(4 * QK).rearrange("p (j c) -> p j c", j=NT)
        take = cut(arena, 0)
        gn = take(2 * D).rearrange("p (a n) -> p a n", a=2)
        cmix = take(KD * P).rearrange("p (k m) -> p k m", k=KD)
        junk = take(2 * D).rearrange("p (a n) -> p a n", a=2)
        ZW = 304
        take = cut(rows[:].rearrange("p a b -> p (a b)"), 0)
        Z = [take(4 * ZW).rearrange("p (c s t) -> p c s t", c=2, s=2) for _ in range(3)]
        A_s = rows[:].rearrange("p j (h t) -> p j h t", t=P)[:, :, 0:4, :]
        masks_f = rows[:, 0, 0:len(LEVELS) * P]
        take = cut(arena, 0)
        slots = [ring[:, 0, :], ring[:, 1, :]] + [take(SLAB) for _ in range(4)]
        xe = take(2 * D).rearrange("p (b n) -> p b n", b=2)
        xeT = take(KD * P).rearrange("p (k s) -> p k s", k=KD)
        sgl = take(FE)
        act_e = take(FE)
        aT = take(KF * P).rearrange("p (k s) -> p k s", k=KF)
        y_e = take(D)
        wtmp, junk2 = sgl, y_e
        yg = arena[:, 0:4 * 2 * D].rearrange("p (i c n) -> p i c n", i=4, c=2)

        take = cut(small, 0)
        cond = take(2 * KD).rearrange("p (a k) -> p a k", a=2)
        ss = take(NT)
        rstd = take(NT)
        mhalf = take(64)
        ssq = take(NT * 10).rearrange("p (j h) -> p j h", j=NT)
        rsq = take(NT * 10).rearrange("p (j h) -> p j h", j=NT)
        mx = take(32)
        nmx = take(32)
        rsum = take(32)
        rinv = take(32)
        lbr = take(8).rearrange("p (l c) -> p l c", l=2)
        lbe = take(16)
        lb = take(8).rearrange("p (l c) -> p l c", l=2)
        oml = take(8).rearrange("p (l c) -> p l c", l=2)
        rsm = take(96)
        wts = take(12).rearrange("p (a i) -> p a i", a=3)
        m16 = take(16)
        rtmp = small[:, 512:1024]

        rconst = ctx.enter_context(nc.sbuf_tensor("rconst", [P, 2 * NE], f32))[:]
        OH0 = 448
        LONG_FROM = P
        ORDER = [[2, 3, 0, 1], [3, 2, 1, 0]]
        PROJ = ([("q", 0), ("q", 1), ("f", (0, 0)), ("f", (0, 1)), ("f", (1, 0)), ("f", (1, 1))] + [("v", j) for j in range(NT)]
                + [("b", 0), ("b", 1)] + [("g", j) for j in range(NT)] + [("cq", j) for j in range(NT)] + [("ck", j) for j in range(NT)])
        NCONST, NGAIN = 16 * 11, 11
        PH = [2 * NT, 6 * NT]

        names = """consts x_in cond_in gains mod_ev condm wl0 wl1 slab_used mod_mm ht ht_ev sqs rstd_d rstd_p rows_d
        proj proj_a proj_d sgm kq_d qk_p qkt qkt_ev sc scmax sexp pnorm ptr pt_ev pv pv_ev
        zbuf bpool dp ymm ymix tot0 lvcp lvup lvdn lvmm lvA kgt kgt_ev umm umask stv omm o_ev ogn rd_p otr omix wo wo_ev
        lg sig ohs posm slots_d scat xl0 xl1 xtr xe_d xe_a gate silu up a_d atr aT_d down y_d y_a ystore moe_used
        gat comb out_s vstep astep pstep lbx lbd memz pres
        ginit repack xdone proj_x condx lvup0 o_fin qk_d2""".split()
        S = {n: sem("s_" + n) for n in names}
        gats = [sem(f"s_gathered{i}") for i in range(NT)]
        LONG = [{n: sem(f"s_long{l}_{n}") for n in "x xT w xe gu silu a aT aTe y yh ye store".split()} for l in range(L)]
        ml = [sem(f"s_expert_slab{i}") for i in range(6)]

        class Eng:
            def __init__(self, eng):
                self.e, self.n = eng, {}

            def up(self, name, k=1):
                self.n[name] = self.n.get(name, 0) + k
                return self.n[name]

            def wait(self, name, value):
                self.e.wait_ge(S[name], value)

            def next(self, name, k=1):
                self.e.wait_ge(S[name], self.up(name, k))

            def lag(self, name, value):
                if value > 0:
                    self.e.wait_ge(S[name], value)

            def step(self, ins, name):
                ins.then_inc(S[name], 1)
                self.e.wait_ge(S[name], self.up(name))

        block = ctx.enter_context(nc.Block())

        def w_view(w, cols):
            return w[:, cols].rearrange("(p k) n -> p k n", k=KD)

        def tiles_of(l):
            return (NT if l == 0 else SEQ // P)

        def long_lists(eng, l):
            n_max = eng.value_load(offs[0:1, NE + 2:NE + 3], min_val=0, max_val=TT)
            return eng.If(n_max > LONG_FROM)

        @block.sync
        def _(sp):
            E = Eng(sp)
            n = [0]

            def slab(src, width=512):
                s = n[0] % 2
                if n[0] >= 2:
                    E.lag("slab_used", n[0] - 1)
                dst = ring[:, s, :].rearrange("p (k n) -> p k n", k=KD)[:, :, 0:width]
                sp.dma_start(dst, src).then_inc(S[f"wl{s}"], 16)
                n[0] += 1

            for s in range(2):
                slab(w_view(T["w_mod"][0], slice(512 * s, 512 * s + 512)))
            for a, src in enumerate((T["x"][0], T["ctx"][0])):
                sp.dma_start(x_sb[64 * a:64 * a + 64, :, :], src.rearrange("(i p) d -> p i d", p=64)).then_inc(S["x_in"], 16)
            for l in range(L):
                for s in range(NMOD):
                    if l or s >= 2:
                        if l and s == 0:
                            E.wait("moe_used", 3 * NE * l)
                            E.wait("comb", NT)
                        slab(w_view(T["w_mod"][l], slice(512 * s, 512 * s + 512)))
                for s in range(NIN):
                    width = 512 if s < 4 else 256
                    slab(w_view(T["w_in"][l], slice(512 * s, 512 * s + width)), width)
                for s in range(NWO):
                    slab(T["w_out"][l][:, 512 * s:512 * s + 512].rearrange("(k p) n -> p k n", p=P))
                wg, wu, wd = T["moe_w_gate"][l], T["moe_w_up"][l], T["moe_w_down"][l]

                def expert_slab(e, u, k):
                    w = (wg, wu, wd)[k]
                    kk = KF if k == 2 else KD
                    src = w[e] if isinstance(e, int) else w[bass.ds(e, 1)].rearrange("o a b -> (o a) b")
                    src = src.rearrange("(p k) n -> p (k n)", k=kk)
                    sp.dma_start(slots[3 * u + k], src).then_inc(ml[3 * u + k], 16)

                def expert_rows(e, u):
                    at = sp.value_load(offs[0:1, e:e + 1] if isinstance(e, int) else offs[0:1, bass.ds(e, 1)],
                                       min_val=0, max_val=2 * TT)
                    sp.dma_start(xe[:, u, :], X_s[bass.ds(at, P), :]).then_inc(S[f"xl{u}"], 16)

                E.wait("slab_used", NSL * (l + 1))
                for u in range(2):
                    for k in range(3):
                        expert_slab(u, u, k)
                E.next("scat", 16 * 2 * (NT if l == 0 else SEQ // P))
                E.next("slots_d", 1)
                for u in range(2):
                    expert_rows(u, u)
                with sp.Fori(0, NE // 2 - 1) as i:
                    for u in range(2):
                        for k in range(3):
                            sp.wait_ge(S["moe_used"], i * 6 + (3 * NE * l + 3 * u + k + 1))
                            expert_slab(i * 2 + (2 + u), u, k)
                        sp.wait_ge(S["xtr"], i * 2 + ((NE + 1) * l + u + 1))
                        expert_rows(i * 2 + (2 + u), u)
                E.wait("xtr", (NE + 1) * l + NE - 1)
                expert_rows(NE, 0)
                E.wait("moe_used", 3 * NE * (l + 1))
                E.wait("ystore", 16 * (NE * (l + 1) + 1))
                with long_lists(sp, l):
                    O, nj = LONG[l], tiles_of(l)
                    with sp.Fori(0, NE) as e:
                        for k in range(3):
                            w, kk = (wg, wu, wd)[k], KF if k == 2 else KD
                            src = w[bass.ds(e, 1)].rearrange("o a b -> (o a) b").rearrange("(p k) n -> p (k n)", k=kk)
                            sp.dma_start(slots[k], src).then_inc(O["w"], 16)
                        at = sp.value_load(offs[0:1, bass.ds(e, 1)], min_val=0, max_val=2 * nj * P)
                        for j in range(nj):
                            sp.dma_start(xe[:, 0, :], X_s[bass.ds(at + j * P, P), :]).then_inc(O["x"], 16)
                            sp.wait_ge(O["yh"], e * nj + (j + 1))
                            sp.wait_ge(O["ye"], e * nj + (j + 1))
                            sp.dma_start(Y_s[bass.ds(at + j * P, P), :], y_e).then_inc(O["store"], 16)
            E.wait("comb", NT + SEQ // P)
            sp.dma_start(T["out"][0].rearrange("(i p) d -> p i d", p=P), x_sb[:, 0::2, :]).then_inc(S["out_s"], 16)
            E.wait("out_s", 16)

        @block.gpsimd
        def _(pool):
            E = Eng(pool)
            g = nc.gpsimd

            def powr(dst, src, l_src, sem_out):
                E.step(g.tensor_tensor(dst, src, mhalf[:, 0:src.shape[-1]] if len(src.shape) == 2 else
                                       mhalf[:, 0:src.shape[1] * src.shape[2]].rearrange("p (a b) -> p a b", a=src.shape[1]),
                                       ALU.pow), sem_out)

            E.step(g.memset(mhalf, -0.5), "pstep")
            g.memset(ones[:], 1.0).then_inc(S["memz"], 1)
            g.memset(pool_bd[:], 0.0).then_inc(S["memz"], 1)
            g.memset(actT[:], 0.0).then_inc(S["memz"], 1)
            for l in range(L):
                nt2 = NT if l == 0 else SEQ // P
                E.next("rstd_d")
                powr(rstd[:, 0:NT], ss[:, 0:NT], None, "rstd_p")
                M = 16
                E.wait("ht", PH[l])
                for z in Z:
                    E.step(g.memset(z[:, :, :, :], 0.0), "zbuf")
                E.next("kq_d")
                powr(rsq, ssq, None, "qk_p")
                E.next("bpool", 2)
                W = ZW - 2 * M + M
                src, dst = Z[0], Z[1]
                n_ = ZW - 16
                E.step(g.tensor_tensor(Z[1][:, :, :, 0:n_], Z[0][:, :, :, 0:n_], Z[0][:, :, :, 1:n_ + 1], ALU.add), "pstep")
                x0 = lambda p0, c: Z[0][p0:p0 + 64, c, :, M:M + SEQ]
                dv = lambda p0, c: dpool[p0:p0 + 64, c, :].rearrange("p (s t) -> p s t", s=2)
                ic = lambda p0, c: invcnt[p0:p0 + 64, c, :].unsqueeze(1).broadcast_to([64, 2, SEQ])

                def finish(zsum, p0, c, half):
                    E.step(g.tensor_tensor(dv(p0, c), zsum[p0:p0 + 64, c, :, M - half:M - half + SEQ], ic(p0, c), ALU.mult), "pstep")
                    E.step(g.tensor_tensor(dv(p0, c), dv(p0, c), x0(p0, c), ALU.subtract), "dp")
                finish(Z[1], 0, 0, 1)
                n_ -= 2
                E.step(g.tensor_tensor(Z[2][:, :, :, 0:n_], Z[1][:, :, :, 0:n_], Z[1][:, :, :, 2:n_ + 2], ALU.add), "pstep")
                finish(Z[2], 64, 0, 2)
                n_ -= 4
                E.step(g.tensor_tensor(Z[1][:, 1, :, 0:n_], Z[2][:, 1, :, 0:n_], Z[2][:, 1, :, 4:n_ + 4], ALU.add), "pstep")
                finish(Z[1], 0, 1, 4)
                n_ -= 8
                E.step(g.tensor_tensor(Z[2][64:128, 1, :, 0:n_], Z[1][64:128, 1, :, 0:n_], Z[1][64:128, 1, :, 8:n_ + 8], ALU.add), "pstep")
                finish(Z[2], 64, 1, 8)
                E.next("tot0")
                tcur = f_t[1]
                toff = 0
                for w in LEVELS:
                    E.next("lvcp", 4)
                    q = QF[1].rearrange("p (n a w) -> p n a w", a=2, w=w)
                    k = KG[1].rearrange("p (n a w) -> p n a w", a=2, w=w)
                    t = tcur.rearrange("p (n a) -> p n a", a=2)
                    nb = 1024 // (2 * w)
                    E.step(g.tensor_tensor(q[:, :, 0, :], q[:, :, 0, :], t[:, :, 1:2].broadcast_to([P, nb, w]), ALU.mult), "pstep")
                    E.step(g.tensor_tensor(k[:, :, 1, :], k[:, :, 1, :], t[:, :, 0:1].broadcast_to([P, nb, w]), ALU.mult), "pstep")
                    tn = tots[1][:, toff:toff + nb]
                    E.step(g.tensor_tensor(tn, t[:, :, 0], t[:, :, 1], ALU.mult), "lvup")
                    tcur = tn
                    toff += nb
                for j in range(nt2):
                    E.next("ogn")
                    powr(rsq[:, j, 0:4], ssq[:, j, 0:4], None, "rd_p")
                E.next("rstd_d")
                powr(rstd[:, 0:nt2], ss[:, 0:nt2], None, "rstd_p")
                E.next("slots_d")
                if l == 0:
                    E.wait("ginit", 16)
                tiles = range(NT) if l == 0 else range(SEQ // P)
                for i in tiles:
                    for c in range(2):
                        g.indirect_dma_start(out=X_s, out_offset=bass.IndirectOffsetOnAxis(ap=idx[:, c, i:i + 1], axis=0),
                                             in_=rows[:, i, :], in_offset=None).then_inc(S["scat"], 16)
                E.wait("ystore", 16 * (NE * (l + 1) + 1))
                with long_lists(pool, l):
                    pool.wait_ge(LONG[l]["store"], 16 * NE * tiles_of(l))
                for i in tiles:
                    for c in range(2):
                        g.indirect_dma_start(out=yg[:, i, c, :], out_offset=None, in_=Y_s[0:2 * TT, :],
                                             in_offset=bass.IndirectOffsetOnAxis(ap=idx[:, c, i:i + 1], axis=0)
                                             ).then_inc(gats[i], 16)

        @block.tensor
        def _(pe):
            E = Eng(pe)
            mm, tr = nc.tensor.matmul, nc.tensor.transpose
            n = [0]

            def slab_in():
                s = n[0] % 2
                pe.wait_ge(S[f"wl{s}"], 16 * (n[0] // 2 + 1))
                n[0] += 1
                return ring[:, s, :].rearrange("p (k n) -> p k n", k=KD)

            def rows_transposed(i):
                for kk in range(2):
                    g_ = E.n.get("ht", 0)
                    E.lag("ht_ev", g_ - 1)
                    for k in range(4):
                        last = tr(ps[2 + g_ % 2][:, k * P:(k + 1) * P], rows[:, i, 4 * kk + k::KD], ident[:])
                    last.then_inc(S["ht"], 1)
                    E.up("ht")

            E.wait("consts", NCONST)
            E.wait("memz", 3)
            for l in range(L):
                nt2 = NT if l == 0 else SEQ // P
                for s in range(NMOD):
                    m = NMOD * l + s
                    if s == 0:
                        E.next("condm")
                    if l and s == 4:
                        E.next("condm")
                    E.lag("mod_ev", m - 1)
                    w = slab_in()
                    for k in range(KD):
                        last = mm(ps[m % 2][:], cmix[:, k, :], w[:, k, :], start=(k == 0), stop=(k == KD - 1))
                    last.then_inc(S["slab_used"], 1)
                E.wait("mod_ev", NMOD * (l + 1))
                for i in range(NT):
                    E.next("rows_d")
                    rows_transposed(i)
                E.wait("ht_ev", E.n["ht"])
                pg = [0]

                def proj(out, k, lhsT, rhs):
                    return mm(out, lhsT, rhs, start=(k == 0), stop=(k == KD - 1))

                def group():
                    b = 4 + E.n.get("proj", 0) % 4
                    E.lag("proj_d", E.n.get("proj", 0) - 3)
                    E.up("proj")
                    return ps[b]
                for s, (tc, tk) in enumerate([((0, 128, 256, 384), None), ((0, 128), (256, 512)), ((256, 384), (0, 256)),
                                              ((), (0, 512)), ((), (0, 256))]):
                    w = slab_in()
                    last_mm = None
                    for c in tc:
                        b = group()
                        for k in range(KD):
                            last = proj(b[:, :], k, w[:, k, c:c + 128], actT[:, k, :])
                        last.then_inc(S["proj"], 1)
                    if tk:
                        for j in range(NT):
                            b = group()
                            for k in range(KD):
                                last = proj(b[:, 0:tk[1] - tk[0]], k, actT[:, k, j * P:(j + 1) * P], w[:, k, tk[0]:tk[1]])
                            last.then_inc(S["proj"], 1)
                    if s < 5:
                        pe.wait_ge(S["proj"], E.n["proj"])
                        pe.sem_inc(S["slab_used"], 1)
                for j in range(NT):
                    E.next("qk_d2")
                    g_ = E.n.get("qkt", 0)
                    E.lag("qkt_ev", g_ - 1)
                    for c in range(4):
                        tr(ps[g_ % 2][:, c * P:(c + 1) * P], qkr[:, j % 2, c * P:(c + 1) * P], ident[:])
                    tr(ps[2 + g_ % 2][:, 0:P], qkr[:, j % 2, 4 * P:5 * P], ident[:]).then_inc(S["qkt"], 1)
                    E.up("qkt")
                E.wait("qkt_ev", E.n["qkt"])
                units = [(j, h) for j in range(nt2) for h in range(8)]

                def scores(u):
                    j, h = units[u]
                    a = 64 * (h // 4)
                    g_ = E.n.get("sc", 0)
                    E.lag("sexp", g_ - 2)
                    keys = slice(0, TT) if j < SEQ // P else slice(SEQ, TT)
                    nk = keys.stop - keys.start
                    mm(ps[g_ % 3][:, 0:nk], qT[a:a + 64, h % 4, j * P:(j + 1) * P], kT[a:a + 64, keys],
                       start=True, stop=True).then_inc(S["sc"], 1)
                    E.up("sc")

                def values(u):
                    j, h = units[u]
                    kt = range(NT) if j < SEQ // P else range(SEQ // P, NT)
                    E.next("pnorm")
                    g_ = E.n.get("ptr", 0)
                    E.lag("pt_ev", g_ - 1)
                    for m, _ in enumerate(kt):
                        last = tr(ps[3 + g_ % 2][:, m * P:(m + 1) * P], Pb[:, g_ % 2, m * P:(m + 1) * P], ident[:])
                    last.then_inc(S["ptr"], 1)
                    E.up("ptr")
                    return g_, kt

                def outv(u, g_, kt):
                    j, h = units[u]
                    E.next("pt_ev")
                    E.lag("pv_ev", g_ - 1)
                    for m, t_ in enumerate(kt):
                        last = mm(ps[5 + g_ % 2][0:64, 0:P], qkv[:, t_, QK + 64 * (h // 4):QK + 64 * (h // 4) + 64],
                                  PT[:, g_ % 2, m * P:(m + 1) * P], start=(m == 0), stop=(m == len(kt) - 1))
                    last.then_inc(S["pv"], 1)
                    E.up("pv")
                scores(0)
                scores(1)
                prev = None
                for u in range(len(units)):
                    if u + 2 < len(units):
                        scores(u + 2)
                    cur = values(u)
                    if prev:
                        outv(u - 1, *prev)
                    prev = cur
                outv(len(units) - 1, *prev)
                E.wait("pv_ev", E.n["pv"])
                E.next("dp", 4)
                for c in range(2):
                    mm(ps[7][:, :], pool_bd[:, c, :], dpool[:, c, :], start=True, stop=True).then_inc(S["ymm"], 1)
                    E.next("ymix")
                E.next("lvdn")
                def pair_products(keys, queries, bank0):
                    for J in range(NT // 2):
                        for m in range(4):
                            j, c = 2 * J + m // 2, m % 2
                            for a in range(2):
                                if m == 0:
                                    E.lag("lvA", E.n["lvmm"] + a - 7 if "lvmm" in E.n else 0)
                                last = mm(ps[bank0 + 2 * J + a][:, m * P:(m + 1) * P],
                                          keys[64 * a:64 * a + 64, c, j * P:(j + 1) * P],
                                          queries[64 * a:64 * a + 64, c, j * P:(j + 1) * P], start=True, stop=True)
                                if m == 3:
                                    last.then_inc(S["lvmm"], 1)
                        E.up("lvmm", 2)
                pair_products(ksum.rearrange("p (c t) -> p c t", c=2), q_t, 0)
                for v, w in enumerate(LEVELS):
                    E.next("lvcp", 4)
                    pb = pair_buf[:, v % 2].rearrange("p w (c t) -> p w c t", c=2)
                    pair_products(pb[:, 1], pb[:, 0], 4 * ((v + 1) % 2))
                E.wait("lvA", E.n["lvmm"])
                E.next("lvdn", len(LEVELS))
                E.next("lvup", len(LEVELS))
                for d in range(2):
                    for c in range(2):
                        for j in range(NT):
                            last = tr(ps[2 * d + c][:, j * P:(j + 1) * P], KG[d][:, c * 512 + j * P:c * 512 + (j + 1) * P], ident[:])
                        last.then_inc(S["kgt"], 1)
                E.next("kgt_ev", 4)
                order = ORDER
                for s in range(3):
                    for d in range(2):
                        for c in range(2):
                            j = order[d][s]
                            last = mm(ps[4 + s][:, (2 * d + c) * P:(2 * d + c + 1) * P], kg_tok[:, d, c, j, :],
                                      v_a[:, j, c * P:(c + 1) * P], start=True, stop=True)
                    last.then_inc(S["umm"], 1)
                E.next("stv")
                E.wait("lvA", E.n["lvmm"])
                for j in range(nt2):
                    for c in range(2):
                        for a in range(2):
                            o, hc = ps[j][:, (2 * c + a) * HD:(2 * c + a + 1) * HD], slice(a * HD, (a + 1) * HD)
                            for d in range(2):
                                mm(o, QF[d][:, c * 512 + j * P:c * 512 + (j + 1) * P], S_st[:, d, c, j, hc], start=(d == 0), stop=False)
                            last = mm(o, A_s[:, j, 2 * c + a, :], v_a[:, j, (2 * c + a) * HD:(2 * c + a + 1) * HD], start=False, stop=True)
                    last.then_inc(S["omm"], 1)
                for j in range(nt2):
                    E.next("o_fin")
                    for c in range(2):
                        last = tr(ps[4 + j][:, c * P:(c + 1) * P], osb[:, j, c * P:(c + 1) * P], ident[:])
                    last.then_inc(S["otr"], 1)
                E.next("omix", nt2)
                for s in range(NWO):
                    w = slab_in()
                    for i in range(nt2):
                        g_ = E.n.get("wo", 0)
                        E.lag("wo_ev", g_ - 3)
                        for k in range(KD):
                            last = mm(ps[g_ % 4][:], actT[:, k, i * P:(i + 1) * P], w[:, k, :], start=(k == 0), stop=(k == KD - 1))
                        last.then_inc(S["wo"], 1)
                        E.up("wo")
                    pe.wait_ge(S["wo"], E.n["wo"])
                    pe.sem_inc(S["slab_used"], 1)
                E.wait("wo_ev", E.n["wo"])
                for i in range(nt2):
                    E.next("rows_d")
                    rows_transposed(i)
                E.wait("ht_ev", E.n["ht"])
                for i in range(nt2):
                    for k in range(KD):
                        last = mm(ps[4][:, i * NE:(i + 1) * NE], actT[:, k, i * P:(i + 1) * P], rw[:, k, :],
                                  start=(k == 0), stop=(k == KD - 1))
                last.then_inc(S["lg"], 1)
                E.next("ohs")
                oh = rtmp[:, OH0:OH0 + nt2 * NE].rearrange("p (i e) -> p i e", e=NE)
                for i in range(nt2 + 1):
                    for j in range(min(i + 1, nt2)):
                        lhs = before if j == i else ones
                        last = mm(ps[5][:, i * NE:(i + 1) * NE], lhs[:], oh[:, j, :], start=(j == 0), stop=(j == min(i, nt2 - 1)))
                last.then_inc(S["posm"], 1)
                E.next("slots_d")
                GB, UB, AB, X0, X1, D0, D1 = 0, 1, 2, 3, 4, 5, 6
                b17 = (NE + 1) * l
                b16 = NE * l

                def x_transposed(u):
                    for k in range(KD):
                        last = tr(ps[X0 + k // 4][:, (k % 4) * P:(k % 4 + 1) * P], xe[:, u, k::KD], ident[:])
                    last.then_inc(S["xtr"], 1)
                pe.wait_ge(S["xl0"], 16 * (9 * l + 1))
                x_transposed(0)
                with pe.Fori(0, NE // 2) as i:
                    for u in range(2):
                        wg = slots[3 * u].rearrange("p (k n) -> p k n", k=KD)
                        wu = slots[3 * u + 1].rearrange("p (k n) -> p k n", k=KD)
                        wd = slots[3 * u + 2].rearrange("p (k n) -> p k n", k=KF)
                        pe.wait_ge(S["xe_d"], i * 2 + (b17 + u + 1))
                        pe.wait_ge(S["xe_a"], i * 2 + (b17 + u + 1))
                        pe.wait_ge(ml[3 * u], i * 16 + 16 * (NE // 2 * l + 1))
                        for k in range(KD):
                            last = mm(ps[GB][:], xeT[:, k, :], wg[:, k, :], start=(k == 0), stop=(k == KD - 1))
                        last.then_inc(S["moe_used"], 1)
                        pe.wait_ge(ml[3 * u + 1], i * 16 + 16 * (NE // 2 * l + 1))
                        for k in range(KD):
                            last = mm(ps[UB][:], xeT[:, k, :], wu[:, k, :], start=(k == 0), stop=(k == KD - 1))
                        last.then_inc(S["moe_used"], 1)
                        if u == 0:
                            pe.wait_ge(S["xl1"], i * 16 + 16 * (8 * l + 1))
                        else:
                            pe.wait_ge(S["xl0"], i * 16 + 16 * (9 * l + 2))
                        x_transposed(1 - u)
                        pe.wait_ge(S["a_d"], i * 2 + (b16 + u + 1))
                        for k in range(KF):
                            last = tr(ps[AB][:, k * P:(k + 1) * P], act_e[:, k::KF], ident[:])
                        last.then_inc(S["atr"], 1)
                        pe.wait_ge(S["aT_d"], i * 2 + (b16 + u + 1))
                        pe.wait_ge(S["y_d"], i * 2 + (b17 + u + 1))
                        pe.wait_ge(S["y_a"], i * 2 + (b17 + u + 1))
                        pe.wait_ge(ml[3 * u + 2], i * 16 + 16 * (NE // 2 * l + 1))
                        for h in range(2):
                            for k in range(KF):
                                last = mm(ps[D0 + h][:], aT[:, k, :], wd[:, k, h * 512:(h + 1) * 512], start=(k == 0), stop=(k == KF - 1))
                        last.then_inc(S["moe_used"], 1)
                E.wait("y_d", b17 + NE + 1)
                E.wait("y_a", b17 + NE + 1)
                E.wait("xe_d", b17 + NE + 1)
                E.wait("xe_a", b17 + NE + 1)
                with long_lists(pe, l):
                    O, nj = LONG[l], tiles_of(l)
                    wg, wu = (slots[k].rearrange("p (k n) -> p k n", k=KD) for k in range(2))
                    wd = slots[2].rearrange("p (k n) -> p k n", k=KF)
                    with pe.Fori(0, NE) as e:
                        for j in range(nj):
                            pe.wait_ge(O["x"], e * (16 * nj) + 16 * (j + 1))
                            for k in range(KD):
                                last = tr(ps[X0 + k // 4][:, (k % 4) * P:(k % 4 + 1) * P], xe[:, 0, k::KD], ident[:])
                            last.then_inc(O["xT"], 1)
                            pe.wait_ge(O["xe"], e * (2 * nj) + 2 * (j + 1))
                            pe.wait_ge(O["w"], e * 48 + 48)
                            for bank, w in ((GB, wg), (UB, wu)):
                                for k in range(KD):
                                    last = mm(ps[bank][:], xeT[:, k, :], w[:, k, :], start=(k == 0), stop=(k == KD - 1))
                            last.then_inc(O["gu"], 1)
                            pe.wait_ge(O["a"], e * nj + (j + 1))
                            for k in range(KF):
                                last = tr(ps[AB][:, k * P:(k + 1) * P], act_e[:, k::KF], ident[:])
                            last.then_inc(O["aT"], 1)
                            pe.wait_ge(O["aTe"], e * nj + (j + 1))
                            for h in range(2):
                                for k in range(KF):
                                    last = mm(ps[D0 + h][:], aT[:, k, :], wd[:, k, h * 512:(h + 1) * 512], start=(k == 0), stop=(k == KF - 1))
                            last.then_inc(O["y"], 1)
                            pe.wait_ge(O["yh"], e * nj + (j + 1))
                            pe.wait_ge(O["ye"], e * nj + (j + 1))

        @block.scalar
        def _(act):
            E = Eng(act)
            A = nc.scalar.activation

            def copy(o, i):
                return A(o, i, ACT.Copy)

            def gains(l):
                act.dma_start(mod[:].rearrange("p a n -> p (a n)"), T["b_mod"][l:l + 1, :].broadcast_to([P, 6 * D])).then_inc(S["gains"], 16)
                for a, nm in enumerate(("norm1_g", "norm2_g")):
                    act.dma_start(gn[:, a, :], T[nm][l:l + 1, :].broadcast_to([P, D])).then_inc(S["gains"], 16)
                act.dma_start(gain_qk[:, 0:512].rearrange("p (h d) -> p h d", h=8),
                              T["q_norm_g"][l:l + 1, :].unsqueeze(1).broadcast_to([P, 8, HD])).then_inc(S["gains"], 16)
                act.dma_start(gain_qk[:, 512:640].rearrange("p (h d) -> p h d", h=2),
                              T["k_norm_g"][l:l + 1, :].unsqueeze(1).broadcast_to([P, 2, HD])).then_inc(S["gains"], 16)
                act.dma_start(gain_o[:], T["hgrn_norm_g"][l:l + 1, :].broadcast_to([P, HD])).then_inc(S["gains"], 16)
                for gi in range(4):
                    a = 64 * (gi % 2)
                    act.dma_start(pool_bd[a:a + 64, gi // 2, a:a + 64], T["pool_w"][l, gi]).then_inc(S["gains"], 16)
                act.dma_start(pool_sc[:], T["pool_scale_cols"][l]).then_inc(S["gains"], 16)

            act.dma_start(cond[:, 0, :], T["c"][0].rearrange("(p k) -> p k", k=KD)).then_inc(S["cond_in"], 16)
            act.dma_start(cond[:, 1, :], T["c_ctx"].rearrange("(p k) -> p k", k=KD)).then_inc(S["cond_in"], 16)
            act.dma_start(ident[:], T["k_ident"]).then_inc(S["consts"], 16)
            act.dma_start(before[:], T["k_before"]).then_inc(S["consts"], 16)
            act.dma_start(headsep[:], T["k_headsep"]).then_inc(S["consts"], 16)
            act.dma_start(masks_f, T["k_masks"].rearrange("p a b -> p (a b)")).then_inc(S["consts"], 16)
            act.dma_start(rope[:], T["k_rope"]).then_inc(S["consts"], 16)
            act.dma_start(invcnt[:], T["k_invcnt"]).then_inc(S["consts"], 16)
            act.dma_start(rw[:], T["router_w"].rearrange("(p k) e -> p k e", k=KD)).then_inc(S["consts"], 16)
            act.dma_start(rb[:], T["router_b"].rearrange("(a e) -> a e", a=1).broadcast_to([P, NE])).then_inc(S["consts"], 16)
            act.dma_start(rconst, T["k_router"]).then_inc(S["consts"], 16)
            for l_ in range(2):
                act.dma_start(lbr[:, l_, :], T["hgrn_lb_cols"][l_]).then_inc(S["consts"], 16)
            E.wait("memz", 3)
            act.dma_start(X_s[2 * TT:2 * TT + CAP, :].rearrange("(a p) d -> p a d", p=P),
                          actT[:].rearrange("p k t -> p (k t)")[:, 0:4 * D].rearrange("p (a d) -> p a d", a=4)).then_inc(S["ginit"], 16)
            act.dma_start(Y_s[0:P, 0:64], actT[:, 0, 0:64]).then_inc(S["ystore"], 16)
            gains(0)
            E.wait("cond_in", 32)
            E.step(A(cond[:], cond[:], ACT.Silu), "condx")
            E.next("lbd")
            E.step(A(lbe[:, 0:8], lbe[:, 0:8], ACT.Exp), "lbx")
            E.wait("ginit", 16)
            for l in range(L):
                nt2 = NT if l == 0 else SEQ // P
                if l:
                    E.wait("comb", NT)
                    gains(l)
                E.wait("x_in", 32)

                def squares(tiles, ts, jb):
                    for i in range(tiles):
                        E.step(A(jb, x_sb[:, ts[i], :], ACT.Square, accum_out=ss[:, i:i + 1]), "sqs")
                squares(NT, range(NT), junk[:, 0, :])

                def ht_evac(n, mixed):
                    for _ in range(n):
                        for kk in range(2):
                            g_ = E.n.get("ht", 0)
                            i = htile[0]
                            E.next("ht")
                            if mixed:
                                dst = actT[:].rearrange("p k (s t) -> p (k s) t", s=2)[:, 8 * kk:8 * kk + 8, 64 * i:64 * i + 64]
                                src = ps[2 + g_ % 2][:].rearrange("p (a t) -> p a t", t=64)
                            else:
                                dst = actT[:, 4 * kk:4 * kk + 4, i * P:(i + 1) * P]
                                src = ps[2 + g_ % 2][:].rearrange("p (a t) -> p a t", t=P)
                            E.step(copy(dst, src), "ht_ev")
                        htile[0] += 1
                htile = [0]
                ht_evac(NT, True)
                for kind, a in PROJ:
                    g_ = E.n.get("proj", 0)
                    b = ps[4 + g_ % 4]
                    E.next("proj")
                    if kind == "q":
                        E.step(A(q_t[:, a, :], b[:], ACT.Sigmoid), "sgm")
                    elif kind == "f":
                        d, c = a
                        E.step(A(f_t[d][:, c * 512:(c + 1) * 512], b[:], ACT.Sigmoid), "astep")
                        E.step(A(KG[d][:, c * 512:(c + 1) * 512], b[:], ACT.Sigmoid, scale=-1.0), "sgm")
                    elif kind == "g":
                        E.step(A(g_a[:, a, :], b[:, 0:256], ACT.Sigmoid), "sgm")
                    elif kind == "v":
                        E.step(copy(v_a[:, a, :], b[:, 0:256]), "proj_x")
                    elif kind == "b":
                        E.lag("zbuf", 3 * (l + 1))
                        E.step(copy(Z[0][:, a, :, 16:16 + SEQ], b[:].rearrange("p (s t) -> p s t", s=2)), "bpool")
                    elif kind == "cq":
                        E.step(copy(qkv[:, a, 0:512], b[:]), "proj_x")
                    elif kind == "ck":
                        E.step(copy(qkv[:, a, 512:768], b[:, 0:256]), "proj_x")
                for j in range(NT):
                    g_ = E.n.get("qkt", 0)
                    E.next("qkt")
                    E.step(copy(qT[:, :, j * P:(j + 1) * P], ps[g_ % 2][:].rearrange("p (c t) -> p c t", c=4)), "astep")
                    E.step(copy(kT[:, j * P:(j + 1) * P], ps[2 + g_ % 2][:, 0:P]), "qkt_ev")
                units = [(j, h) for j in range(nt2) for h in range(8)]
                for u in range(len(units) + 1):
                    if u < len(units):
                        j, h = units[u]
                        nk = TT if j < SEQ // P else CTX
                        g_ = E.n.get("sexp", 0)
                        E.next("scmax")
                        E.lag("ptr", g_ - 1)
                        E.step(A(Pb[:, g_ % 2, 0:nk], ps[g_ % 3][:, 0:nk], ACT.Exp, bias=nmx[:, u:u + 1], scale=HD ** -0.5,
                                 accum_out=rsum[:, u:u + 1]), "sexp")
                    if u >= 1:
                        j, h = units[u - 1]
                        nk = TT if j < SEQ // P else CTX
                        g_ = E.n.get("pt_ev", 0)
                        E.next("ptr")
                        E.lag("pv", g_ - 1)
                        E.step(copy(PT[:, g_ % 2, 0:nk], ps[3 + g_ % 2][:, 0:nk]), "pt_ev")
                E.wait("pv", E.n["pt_ev"])
                E.next("lvup0")
                for v, w in enumerate(LEVELS):
                    if v:
                        E.next("lvdn")
                        E.next("lvup")
                    else:
                        E.next("lvdn")
                    if v >= 2:
                        E.wait("lvmm", 32 * l + 4 * v)
                    Qo, Ko = (pair_buf[:, v % 2, a, :].rearrange("p (n a w) -> p n a w", a=2, w=w) for a in range(2))
                    qf, qb, kf, kb = (z.rearrange("p (n a w) -> p n a w", a=2, w=w) for z in (*QF, *KG))
                    for o, i_ in ((Qo[:, :, 1, :], qf[:, :, 1, :]), (Qo[:, :, 0, :], qb[:, :, 0, :]),
                                  (Ko[:, :, 0, :], kf[:, :, 0, :]), (Ko[:, :, 1, :], kb[:, :, 1, :])):
                        copy(o, i_).then_inc(S["lvcp"], 1)
                E.up("lvdn")
                E.up("lvup")
                for b in range(4):
                    E.next("kgt")
                    E.step(copy(kg_tok[:, b // 2, b % 2], ps[b][:].rearrange("p (j k) -> p j k", j=NT)), "kgt_ev")
                for j in range(nt2):
                    E.next("omm")
                    E.step(copy(osb[:, j, :], ps[j][:, 0:256]), "o_ev")
                for j in range(nt2):
                    E.next("otr")
                    dst = actT[:, 0:2, :]
                    if l == 0:
                        s_, i0 = j // 2, 2 * (j % 2)
                        dst = dst.rearrange("p c (i s t) -> p c i s t", i=4, s=2)[:, :, i0:i0 + 2, s_, :]
                        src = ps[4 + j][:, 0:256].rearrange("p (c i t) -> p c i t", c=2, i=2)
                    else:
                        dst = dst[:, :, j * P:(j + 1) * P]
                        src = ps[4 + j][:, 0:256].rearrange("p (c t) -> p c t", c=2)
                    E.step(copy(dst, src), "omix")
                for i in range(nt2):
                    E.next("xdone")
                    E.step(A(junk2, x_sb[:, (i if l == 0 else 2 * i), :], ACT.Square, accum_out=ss[:, i:i + 1]), "sqs")
                htile = [0]
                ht_evac(nt2, False)
                E.next("lg")
                E.step(A(rtmp[:, 0:nt2 * NE], ps[4][:, 0:nt2 * NE], ACT.Sigmoid), "sig")
                GB, UB, AB, X0, X1, D0, D1 = 0, 1, 2, 3, 4, 5, 6
                b17, b16 = (NE + 1) * l, NE * l
                E.wait("scat", 16 * 2 * (NT if l == 0 else NT + SEQ // P))
                act.wait_ge(S["xtr"], b17 + 1)
                copy(xeT[:, 4:8, :], ps[X1][:].rearrange("p (k s) -> p k s", k=4)).then_inc(S["xe_a"], 1)
                if l == 0:
                    act.sem_inc(S["y_a"], 1)
                else:
                    act.sem_inc(S["y_a"], 1)
                with act.Fori(0, NE // 2) as i:
                    for u in range(2):
                        act.wait_ge(S["moe_used"], i * 6 + (3 * b16 + 3 * u + 1))
                        A(sgl, ps[GB][:], ACT.Silu).then_inc(S["silu"], 1)
                        act.wait_ge(S["xtr"], i * 2 + (b17 + u + 2))
                        copy(xeT[:, 4:8, :], ps[X1][:].rearrange("p (k s) -> p k s", k=4)).then_inc(S["xe_a"], 1)
                        act.wait_ge(S["moe_used"], i * 6 + (3 * b16 + 3 * u + 3))
                        act.wait_ge(S["ystore"], i * 32 + 16 * (b16 + u + 1))
                        copy(y_e[:, 0:512], ps[D0][:]).then_inc(S["y_a"], 1)
                        act.wait_ge(S["y_a"], i * 2 + (b17 + u + 2))
                        act.wait_ge(S["y_d"], i * 2 + (b17 + u + 2))
                        at = act.value_load(offs[0:1, bass.ds(i * 2 + u, 1)], min_val=0, max_val=2 * TT)
                        act.dma_start(Y_s[bass.ds(at, P), :], y_e).then_inc(S["ystore"], 16)
                with long_lists(act, l):
                    O, nj = LONG[l], tiles_of(l)
                    with act.Fori(0, NE) as e:
                        for j in range(nj):
                            act.wait_ge(O["gu"], e * nj + (j + 1))
                            A(sgl, ps[GB][:], ACT.Silu).then_inc(O["silu"], 1)

        @block.vector
        def _(dve):
            E = Eng(dve)
            v = nc.vector

            def st(ins):
                E.step(ins, "vstep")

            def tt(o, a, b, op, name="vstep"):
                E.step(v.tensor_tensor(o, a, b, op), name)
            E.wait("consts", NCONST)
            st(v.tensor_copy(masks[:].rearrange("p a b -> p (a b)"), masks_f))
            tt(lbe[:, 8:12], lbr[:, 0, :], lbr[:, 1, :], ALU.max)
            tt(lbe[:, 0:4], lbr[:, 0, :], lbe[:, 8:12], ALU.subtract)
            tt(lbe[:, 4:8], lbr[:, 1, :], lbe[:, 8:12], ALU.subtract, "lbd")
            E.next("lbx")
            tt(lbe[:, 8:12], lbe[:, 0:4], lbe[:, 4:8], ALU.add)
            st(v.reciprocal(lbe[:, 12:16], lbe[:, 8:12]))
            tt(lbe[:, 0:4], lbe[:, 0:4], lbe[:, 12:16], ALU.mult)
            tt(lbe[:, 4:8], lbe[:, 4:8], lbe[:, 12:16], ALU.mult)
            tt(lb[:, 0, :], lbe[:, 0:4], lbe[:, 0:4], ALU.subtract)
            tt(lb[:, 1, :], lbe[:, 0:4], lbe[:, 4:8], ALU.add)
            tt(lb[:, 1, :], lb[:, 1, :], lbe[:, 0:4], ALU.subtract)
            st(v.tensor_scalar(lb[:], lb[:], 1e-30, None, ALU.max))
            st(v.tensor_scalar(oml[:], lb[:], -1.0, 1.0, ALU.mult, ALU.add))
            E.next("condx")
            for l in range(L):
                nt2 = NT if l == 0 else SEQ // P
                if l:
                    E.wait("moe_used", 3 * NE * l)
                tt(cmix[:, :, 0:64], ones[:, 0:64].unsqueeze(1).broadcast_to([P, KD, 64]),
                   cond[:, 0, :].unsqueeze(2).broadcast_to([P, KD, 64]), ALU.mult)
                tt(cmix[:, :, 64:128], ones[:, 0:64].unsqueeze(1).broadcast_to([P, KD, 64]),
                   cond[:, 1, :].unsqueeze(2).broadcast_to([P, KD, 64]), ALU.mult, "condm")
                E.wait("gains", 16 * NGAIN * (l + 1))
                for s in range(NMOD):
                    m = NMOD * l + s
                    if l and s == 4:
                        E.wait("slab_used", NSL * l + 4)
                        tt(cmix[:, :, 64:128], ones[:, 0:64].unsqueeze(1).broadcast_to([P, KD, 64]),
                           cond[:, 0, :].unsqueeze(2).broadcast_to([P, KD, 64]), ALU.mult, "condm")
                    E.wait("slab_used", NSL * l + s + 1)
                    seg, half = s // 2, s % 2
                    dst = mod[:, seg, 512 * half:512 * half + 512]
                    tt(dst, ps[m % 2][:], dst, ALU.add, "mod_ev")
                    if seg in (1, 4):
                        st(v.scalar_tensor_tensor(out=dst, in0=dst, scalar=1.0, in1=gn[:, seg // 3, 512 * half:512 * half + 512],
                                                  op0=ALU.add, op1=ALU.mult))

                def norm_rows(n, ts, seg):
                    E.next("sqs", n)
                    E.step(v.tensor_scalar(ss[:, 0:n], ss[:, 0:n], 1.0 / D, EPS, ALU.mult, ALU.add), "rstd_d")
                    E.next("rstd_p")
                    for i in range(n):
                        st(v.scalar_tensor_tensor(out=rows[:, i, :], in0=x_sb[:, ts[i], :], scalar=rstd[:, i:i + 1],
                                                  in1=mod[:, seg + 1, :], op0=ALU.mult, op1=ALU.mult))
                        tt(rows[:, i, :], rows[:, i, :], mod[:, seg, :], ALU.add, "rows_d")
                norm_rows(NT, range(NT), 0)
                for kind, a in PROJ:
                    g_ = E.n.get("proj", 0)
                    b = ps[4 + g_ % 4]
                    E.next("proj")
                    if kind == "q":
                        E.next("sgm")
                        tt(q_t[:, a, :], q_t[:, a, :], b[:], ALU.mult, "proj_d")
                    elif kind == "f":
                        d, c = a
                        E.next("sgm")
                        o_ = oml[:, l, 2 * d + c:2 * d + c + 1]
                        l_ = lb[:, l, 2 * d + c:2 * d + c + 1]
                        fs, ks = f_t[d][:, c * 512:(c + 1) * 512], KG[d][:, c * 512:(c + 1) * 512]
                        st(v.tensor_scalar(fs, fs, o_, l_, ALU.mult, ALU.add))
                        E.step(v.tensor_scalar(ks, ks, o_, None, ALU.mult), "proj_d")
                    elif kind == "g":
                        E.next("sgm")
                        tt(g_a[:, a, :], g_a[:, a, :], b[:, 0:256], ALU.mult)
                        gv = g_a[:, a, :].rearrange("p (h d) -> p h d", h=4)
                        tt(gv, gv, gain_o[:].unsqueeze(1).broadcast_to([P, 4, HD]), ALU.mult, "proj_d")
                    elif kind == "b":
                        E.next("bpool")
                        dve.sem_inc(S["proj_d"], 1)
                        E.up("proj_d")
                    else:
                        E.next("proj_x")
                        dve.sem_inc(S["proj_d"], 1)
                        E.up("proj_d")
                tt(sqk, qkv[:, :, 0:QK], qkv[:, :, 0:QK], ALU.mult)
                st(v.tensor_reduce(ssq, sqk.rearrange("p j (h d) -> p j h d", d=HD), AX, ALU.add))
                E.step(v.tensor_scalar(ssq, ssq, 1.0 / HD, EPS, ALU.mult, ALU.add), "kq_d")
                E.next("qk_p")
                for j in range(NT):
                    qk = qkv[:, j, 0:QK].rearrange("p (h d) -> p h d", d=HD)
                    tt(qk, qk, rsq[:, j, :].unsqueeze(2).broadcast_to([P, 10, HD]), ALU.mult)
                    oq = qkr[:, j % 2, 0:512].rearrange("p (c g d) -> p g c d", g=2, d=HD)
                    ok = qkr[:, j % 2, 512:QK]
                    if j >= 2:
                        E.wait("qkt", NT * l + j - 1)
                    if j >= SEQ // P:
                        tt(oq, qk[:, 0:8, :].rearrange("p (g c) d -> p g c d", g=2),
                           gain_qk[:, 0:512].rearrange("p (g c d) -> p g c d", g=2, d=HD), ALU.mult)
                        tt(ok, qkv[:, j, 512:QK], gain_qk[:, 512:QK], ALU.mult, "qk_d2")
                    else:
                        tt(qkv[:, j, 0:QK], qkv[:, j, 0:QK], gain_qk[:], ALU.mult)
                        qp = qkv[:, j, 0:QK].rearrange("p (h e b) -> p h e b", e=HD // 2, b=2)
                        sw = swp[:, j % 2, :].rearrange("p (h e b) -> p h e b", e=HD // 2, b=2)
                        rs = rope[:, j, 1, :].rearrange("p (e b) -> p e b", b=2)
                        for b in range(2):
                            tt(sw[:, :, :, b], qp[:, :, :, 1 - b], rs[:, :, b].unsqueeze(1).broadcast_to([P, 10, HD // 2]), ALU.mult)
                        tt(qk, qk, rope[:, j, 0, :].unsqueeze(1).broadcast_to([P, 10, HD]), ALU.mult)
                        s3 = swp[:, j % 2, :].rearrange("p (h d) -> p h d", d=HD)
                        tt(oq, qk[:, 0:8, :].rearrange("p (g c) d -> p g c d", g=2),
                           s3[:, 0:8, :].rearrange("p (g c) d -> p g c d", g=2), ALU.add)
                        tt(ok, qkv[:, j, 512:QK], swp[:, j % 2, 512:QK], ALU.add, "qk_d2")

                def mixcols(k, a, j):
                    o = actT[a:a + 64, k, :]
                    if l == 0:
                        return o.rearrange("p (i s t) -> p i s t", i=4, s=2)[:, 2 * (j % 2):2 * (j % 2) + 2, j // 2, :]
                    return o[:, j * P:(j + 1) * P]
                units = [(j, h) for j in range(nt2) for h in range(8)]
                for u in range(len(units) + 2):
                    if u < len(units):
                        j, h = units[u]
                        nk = TT if j < SEQ // P else CTX
                        g_ = E.n.get("sc", 0)
                        E.next("sc")
                        st(v.reduce_max(mx[:, u:u + 1], ps[g_ % 3][:, 0:nk], AX))
                        E.step(v.tensor_scalar(nmx[:, u:u + 1], mx[:, u:u + 1], -HD ** -0.5, None, ALU.mult), "scmax")
                    if 1 <= u <= len(units):
                        j, h = units[u - 1]
                        nk = TT if j < SEQ // P else CTX
                        g_ = E.n.get("sexp", 0)
                        E.next("sexp")
                        st(v.reciprocal(rinv[:, u - 1:u], rsum[:, u - 1:u]))
                        E.step(v.tensor_scalar(Pb[:, g_ % 2, 0:nk], Pb[:, g_ % 2, 0:nk], rinv[:, u - 1:u], None, ALU.mult), "pnorm")
                    if u >= 2:
                        j, h = units[u - 2]
                        g_ = E.n.get("pv", 0)
                        E.next("pv")
                        src = ps[5 + g_ % 2][0:64, 0:P]
                        if l == 0:
                            src = src.rearrange("p (i t) -> p i t", i=2)
                        E.step(v.tensor_copy(mixcols(4 + h // 2, 64 * (h % 2), j), src), "pv_ev")
                for c in range(2):
                    E.next("ymm")
                    if l == 0:
                        dst = actT[:, 2 + c, :].rearrange("p (i s t) -> p s i t", i=4, s=2)
                        src = ps[7][:].rearrange("p (s i t) -> p s i t", s=2, i=4)
                    else:
                        dst, src = actT[:, 2 + c, 0:SEQ], ps[7][:, 0:SEQ]
                    E.step(v.tensor_scalar(dst, src, pool_sc[:, c:c + 1], None, ALU.mult), "ymix")
                qflat = q_t.rearrange("p c t -> p (c t)")
                tt(ksum, KG[0], KG[1], ALU.add)
                tt(QF[0], qflat, f_t[0], ALU.mult)
                tt(QF[1], qflat, f_t[1], ALU.mult, "lvdn")
                dve.sem_inc(S["lvup0"], 1)
                dve.sem_inc(S["tot0"], 1)
                def bank_scores(b):
                    J, a = b // 2, b % 2
                    return (A_s.rearrange("p j (c a) t -> p j c a t", a=2)[:, 2 * J:2 * J + 2, :, a, :])
                b4 = lambda m_: m_.unsqueeze(1).unsqueeze(1).broadcast_to([P, 2, 2, P])
                for b in range(4):
                    E.next("lvmm")
                    E.step(v.tensor_tensor(bank_scores(b), ps[b][:].rearrange("p (j c t) -> p j c t", j=2, c=2),
                                           b4(ident[:]), ALU.mult), "lvA")
                tcur, toff = f_t[0], 0
                for lv, w in enumerate(LEVELS):
                    nb = 1024 // (2 * w)
                    E.next("lvcp", 4)
                    q = QF[0].rearrange("p (n a w) -> p n a w", a=2, w=w)
                    k = KG[0].rearrange("p (n a w) -> p n a w", a=2, w=w)
                    t = tcur.rearrange("p (n a) -> p n a", a=2)
                    tt(q[:, :, 1, :], q[:, :, 1, :], t[:, :, 0:1].broadcast_to([P, nb, w]), ALU.mult)
                    tt(k[:, :, 0, :], k[:, :, 0, :], t[:, :, 1:2].broadcast_to([P, nb, w]), ALU.mult)
                    tn = tots[0][:, toff:toff + nb]
                    tt(tn, t[:, :, 0], t[:, :, 1], ALU.mult, "lvdn")
                    tcur, toff = tn, toff + nb
                    for b in range(4):
                        E.next("lvmm")
                        E.step(v.copy_predicated(bank_scores(b), b4(masks[:, lv, :]),
                                                 ps[4 * ((lv + 1) % 2) + b][:].rearrange("p (j c t) -> p j c t", j=2, c=2)), "lvA")
                E.wait("lvup", len(LEVELS) * (l + 1))
                E.wait("kgt_ev", 4 * (l + 1))
                for d in range(2):
                    st(v.memset(S_st[:, d, :, ORDER[d][0], :], 0.0))
                for s in range(3):
                    E.next("umm")
                    tt(U_m[:, s, :].rearrange("p (a v) -> p a v", a=4), ps[4 + s][:].rearrange("p (a v) -> p a v", a=4),
                       headsep[:].unsqueeze(1).broadcast_to([P, 4, P]), ALU.mult)
                    for d in range(2):
                        for c in range(2):
                            j, jn = ORDER[d][s], ORDER[d][s + 1]
                            tot = tots[d][:, toff - nb + 4 * c + j:toff - nb + 4 * c + j + 1]
                            E.step(v.scalar_tensor_tensor(out=S_st[:, d, c, jn, :], in0=S_st[:, d, c, j, :], scalar=tot,
                                                          in1=U_m[:, s, (2 * d + c) * P:(2 * d + c + 1) * P],
                                                          op0=ALU.mult, op1=ALU.add), "vstep")
                dve.sem_inc(S["stv"], 1)
                for j in range(nt2):
                    E.next("o_ev")
                    tt(osq[:, j, :], osb[:, j, :], osb[:, j, :], ALU.mult)
                    st(v.tensor_reduce(ssq[:, j, 0:4], osq[:, j, :].rearrange("p (h d) -> p h d", d=HD), AX, ALU.add))
                    E.step(v.tensor_scalar(ssq[:, j, 0:4], ssq[:, j, 0:4], 1.0 / HD, EPS, ALU.mult, ALU.add), "ogn")
                for j in range(nt2):
                    E.next("rd_p")
                    o3 = osb[:, j, :].rearrange("p (h d) -> p h d", d=HD)
                    tt(o3, o3, rsq[:, j, 0:4].unsqueeze(2).broadcast_to([P, 4, HD]), ALU.mult)
                    tt(osb[:, j, :], osb[:, j, :], g_a[:, j, :], ALU.mult, "o_fin")
                if l:
                    for t_ in range(SEQ // P):
                        st(v.tensor_copy(x_sb[64:128, 2 * t_, :], x_sb[0:64, 2 * t_ + 1, :]))
                for s in range(NWO):
                    for i in range(nt2):
                        g_ = E.n.get("wo", 0)
                        E.next("wo")
                        cs = slice(512 * s, 512 * s + 512)
                        tt(wtmp, ps[g_ % 4][:], mod[:, 2, cs], ALU.mult, "wo_ev")
                        xt = x_sb[:, (i if l == 0 else 2 * i), cs]
                        tt(xt, xt, wtmp, ALU.add, "xdone" if s == NWO - 1 else "vstep")
                norm_rows(nt2, [i if l == 0 else 2 * i for i in range(nt2)], 3)
                R = cut(rtmp, 0)
                n16, n4 = nt2 * NE, nt2 * NG
                scs = R(64)[:, 0:n16]
                sel, t1, t2, oh1, oh2, msl = (R(64)[:, 0:n16] for _ in range(6))
                ohb = rtmp[:, OH0:OH0 + n16]
                m1, m2, gs, t4, ohg, tm = (rsm[:, 16 * a:16 * a + n4] for a in range(6))
                w1, w2, d1 = (wts[:, a, 0:nt2] for a in range(3))
                r3 = lambda a, n: a.rearrange("p (g e) -> p g e", e=n)
                bc = lambda a, g_, n: a.unsqueeze(2).broadcast_to([P, g_, n])
                E.next("sig")
                tt(r3(sel, NE), r3(scs, NE), rb[:].unsqueeze(1).broadcast_to([P, nt2, NE]), ALU.add)

                def first_max(dst, src, groups, n, top, tmp, red):
                    st(v.tensor_reduce(top, r3(src, n), AX, ALU.max))
                    tt(r3(tmp, n), r3(src, n), bc(top, groups, n), ALU.is_equal)
                    tt(r3(tmp, n), r3(tmp, n), rconst[:, 0:n].unsqueeze(1).broadcast_to([P, groups, n]) if n == NE else
                       rconst[:, NE - n:NE].unsqueeze(1).broadcast_to([P, groups, n]), ALU.mult)
                    st(v.tensor_reduce(red, r3(tmp, n), AX, ALU.max))
                    tt(r3(dst, n), r3(tmp, n), bc(red, groups, n), ALU.is_equal)
                first_max(t2, sel, n4, EG, m1, t1, tm)
                st(v.scalar_tensor_tensor(out=t1, in0=t2, scalar=NEG, in1=sel, op0=ALU.mult, op1=ALU.add))
                st(v.tensor_reduce(m2, r3(t1, EG), AX, ALU.max))
                tt(gs, m1, m2, ALU.add)
                first_max(ohg, gs, nt2, NG, m1[:, 0:nt2], t4, tm[:, 0:nt2])
                st(v.memset(msl, -1e4))
                st(v.copy_predicated(r3(msl, EG), bc(ohg.bitcast(i32), n4, EG), r3(sel, EG)))
                first_max(oh1, msl, nt2, NE, m1[:, 0:nt2], t1, tm[:, 0:nt2])
                st(v.scalar_tensor_tensor(out=msl, in0=oh1, scalar=NEG, in1=msl, op0=ALU.mult, op1=ALU.add))
                first_max(oh2, msl, nt2, NE, m1[:, 0:nt2], t1, tm[:, 0:nt2])
                tt(ohb, oh1, oh2, ALU.add, "ohs")
                for w_, o_ in ((w1, oh1), (w2, oh2)):
                    tt(t1, scs, o_, ALU.mult)
                    st(v.tensor_reduce(w_, r3(t1, NE), AX, ALU.add))
                tt(d1, w1, w2, ALU.add)
                st(v.reciprocal(d1, d1))
                tt(w1, w1, d1, ALU.mult)
                tt(w2, w2, d1, ALU.mult)
                E.next("posm")
                pos, cnt = t2, rsm[:, 0:NE]
                st(v.tensor_copy(pos, ps[5][:, 0:n16]))
                st(v.tensor_copy(cnt, ps[5][:, n16:n16 + NE]))
                ca, cb = rsm[:, 16:16 + 18], rsm[:, 48:48 + 18]
                st(v.memset(rsm[:, 16:96], 0.0))
                st(v.tensor_copy(ca[:, 1:NE], cnt[:, 0:NE - 1]))
                for sh in (1, 2, 4, 8):
                    st(v.tensor_copy(cb[:, 0:NE], ca[:, 0:NE]))
                    tt(cb[:, sh:NE], ca[:, sh:NE], ca[:, 0:NE - sh], ALU.add)
                    ca, cb = cb, ca
                off = ca[:, 0:NE]
                tt(r3(t1, NE), r3(pos, NE), off.unsqueeze(1).broadcast_to([P, nt2, NE]), ALU.add)
                for a, o_ in enumerate((oh1, oh2)):
                    tt(sel, t1, o_, ALU.mult)
                    st(v.tensor_reduce(m16[:, 0:nt2], r3(sel, NE), AX, ALU.add))
                    st(v.tensor_copy(idx[:, a, 0:nt2], m16[:, 0:nt2]))
                st(v.memset(ca[:, NE:NE + 2], 2.0 * nt2 * P))
                st(v.tensor_reduce(m16[:, 0:1], cnt, AX, ALU.max))
                st(v.tensor_copy(offs[:, NE + 2:NE + 3], m16[:, 0:1]))
                E.step(v.tensor_copy(offs[:, 0:NE + 2], ca[:, 0:NE + 2]), "slots_d")
                GB, UB, AB, X0, X1, D0, D1 = 0, 1, 2, 3, 4, 5, 6
                b17, b16 = (NE + 1) * l, NE * l
                dve.wait_ge(S["xtr"], b17 + 1)
                v.tensor_copy(xeT[:, 0:4, :], ps[X0][:].rearrange("p (k s) -> p k s", k=4)).then_inc(S["xe_d"], 1)
                dve.sem_inc(S["y_d"], 1)
                with dve.Fori(0, NE // 2) as i:
                    for u in range(2):
                        dve.wait_ge(S["moe_used"], i * 6 + (3 * b16 + 3 * u + 2))
                        dve.wait_ge(S["silu"], i * 2 + (b16 + u + 1))
                        v.tensor_tensor(act_e, sgl, ps[UB][:], ALU.mult).then_inc(S["a_d"], 1)
                        dve.wait_ge(S["xtr"], i * 2 + (b17 + u + 2))
                        v.tensor_copy(xeT[:, 0:4, :], ps[X0][:].rearrange("p (k s) -> p k s", k=4)).then_inc(S["xe_d"], 1)
                        dve.wait_ge(S["atr"], i * 2 + (b16 + u + 1))
                        v.tensor_copy(aT, ps[AB][:].rearrange("p (k s) -> p k s", k=KF)).then_inc(S["aT_d"], 1)
                        dve.wait_ge(S["moe_used"], i * 6 + (3 * b16 + 3 * u + 3))
                        dve.wait_ge(S["ystore"], i * 32 + 16 * (b16 + u + 1))
                        v.tensor_copy(y_e[:, 512:1024], ps[D1][:]).then_inc(S["y_d"], 1)
                with long_lists(dve, l):
                    O, nj = LONG[l], tiles_of(l)
                    with dve.Fori(0, NE) as e:
                        for j in range(nj):
                            dve.wait_ge(O["xT"], e * nj + (j + 1))
                            for a in range(2):
                                v.tensor_copy(xeT[:, 4 * a:4 * a + 4, :], ps[X0 + a][:].rearrange("p (k s) -> p k s", k=4)).then_inc(O["xe"], 1)
                            dve.wait_ge(O["silu"], e * nj + (j + 1))
                            v.tensor_tensor(act_e, sgl, ps[UB][:], ALU.mult).then_inc(O["a"], 1)
                            dve.wait_ge(O["aT"], e * nj + (j + 1))
                            v.tensor_copy(aT, ps[AB][:].rearrange("p (k s) -> p k s", k=KF)).then_inc(O["aTe"], 1)
                            dve.wait_ge(O["y"], e * nj + (j + 1))
                            v.tensor_copy(y_e[:, 0:512], ps[D0][:]).then_inc(O["yh"], 1)
                            v.tensor_copy(y_e[:, 512:1024], ps[D1][:]).then_inc(O["ye"], 1)
                            dve.wait_ge(O["store"], e * (16 * nj) + 16 * (j + 1))
                for i in range(nt2):
                    dve.wait_ge(gats[i], 32 * (l + 1))
                    st(v.tensor_scalar(yg[:, i, 0, :], yg[:, i, 0, :], wts[:, 0, i:i + 1], None, ALU.mult))
                    st(v.scalar_tensor_tensor(out=yg[:, i, 0, :], in0=yg[:, i, 1, :], scalar=wts[:, 1, i:i + 1], in1=yg[:, i, 0, :],
                                              op0=ALU.mult, op1=ALU.add))
                    tt(yg[:, i, 0, :], yg[:, i, 0, :], mod[:, 5, :], ALU.mult)
                    xt = x_sb[:, (i if l == 0 else 2 * i), :]
                    tt(xt, xt, yg[:, i, 0, :], ALU.add, "comb")


def shape_constants(seq, ne, cap):
    import numpy as np
    p = np.arange(128)
    ident = np.eye(128, dtype=np.float32)
    before = (p[:, None] < p[None, :]).astype(np.float32)
    headsep = ((p[:, None] // 64) == (p[None, :] // 64)).astype(np.float32)
    masks = np.stack([((p[:, None] // w) ^ (p[None, :] // w)) == 1 for w in (1, 2, 4, 8, 16, 32, 64)], 1).astype(np.float32)
    t = np.arange(seq)
    inv = np.float32(10000.0) ** (-np.arange(16, dtype=np.float32) / np.float32(16))
    ang = np.concatenate([(t // 64).astype(np.float32)[:, None] * inv, (t % 64).astype(np.float32)[:, None] * inv], -1)
    cos, sin = np.repeat(np.cos(ang), 2, 1), np.repeat(np.sin(ang), 2, 1)
    sin[:, 0::2] *= -1
    rope = np.stack([cos, sin], 1).reshape(seq // 128, 128, 2, 64).transpose(1, 0, 2, 3).astype(np.float32)
    invcnt = np.zeros((128, 2, seq), np.float32)
    for g, w in enumerate((2, 4, 8, 16)):
        cnt = np.minimum(t + w // 2, seq) - np.maximum(t - w // 2, 0)
        invcnt[64 * (g % 2):64 * (g % 2) + 64, g // 2] = np.float32(1) / cnt.astype(np.float32)
    router = np.broadcast_to(np.concatenate([np.arange(ne, 0, -1), cap * np.arange(ne)]).astype(np.float32), (128, 2 * ne))
    return {"k_ident": ident, "k_before": before, "k_headsep": headsep, "k_masks": masks, "k_rope": rope,
            "k_invcnt": invcnt, "k_router": router}


def kernel(**inputs):
    import numpy as _np
    import concourse.bacc as _bacc
    from concourse import mybir as _mybir
    from concourse.bass_utils import run_bass_kernel_spmd as _run

    nc = _bacc.Bacc("TRN2", target_bir_lowering=False, num_devices=1)
    named = dict(inputs)
    seq = inputs["x"].shape[1]
    lbs, psc = _np.asarray(named.pop("hgrn_lb")), _np.asarray(named.pop("pool_scale"))
    named["hgrn_lb_cols"] = lbs.reshape(lbs.shape[0], -1, 128).transpose(0, 2, 1)
    named["pool_scale_cols"] = psc.reshape(psc.shape[0], -1, 128).transpose(0, 2, 1)
    named.update(shape_constants(seq, inputs["router_w"].shape[1], seq + inputs["ctx"].shape[1]))
    arrays, T = {}, {}
    for name, a in named.items():
        a = _np.ascontiguousarray(a)
        arrays["in_" + name] = a
        T[name] = nc.dram_tensor("in_" + name, a.shape, _mybir.dt.from_np(a.dtype), kind="ExternalInput").ap()
    T["out"] = nc.dram_tensor("out_latent", inputs["x"].shape, _mybir.dt.float32, kind="ExternalOutput").ap()
    build(nc, T)
    r = _run(nc, [arrays], core_ids=[0])
    return r.results[0]["out_latent"]
```

```python
def build(nc, T, debug=None):
    import concourse.bass as bass
    from concourse import mybir
    from concourse.alu_op_type import AluOpType as ALU
    from contextlib import ExitStack

    f32, i32, u32, u8 = mybir.dt.float32, mybir.dt.int32, mybir.dt.uint32, mybir.dt.uint8
    ACT, AX = mybir.ActivationFunctionType, mybir.AxisListType.X

    P = 128
    D = T["x"].shape[-1]
    SEQ, CTX = T["x"].shape[1], T["ctx"].shape[1]
    L = T["w_mod"].shape[0]
    KD = D // P
    HD = 64
    TT = SEQ + CTX
    NT = TT // P
    NE = T["router_w"].shape[1]
    NG = 4
    EG = NE // NG
    FE = T["moe_w_gate"].shape[-1]
    KF = FE // P
    CAP = TT
    EPS = 1e-6
    LEVELS = [1, 2, 4, 8, 16, 32, 64]
    SLAB = KD * 512
    NMOD, NIN, NWO = 6 * D // 512, 5, D // 512
    NSL = NMOD + NIN + NWO
    QK = 640
    NEG = -1e30

    ctx = ExitStack()
    with ctx:
        def sb(name, shape, dt=f32):
            return ctx.enter_context(nc.sbuf_tensor(name, shape, dt))

        def sem(name):
            return ctx.enter_context(nc.semaphore(name))

        x_sb = sb("x_sb", [P, NT, D])
        mod = sb("mod", [P, 6, D])
        ring = sb("ring", [P, 2, SLAB])
        actT = sb("actT", [P, KD, TT])
        rows = sb("rows", [P, NT, D])
        arena = sb("arena", [P, 22528])
        ident = sb("ident", [P, P])
        before = sb("before", [P, P])
        ones = sb("ones", [P, P])
        headsep = sb("headsep", [P, P])
        masks = sb("masks", [P, len(LEVELS), P], u8)
        rope = sb("rope", [P, SEQ // P, 2, HD])
        invcnt = sb("invcnt", [P, 2, SEQ])
        gain_qk = sb("gain_qk", [P, 2, HD])
        cmix = sb("cmix", [P, KD, P])
        gain_o = sb("gain_o", [P, HD])
        pool_bd = sb("pool_bd", [P, 2, P])
        pool_sc = sb("pool_sc", [P, 2])
        rw = sb("rw", [P, KD, NE])
        rb = sb("rb", [P, NE])
        small = sb("small", [P, 864])
        idx = sb("idx", [P, 2, NT], u32)
        offs = sb("offs", [P, NE + 4], i32)

        ps = [ctx.enter_context(nc.psum_tensor(f"bank{i}", [P, 512], f32)) for i in range(8)]

        X_s = nc.dram_tensor("expert_in", [2 * TT + CAP, D], f32).ap()
        Y_s = nc.dram_tensor("expert_out", [2 * TT + CAP, D], f32).ap()

        def cut(tensor, start):
            at = [start]

            def take(n):
                at[0] += n
                return tensor[:, at[0] - n:at[0]]
            return take

        take = cut(arena, 0)
        q_t = take(1024).rearrange("p (c t) -> p c t", c=2)
        f_t = [take(1024), take(1024)]
        v_a = take(1024).rearrange("p (j c) -> p j c", j=NT)
        g_a = take(1024).rearrange("p (j c) -> p j c", j=NT)
        qkv = take(3072).rearrange("p (j c) -> p j c", j=NT)
        dpool = take(1024).rearrange("p (c t) -> p c t", c=2)
        hg0 = 9 * 1024
        KG = [take(1024), take(1024)]
        QF = [take(1024), take(1024)]
        ksum = take(1024)
        tots = [take(1024), take(1024)]
        pair_buf = take(4096).rearrange("p (b w n) -> p b w n", b=2, w=2)
        kg_tok = pair_buf.rearrange("p b w n -> p (b w n)")[:, 0:2048].rearrange("p (d c j k) -> p d c j k", d=2, c=2, j=NT)
        osb = pair_buf.rearrange("p b w n -> p (b w n)")[:, 2048:3072].rearrange("p (j c) -> p j c", j=NT)
        osq = pair_buf.rearrange("p b w n -> p (b w n)")[:, 3072:4096].rearrange("p (j c) -> p j c", j=NT)
        S_st = take(2048).rearrange("p (d c j v) -> p d c j v", d=2, c=2, j=NT)
        U_m = arena[:, hg0:hg0 + 1536].rearrange("p (s n) -> p s n", s=3)
        take = cut(arena, hg0 + 2048)
        qkr = take(2 * QK).rearrange("p (b c) -> p b c", b=2)
        swp = take(2 * QK).rearrange("p (b c) -> p b c", b=2)
        qT = take(2048).rearrange("p (c t) -> p c t", c=4)
        kT = take(512)
        Pb = take(2048).rearrange("p (b k) -> p b k", b=4)
        PT = take(1024).rearrange("p (b k) -> p b k", b=2)
        sqk = take(4 * QK).rearrange("p (j c) -> p j c", j=NT)
        take = cut(arena, 0)
        gn = take(2 * D).rearrange("p (a n) -> p a n", a=2)
        take(KD * P)
        junk = take(2 * D).rearrange("p (a n) -> p a n", a=2)
        ZW = 272
        take = cut(rows[:].rearrange("p a b -> p (a b)"), 0)
        Z = [take(4 * ZW).rearrange("p (c s t) -> p c s t", c=2, s=2) for _ in range(3)]
        A_s = rows[:].rearrange("p j (h t) -> p j h t", t=P)[:, :, 0:4, :]
        gn_half = [rows[:].rearrange("p a b -> p (a b)")[:, 3264:3776], arena[:, 22016:22528]]
        masks_f = rows[:, 0, 0:len(LEVELS) * P]
        take = cut(arena, 0)
        slots = [take(SLAB) for _ in range(3)] + [ring[:, 0, :], ring[:, 1, :]] + [take(SLAB)]
        xe = take(2 * D).rearrange("p (b n) -> p b n", b=2)
        xeT = take(KD * P).rearrange("p (k s) -> p k s", k=KD)
        sgl = take(FE)
        act_e = take(FE)
        aT = take(KF * P).rearrange("p (k s) -> p k s", k=KF)
        y_e = take(D)
        wtmp, junk2 = sgl, y_e
        yg = arena[:, 0:4 * 2 * D].rearrange("p (i c n) -> p i c n", i=4, c=2)

        take = cut(small, 0)
        cond = take(2 * KD).rearrange("p (a k) -> p a k", a=2)
        ss = take(NT)
        rstd = take(NT)
        mhalf = take(64)
        ssq = take(NT * 10).rearrange("p (j h) -> p j h", j=NT)
        rsq = take(NT * 10).rearrange("p (j h) -> p j h", j=NT)
        lbr = take(8).rearrange("p (l c) -> p l c", l=2)
        lbe = take(16)
        lb = take(8).rearrange("p (l c) -> p l c", l=2)
        oml = take(8).rearrange("p (l c) -> p l c", l=2)
        rsm = take(96)
        wts = take(12).rearrange("p (a i) -> p a i", a=3)
        m16 = take(16)
        rtmp = small[:, 352:864]
        mx, nmx, rsum, rinv = (rtmp[:, 32 * a:32 * a + 32] for a in range(4))

        rconst = ctx.enter_context(nc.sbuf_tensor("rconst", [P, 2 * NE], f32))[:]
        OH0 = 448
        LONG_FROM = P
        ORDER = [[2, 3, 0, 1], [3, 2, 1, 0]]
        PROJ = ([("cq", j) for j in range(NT)] + [("ck", j) for j in range(NT)]
                + [("q", 0), ("q", 1), ("f", (0, 0)), ("f", (0, 1)), ("f", (1, 0)), ("f", (1, 1))] + [("v", j) for j in range(NT)]
                + [("b", 0), ("b", 1)] + [("g", j) for j in range(NT)])
        QK_NORM = {8: 0, 11: 1, 14: 2, 16: 3}
        QK_TURN = {12: 0, 15: 1, 18: 2, 21: 3}
        NCONST, NGAIN = 16 * 11, 8
        m_ = lambda l, a: [("m", l, s) for s in a]
        w_ = lambda k, l, a: [(k, l, s) for s in a]
        IN_ORDER = (3, 4, 0, 1, 2)
        RING = (m_(0, range(5)) + w_("i", 0, IN_ORDER) + m_(0, range(5, 11)) + w_("o", 0, range(NWO)) + m_(0, [11]) + m_(1, [0, 1])
                + m_(1, range(2, 8)) + w_("i", 1, IN_ORDER) + m_(1, [8, 9, 10]) + w_("o", 1, range(NWO)) + m_(1, [11]))
        RING_LOOP = [RING.index(("m", 1, 2)), len(RING)]
        AMONG = [{4: 5, 9: 6, 14: 7, 19: 8, 24: 9}, {3: 8, 7: 9, 11: 10}]
        IN_STATES = [[10], []]

        def used(key):
            return RING.index(key) + 1

        def mod_bank(l, s):
            return 6 + s % 2 if (l, s) in [(0, a) for a in range(5)] + [(1, a) for a in range(2, 8)] else 7

        def mod_free(l, s):
            m = NMOD * l + s
            return m - 1 if mod_bank(l, s) != mod_bank(*divmod(m - 1, NMOD)) else m
        PH = [2 * NT, 6 * NT]

        names = """consts x_in cond_in gains mod_ev condm wl0 wl1 slab_used mod_mm ht ht_ev sqs rstd_d rstd_p rows_d
        proj proj_a proj_d sgm kq_d qk_p qkt qkt_ev sc scmax sexp pnorm ptr pt_ev pv pv_ev
        zbuf bpool dp ymm ymix tot0 lvcp lvup lvdn lvmm lvA kgt kgt_ev umm umask stv omm o_ev ogn rd_p otr omix wo wo_ev
        lg sig ohs posm slots_d scat xl0 xl1 xtr xe_d xe_a gate silu up a_d atr aT_d down y_d y_a ystore moe_used
        gat comb out_s vstep astep pstep lbx lbd memz pres
        ginit repack xdone proj_x condx lvup0 o_fin qk_d2 modb gnb comb_a comb_v comb_p""".split()
        S = {n: sem("s_" + n) for n in names}
        gats = [sem(f"s_gathered{i}") for i in range(NT)]
        LONG = [{n: sem(f"s_long{l}_{n}") for n in "x xT w xe gu silu a aT aTe y yh ye store".split()} for l in range(L)]
        ml = [sem(f"s_expert_slab{i}") for i in range(6)]

        class Eng:
            def __init__(self, eng):
                self.e, self.n = eng, {}

            def up(self, name, k=1):
                self.n[name] = self.n.get(name, 0) + k
                return self.n[name]

            def wait(self, name, value):
                self.e.wait_ge(S[name], value)

            def next(self, name, k=1):
                self.e.wait_ge(S[name], self.up(name, k))

            def lag(self, name, value):
                if value > 0:
                    self.e.wait_ge(S[name], value)

            def step(self, ins, name):
                ins.then_inc(S[name], 1)
                self.e.wait_ge(S[name], self.up(name))

        block = ctx.enter_context(nc.Block())

        def w_view(w, cols):
            return w[:, cols].rearrange("(p k) n -> p k n", k=KD)

        def tiles_of(l):
            return (NT if l == 0 else SEQ // P)

        def long_lists(eng, l):
            n_max = eng.value_load(offs[0:1, NE + 2:NE + 3], min_val=0, max_val=TT)
            return eng.If(n_max > LONG_FROM)

        @block.sync
        def _(sp):
            E = Eng(sp)
            n = [0]

            def slabs(upto):
                while n[0] < upto:
                    kind, l, c = RING[n[0]]
                    width = 256 if (kind, c) == ("i", 4) else 512
                    cols = slice(512 * c, 512 * c + width)
                    if kind == "o":
                        src = T["w_out"][l][:, cols].rearrange("(k p) n -> p k n", p=P)
                    else:
                        src = w_view(T["w_mod" if kind == "m" else "w_in"][l], cols)
                    E.lag("slab_used", n[0] - 1)
                    if n[0] in (RING_LOOP[0], RING_LOOP[0] + 1):
                        E.wait("moe_used", 3 * NE - 1)
                    sp.dma_start(ring[:, n[0] % 2, :].rearrange("p (k n) -> p k n", k=KD)[:, :, 0:width], src).then_inc(S[f"wl{n[0] % 2}"], 16)
                    n[0] += 1

            slabs(2)
            for a, src in enumerate((T["x"][0], T["ctx"][0])):
                sp.dma_start(x_sb[64 * a:64 * a + 64, :, :], src.rearrange("(i p) d -> p i d", p=64)).then_inc(S["x_in"], 16)
            for l in range(L):
                slabs(used(("o", l, NWO - 1)))
                wg, wu, wd = T["moe_w_gate"][l], T["moe_w_up"][l], T["moe_w_down"][l]

                def expert_slab(e, u, k):
                    w = (wg, wu, wd)[k]
                    kk = KF if k == 2 else KD
                    src = w[e] if isinstance(e, int) else w[bass.ds(e, 1)].rearrange("o a b -> (o a) b")
                    src = src.rearrange("(p k) n -> p (k n)", k=kk)
                    sp.dma_start(slots[3 * u + k], src).then_inc(ml[3 * u + k], 16)

                def expert_rows(e, u):
                    at = sp.value_load(offs[0:1, e:e + 1] if isinstance(e, int) else offs[0:1, bass.ds(e, 1)],
                                       min_val=0, max_val=2 * TT)
                    sp.dma_start(xe[:, u, :], X_s[bass.ds(at, P), :]).then_inc(S[f"xl{u}"], 16)

                slabs(used(("m", l, 11)))
                E.wait("slab_used", used(("o", l, NWO - 1)))
                for k in range(3):
                    expert_slab(0, 0, k)
                slabs(RING_LOOP[l])
                expert_slab(1, 1, 2)
                E.next("scat", 16 * 2 * (NT if l == 0 else SEQ // P))
                E.next("slots_d", 1)
                for u in range(2):
                    expert_rows(u, u)
                E.wait("slab_used", RING_LOOP[l])
                for k in range(2):
                    expert_slab(1, 1, k)
                with sp.Fori(0, NE // 2 - 1) as i:
                    for u in range(2):
                        for k in range(3):
                            sp.wait_ge(S["moe_used"], i * 6 + (3 * NE * l + 3 * u + k + 1))
                            expert_slab(i * 2 + (2 + u), u, k)
                        sp.wait_ge(S["xtr"], i * 2 + ((NE + 1) * l + u + 1))
                        expert_rows(i * 2 + (2 + u), u)
                E.wait("xtr", (NE + 1) * l + NE - 1)
                expert_rows(NE, 0)
                E.wait("moe_used", 3 * NE * (l + 1))
                E.wait("ystore", 16 * (NE * (l + 1) + 1))
                with long_lists(sp, l):
                    O, nj = LONG[l], tiles_of(l)
                    with sp.Fori(0, NE) as e:
                        for k in range(3):
                            w, kk = (wg, wu, wd)[k], KF if k == 2 else KD
                            src = w[bass.ds(e, 1)].rearrange("o a b -> (o a) b").rearrange("(p k) n -> p (k n)", k=kk)
                            sp.dma_start(slots[k], src).then_inc(O["w"], 16)
                        at = sp.value_load(offs[0:1, bass.ds(e, 1)], min_val=0, max_val=2 * nj * P)
                        for j in range(nj):
                            sp.dma_start(xe[:, 0, :], X_s[bass.ds(at + j * P, P), :]).then_inc(O["x"], 16)
                            sp.wait_ge(O["yh"], e * nj + (j + 1))
                            sp.wait_ge(O["ye"], e * nj + (j + 1))
                            sp.dma_start(Y_s[bass.ds(at + j * P, P), :], y_e).then_inc(O["store"], 16)
            E.wait("comb", NT // 2 + 1)
            E.wait("comb_p", NT // 2 + 1)
            sp.dma_start(T["out"][0].rearrange("(i p) d -> p i d", p=P), x_sb[:, 0::2, :]).then_inc(S["out_s"], 16)
            E.wait("out_s", 16)

        @block.gpsimd
        def _(pool):
            E = Eng(pool)
            g = nc.gpsimd

            def powr(dst, src, l_src, sem_out):
                E.step(g.tensor_tensor(dst, src, mhalf[:, 0:src.shape[-1]] if len(src.shape) == 2 else
                                       mhalf[:, 0:src.shape[1] * src.shape[2]].rearrange("p (a b) -> p a b", a=src.shape[1]),
                                       ALU.pow), sem_out)

            E.step(g.memset(mhalf, -0.5), "pstep")
            g.memset(pool_bd[:], 0.0).then_inc(S["memz"], 1)
            g.memset(ones[:], 1.0).then_inc(S["memz"], 1)
            g.memset(actT[:], 0.0).then_inc(S["memz"], 1)
            for l in range(L):
                nt2 = NT if l == 0 else SEQ // P
                E.next("rstd_d")
                powr(rstd[:, 0:NT], ss[:, 0:NT], None, "rstd_p")
                M = 8
                E.wait("ht", PH[l])
                for z in Z:
                    E.step(g.memset(z[:, :, :, :], 0.0), "zbuf")
                E.next("kq_d")
                powr(rsq, ssq, None, "qk_p")
                E.next("bpool", 2)
                n_ = ZW - 1
                E.step(g.tensor_tensor(Z[1][:, :, :, 0:n_], Z[0][:, :, :, 0:n_], Z[0][:, :, :, 1:n_ + 1], ALU.add), "pstep")
                x0 = lambda p0, c: Z[0][p0:p0 + 64, c, :, M:M + SEQ]
                dv = lambda p0, c: dpool[p0:p0 + 64, c, :].rearrange("p (s t) -> p s t", s=2)
                ic = lambda p0, c: invcnt[p0:p0 + 64, c, :].unsqueeze(1).broadcast_to([64, 2, SEQ])

                def finish(zsum, p0, c, half):
                    E.step(g.tensor_tensor(dv(p0, c), zsum[p0:p0 + 64, c, :, M - half:M - half + SEQ], ic(p0, c), ALU.mult), "pstep")
                    E.step(g.tensor_tensor(dv(p0, c), dv(p0, c), x0(p0, c), ALU.subtract), "dp")
                finish(Z[1], 0, 0, 1)
                n_ -= 2
                E.step(g.tensor_tensor(Z[2][:, :, :, 0:n_], Z[1][:, :, :, 0:n_], Z[1][:, :, :, 2:n_ + 2], ALU.add), "pstep")
                finish(Z[2], 64, 0, 2)
                n_ -= 4
                E.step(g.tensor_tensor(Z[1][:, 1, :, 0:n_], Z[2][:, 1, :, 0:n_], Z[2][:, 1, :, 4:n_ + 4], ALU.add), "pstep")
                finish(Z[1], 0, 1, 4)
                n_ -= 8
                E.step(g.tensor_tensor(Z[2][64:128, 1, :, 0:n_], Z[1][64:128, 1, :, 0:n_], Z[1][64:128, 1, :, 8:n_ + 8], ALU.add), "pstep")
                finish(Z[2], 64, 1, 8)
                E.next("tot0")
                tcur = f_t[1]
                toff = 0
                for w in LEVELS:
                    E.next("lvcp", 4)
                    q = QF[1].rearrange("p (n a w) -> p n a w", a=2, w=w)
                    k = KG[1].rearrange("p (n a w) -> p n a w", a=2, w=w)
                    t = tcur.rearrange("p (n a) -> p n a", a=2)
                    nb = 1024 // (2 * w)
                    E.step(g.tensor_tensor(q[:, :, 0, :], q[:, :, 0, :], t[:, :, 1:2].broadcast_to([P, nb, w]), ALU.mult), "pstep")
                    E.step(g.tensor_tensor(k[:, :, 1, :], k[:, :, 1, :], t[:, :, 0:1].broadcast_to([P, nb, w]), ALU.mult), "pstep")
                    tn = tots[1][:, toff:toff + nb]
                    E.step(g.tensor_tensor(tn, t[:, :, 0], t[:, :, 1], ALU.mult), "lvup")
                    tcur = tn
                    toff += nb
                for j in range(nt2):
                    E.next("ogn")
                    powr(rsq[:, j, 0:4], ssq[:, j, 0:4], None, "rd_p")
                E.next("rstd_d")
                powr(rstd[:, 0:nt2], ss[:, 0:nt2], None, "rstd_p")
                E.next("slots_d")
                if l == 0:
                    E.wait("ginit", 16)
                tiles = range(NT) if l == 0 else range(SEQ // P)
                for i in tiles:
                    for c in range(2):
                        g.indirect_dma_start(out=X_s, out_offset=bass.IndirectOffsetOnAxis(ap=idx[:, c, i:i + 1], axis=0),
                                             in_=rows[:, i, :], in_offset=None).then_inc(S["scat"], 16)
                E.wait("ystore", 16 * (NE * (l + 1) + 1))
                with long_lists(pool, l):
                    pool.wait_ge(LONG[l]["store"], 16 * NE * tiles_of(l))
                for i in tiles:
                    for c in range(2):
                        g.indirect_dma_start(out=yg[:, i, c, :], out_offset=None, in_=Y_s[0:2 * TT, :],
                                             in_offset=bass.IndirectOffsetOnAxis(ap=idx[:, c, i:i + 1], axis=0)
                                             ).then_inc(gats[i], 16)
                for i in tiles:
                    if i % 2:
                        E.n["comb_v"] = E.n.get("comb_v", 0) + 1
                        E.wait("comb_v", E.n["comb_v"])
                        E.step(g.tensor_tensor(yg[:, i, 0, :], yg[:, i, 0, :], mod[:, 5, :], ALU.mult), "pstep")
                        xt = x_sb[:, (i if l == 0 else 2 * i), :]
                        g.tensor_tensor(xt, xt, yg[:, i, 0, :], ALU.add).then_inc(S["comb_p"], 1)

        @block.tensor
        def _(pe):
            E = Eng(pe)
            mm, tr = nc.tensor.matmul, nc.tensor.transpose
            n = [0]

            def slab_in(key):
                assert RING[n[0]] == key
                s = n[0] % 2
                pe.wait_ge(S[f"wl{s}"], 16 * (n[0] // 2 + 1))
                n[0] += 1
                return ring[:, s, :].rearrange("p (k n) -> p k n", k=KD)

            def rows_transposed(i):
                for kk in range(2):
                    g_ = E.n.get("ht", 0)
                    E.lag("ht_ev", g_ - 1)
                    for k in range(4):
                        last = tr(ps[2 + g_ % 2][:, k * P:(k + 1) * P], rows[:, i, 4 * kk + k::KD], ident[:])
                    last.then_inc(S["ht"], 1)
                    E.up("ht")

            def mod_slab(l, s):
                if (l, s) in ((0, 0), (1, 4)):
                    E.next("condm")
                E.lag("mod_ev", mod_free(l, s))
                w = slab_in(("m", l, s))
                for k in range(KD):
                    last = mm(ps[mod_bank(l, s)][:], cmix[:, k, :], w[:, k, :], start=(k == 0), stop=(k == KD - 1))
                last.then_inc(S["slab_used"], 1)

            for l in range(L):
                nt2 = NT if l == 0 else SEQ // P
                for s in (range(5) if l == 0 else [7]):
                    mod_slab(l, s)
                if l == 0:
                    E.wait("consts", NCONST)
                    E.wait("memz", 3)
                for i in range(NT):
                    E.next("rows_d")
                    rows_transposed(i)
                E.wait("ht_ev", E.n["ht"])
                pg = [0]

                def proj(out, k, lhsT, rhs):
                    return mm(out, lhsT, rhs, start=(k == 0), stop=(k == KD - 1))

                def group():
                    b = 4 + E.n.get("proj", 0) % 4
                    E.lag("proj_d", E.n.get("proj", 0) - 3)
                    E.up("proj")
                    return ps[b]
                def qk_turned(j):
                    E.next("qk_d2")
                    g_ = E.n.get("qkt", 0)
                    E.lag("qkt_ev", g_ - 1)
                    for c in range(4):
                        tr(ps[g_ % 2][:, c * P:(c + 1) * P], qkr[:, j % 2, c * P:(c + 1) * P], ident[:])
                    tr(ps[2 + g_ % 2][:, 0:P], qkr[:, j % 2, 4 * P:5 * P], ident[:]).then_inc(S["qkt"], 1)
                    E.up("qkt")

                E.wait("mod_ev", NMOD * l + (5 if l == 0 else 8))
                gi = 0
                for s in IN_ORDER:
                    tc, tk = [((0, 128, 256, 384), None), ((0, 128), (256, 512)), ((256, 384), (0, 256)),
                              ((), (0, 512)), ((), (0, 256))][s]
                    w = slab_in(("i", l, s))
                    jobs = [(c, None) for c in tc] + [(None, j) for j in (range(NT) if tk else ())]
                    for c, j in jobs:
                        b = group()
                        for k in range(KD):
                            if j is None:
                                last = proj(b[:, :], k, w[:, k, c:c + 128], actT[:, k, :])
                            else:
                                last = proj(b[:, 0:tk[1] - tk[0]], k, actT[:, k, j * P:(j + 1) * P], w[:, k, tk[0]:tk[1]])
                        last.then_inc(S["proj"], 1)
                        if (c, j) == jobs[-1]:
                            pe.wait_ge(S["proj"], E.n["proj"])
                            pe.sem_inc(S["slab_used"], 1)
                        if gi in QK_TURN:
                            qk_turned(QK_TURN[gi])
                        gi += 1
                E.wait("qkt_ev", E.n["qkt"])
                E.wait("proj_d", E.n["proj"])
                units = [(j, h) for j in range(nt2) for h in range(8)]

                def scores(u):
                    j, h = units[u]
                    a = 64 * (h // 4)
                    g_ = E.n.get("sc", 0)
                    E.lag("sexp", g_ - 2)
                    keys = slice(0, TT) if j < SEQ // P else slice(SEQ, TT)
                    nk = keys.stop - keys.start
                    mm(ps[g_ % 3][:, 0:nk], qT[a:a + 64, h % 4, j * P:(j + 1) * P], kT[a:a + 64, keys],
                       start=True, stop=True).then_inc(S["sc"], 1)
                    E.up("sc")

                def values(u):
                    j, h = units[u]
                    kt = range(NT) if j < SEQ // P else range(SEQ // P, NT)
                    E.next("pnorm")
                    g_ = E.n.get("ptr", 0)
                    E.lag("pt_ev", g_ - 1)
                    for m, _ in enumerate(kt):
                        last = tr(ps[3 + g_ % 2][:, m * P:(m + 1) * P], Pb[:, g_ % 4, m * P:(m + 1) * P], ident[:])
                    last.then_inc(S["ptr"], 1)
                    E.up("ptr")
                    return g_, kt

                def outv(u, g_, kt):
                    j, h = units[u]
                    E.next("pt_ev")
                    E.lag("pv_ev", g_ - 1)
                    for m, t_ in enumerate(kt):
                        last = mm(ps[5 + g_ % 2][0:64, 0:P], qkv[:, t_, QK + 64 * (h // 4):QK + 64 * (h // 4) + 64],
                                  PT[:, g_ % 2, m * P:(m + 1) * P], start=(m == 0), stop=(m == len(kt) - 1))
                    last.then_inc(S["pv"], 1)
                    E.up("pv")
                for u in range(3):
                    scores(u)
                turned = {}
                for u in range(len(units) + 2):
                    if 1 <= u and u + 2 < len(units):
                        scores(u + 2)
                    if u >= 2:
                        outv(u - 2, *turned.pop(u - 2))
                    if u in AMONG[l]:
                        mod_slab(l, AMONG[l][u])
                    if u < len(units):
                        turned[u] = values(u)
                E.wait("pv_ev", E.n["pv"])
                E.wait("mod_ev", NMOD * l + max(AMONG[l].values()) + 1)
                E.next("dp", 4)
                for c in range(2):
                    mm(ps[7][:, :], pool_bd[:, c, :], dpool[:, c, :], start=True, stop=True).then_inc(S["ymm"], 1)
                    E.next("ymix")
                E.next("lvdn")
                def pair_products(keys, queries, bank0):
                    for J in range(NT // 2):
                        for m in range(4):
                            j, c = 2 * J + m // 2, m % 2
                            for a in range(2):
                                if m == 0:
                                    E.lag("lvA", E.n["lvmm"] + a - 7 if "lvmm" in E.n else 0)
                                last = mm(ps[bank0 + 2 * J + a][:, m * P:(m + 1) * P],
                                          keys[64 * a:64 * a + 64, c, j * P:(j + 1) * P],
                                          queries[64 * a:64 * a + 64, c, j * P:(j + 1) * P], start=True, stop=True)
                                if m == 3:
                                    last.then_inc(S["lvmm"], 1)
                        E.up("lvmm", 2)
                pair_products(ksum.rearrange("p (c t) -> p c t", c=2), q_t, 0)
                for v, w in enumerate(LEVELS):
                    E.next("lvcp", 4)
                    pb = pair_buf[:, v % 2].rearrange("p w (c t) -> p w c t", c=2)
                    pair_products(pb[:, 1], pb[:, 0], 4 * ((v + 1) % 2))
                E.wait("lvA", E.n["lvmm"])
                E.next("lvdn", len(LEVELS))
                E.next("lvup", len(LEVELS))
                for d in range(2):
                    for c in range(2):
                        for j in range(NT):
                            last = tr(ps[2 * d + c][:, j * P:(j + 1) * P], KG[d][:, c * 512 + j * P:c * 512 + (j + 1) * P], ident[:])
                        last.then_inc(S["kgt"], 1)
                E.next("kgt_ev", 4)
                order = ORDER
                for s in range(3):
                    for d in range(2):
                        for c in range(2):
                            j = order[d][s]
                            last = mm(ps[4 + s][:, (2 * d + c) * P:(2 * d + c + 1) * P], kg_tok[:, d, c, j, :],
                                      v_a[:, j, c * P:(c + 1) * P], start=True, stop=True)
                    last.then_inc(S["umm"], 1)
                for s in IN_STATES[l]:
                    mod_slab(l, s)
                E.next("stv")
                E.wait("lvA", E.n["lvmm"])
                for j in range(nt2):
                    for c in range(2):
                        for a in range(2):
                            o, hc = ps[j][:, (2 * c + a) * HD:(2 * c + a + 1) * HD], slice(a * HD, (a + 1) * HD)
                            for d in range(2):
                                mm(o, QF[d][:, c * 512 + j * P:c * 512 + (j + 1) * P], S_st[:, d, c, j, hc], start=(d == 0), stop=False)
                            last = mm(o, A_s[:, j, 2 * c + a, :], v_a[:, j, (2 * c + a) * HD:(2 * c + a + 1) * HD], start=False, stop=True)
                    last.then_inc(S["omm"], 1)
                for j in range(nt2):
                    E.next("o_fin")
                    for c in range(2):
                        last = tr(ps[4 + j][:, c * P:(c + 1) * P], osb[:, j, c * P:(c + 1) * P], ident[:])
                    last.then_inc(S["otr"], 1)
                E.next("omix", nt2)
                for s in range(NWO):
                    w = slab_in(("o", l, s))
                    for i in range(nt2):
                        g_ = E.n.get("wo", 0)
                        E.lag("wo_ev", g_ - 3)
                        for k in range(KD):
                            last = mm(ps[g_ % 4][:], actT[:, k, i * P:(i + 1) * P], w[:, k, :], start=(k == 0), stop=(k == KD - 1))
                        last.then_inc(S["wo"], 1)
                        E.up("wo")
                    pe.wait_ge(S["wo"], E.n["wo"])
                    pe.sem_inc(S["slab_used"], 1)
                mod_slab(l, 11)
                E.wait("wo_ev", E.n["wo"])

                def logits(i):
                    E.wait("ht_ev", E.n["ht"] - 2 * (nt2 - 1 - i) if i == nt2 - 1 else E.n["ht"] - 2)
                    for k in range(KD):
                        last = mm(ps[4][:, i * NE:(i + 1) * NE], actT[:, k, i * P:(i + 1) * P], rw[:, k, :],
                                  start=(k == 0), stop=(k == KD - 1))
                    return last
                for i in range(nt2):
                    E.next("rows_d")
                    rows_transposed(i)
                    if i:
                        logits(i - 1)
                logits(nt2 - 1).then_inc(S["lg"], 1)
                if l == 0:
                    mod_slab(1, 0)
                E.next("ohs")
                oh = rtmp[:, OH0:OH0 + nt2 * NE].rearrange("p (i e) -> p i e", e=NE)
                for i in range(nt2 + 1):
                    for j in range(min(i + 1, nt2)):
                        lhs = before if j == i else ones
                        last = mm(ps[5][:, i * NE:(i + 1) * NE], lhs[:], oh[:, j, :], start=(j == 0), stop=(j == min(i, nt2 - 1)))
                last.then_inc(S["posm"], 1)
                if l == 0:
                    mod_slab(1, 1)
                E.next("slots_d")
                GB, UB, AB, X0, X1, D0, D1 = 0, 1, 2, 3, 4, 5, 6
                b17 = (NE + 1) * l
                b16 = NE * l

                def x_transposed(u):
                    for k in range(KD):
                        last = tr(ps[X0 + k // 4][:, (k % 4) * P:(k % 4 + 1) * P], xe[:, u, k::KD], ident[:])
                    last.then_inc(S["xtr"], 1)
                pe.wait_ge(S["xl0"], 16 * (9 * l + 1))
                x_transposed(0)
                with pe.Fori(0, NE // 2) as i:
                    for u in range(2):
                        wg = slots[3 * u].rearrange("p (k n) -> p k n", k=KD)
                        wu = slots[3 * u + 1].rearrange("p (k n) -> p k n", k=KD)
                        wd = slots[3 * u + 2].rearrange("p (k n) -> p k n", k=KF)
                        pe.wait_ge(S["xe_d"], i * 2 + (b17 + u + 1))
                        pe.wait_ge(S["xe_a"], i * 2 + (b17 + u + 1))
                        pe.wait_ge(ml[3 * u], i * 16 + 16 * (NE // 2 * l + 1))
                        for k in range(KD):
                            last = mm(ps[GB][:], xeT[:, k, :], wg[:, k, :], start=(k == 0), stop=(k == KD - 1))
                        last.then_inc(S["moe_used"], 1)
                        pe.wait_ge(ml[3 * u + 1], i * 16 + 16 * (NE // 2 * l + 1))
                        for k in range(KD):
                            last = mm(ps[UB][:], xeT[:, k, :], wu[:, k, :], start=(k == 0), stop=(k == KD - 1))
                        last.then_inc(S["moe_used"], 1)
                        if u == 0:
                            pe.wait_ge(S["xl1"], i * 16 + 16 * (8 * l + 1))
                        else:
                            pe.wait_ge(S["xl0"], i * 16 + 16 * (9 * l + 2))
                        x_transposed(1 - u)
                        pe.wait_ge(S["a_d"], i * 2 + (b16 + u + 1))
                        for k in range(KF):
                            last = tr(ps[AB][:, k * P:(k + 1) * P], act_e[:, k::KF], ident[:])
                        last.then_inc(S["atr"], 1)
                        pe.wait_ge(S["aT_d"], i * 2 + (b16 + u + 1))
                        pe.wait_ge(S["y_d"], i * 2 + (b17 + u + 1))
                        pe.wait_ge(S["y_a"], i * 2 + (b17 + u + 1))
                        pe.wait_ge(ml[3 * u + 2], i * 16 + 16 * (NE // 2 * l + 1))
                        for h in range(2):
                            for k in range(KF):
                                last = mm(ps[D0 + h][:], aT[:, k, :], wd[:, k, h * 512:(h + 1) * 512], start=(k == 0), stop=(k == KF - 1))
                        last.then_inc(S["moe_used"], 1)
                E.wait("y_d", b17 + NE + 1)
                E.wait("y_a", b17 + NE + 1)
                E.wait("xe_d", b17 + NE + 1)
                E.wait("xe_a", b17 + NE + 1)
                with long_lists(pe, l):
                    O, nj = LONG[l], tiles_of(l)
                    wg, wu = (slots[k].rearrange("p (k n) -> p k n", k=KD) for k in range(2))
                    wd = slots[2].rearrange("p (k n) -> p k n", k=KF)
                    with pe.Fori(0, NE) as e:
                        for j in range(nj):
                            pe.wait_ge(O["x"], e * (16 * nj) + 16 * (j + 1))
                            for k in range(KD):
                                last = tr(ps[X0 + k // 4][:, (k % 4) * P:(k % 4 + 1) * P], xe[:, 0, k::KD], ident[:])
                            last.then_inc(O["xT"], 1)
                            pe.wait_ge(O["xe"], e * (2 * nj) + 2 * (j + 1))
                            pe.wait_ge(O["w"], e * 48 + 48)
                            for bank, w in ((GB, wg), (UB, wu)):
                                for k in range(KD):
                                    last = mm(ps[bank][:], xeT[:, k, :], w[:, k, :], start=(k == 0), stop=(k == KD - 1))
                            last.then_inc(O["gu"], 1)
                            pe.wait_ge(O["a"], e * nj + (j + 1))
                            for k in range(KF):
                                last = tr(ps[AB][:, k * P:(k + 1) * P], act_e[:, k::KF], ident[:])
                            last.then_inc(O["aT"], 1)
                            pe.wait_ge(O["aTe"], e * nj + (j + 1))
                            for h in range(2):
                                for k in range(KF):
                                    last = mm(ps[D0 + h][:], aT[:, k, :], wd[:, k, h * 512:(h + 1) * 512], start=(k == 0), stop=(k == KF - 1))
                            last.then_inc(O["y"], 1)
                            pe.wait_ge(O["yh"], e * nj + (j + 1))
                            pe.wait_ge(O["ye"], e * nj + (j + 1))
                if l == 0:
                    E.wait("mod_ev", NMOD + 2)
                    for s in range(2, 7):
                        mod_slab(1, s)

        @block.scalar
        def _(act):
            E = Eng(act)
            A = nc.scalar.activation

            def copy(o, i):
                return A(o, i, ACT.Copy)

            def bias(l, a, b):
                act.dma_start(mod[:, a:b, :].rearrange("p a n -> p (a n)"),
                              T["b_mod"][l:l + 1, a * D:b * D].broadcast_to([P, (b - a) * D])).then_inc(S["modb"], 16)

            def norm_gain(l, name):
                for h in range(2):
                    act.dma_start(gn_half[h], T[name][l:l + 1, 512 * h:512 * h + 512].broadcast_to([P, 512])).then_inc(S["gnb"], 16)

            def gains(l):
                act.dma_start(gain_qk[:, 0, :], T["q_norm_g"][l:l + 1, :].broadcast_to([P, HD])).then_inc(S["gains"], 16)
                act.dma_start(gain_qk[:, 1, :], T["k_norm_g"][l:l + 1, :].broadcast_to([P, HD])).then_inc(S["gains"], 16)
                act.dma_start(gain_o[:], T["hgrn_norm_g"][l:l + 1, :].broadcast_to([P, HD])).then_inc(S["gains"], 16)
                for gi in range(4):
                    a = 64 * (gi % 2)
                    act.dma_start(pool_bd[a:a + 64, gi // 2, a:a + 64], T["pool_w"][l, gi]).then_inc(S["gains"], 16)
                act.dma_start(pool_sc[:], T["pool_scale_cols"][l]).then_inc(S["gains"], 16)

            act.dma_start(cond[:, 0, :], T["c"][0].rearrange("(p k) -> p k", k=KD)).then_inc(S["cond_in"], 16)
            act.dma_start(cond[:, 1, :], T["c_ctx"].rearrange("(p k) -> p k", k=KD)).then_inc(S["cond_in"], 16)
            E.wait("cond_in", 32)
            E.step(A(cond[:], cond[:], ACT.Silu), "condx")
            bias(0, 0, 6)
            act.dma_start(gn[:, 0, :], T["norm1_g"][0:1, :].broadcast_to([P, D])).then_inc(S["modb"], 16)
            act.dma_start(ident[:], T["k_ident"]).then_inc(S["consts"], 16)
            act.dma_start(before[:], T["k_before"]).then_inc(S["consts"], 16)
            act.dma_start(headsep[:], T["k_headsep"]).then_inc(S["consts"], 16)
            act.dma_start(masks_f, T["k_masks"].rearrange("p a b -> p (a b)")).then_inc(S["consts"], 16)
            act.dma_start(rope[:], T["k_rope"]).then_inc(S["consts"], 16)
            act.dma_start(invcnt[:], T["k_invcnt"]).then_inc(S["consts"], 16)
            act.dma_start(rw[:], T["router_w"].rearrange("(p k) e -> p k e", k=KD)).then_inc(S["consts"], 16)
            act.dma_start(rb[:], T["router_b"].rearrange("(a e) -> a e", a=1).broadcast_to([P, NE])).then_inc(S["consts"], 16)
            act.dma_start(rconst, T["k_router"]).then_inc(S["consts"], 16)
            for l_ in range(2):
                act.dma_start(lbr[:, l_, :], T["hgrn_lb_cols"][l_]).then_inc(S["consts"], 16)
            E.wait("memz", 3)
            gains(0)
            act.dma_start(X_s[2 * TT:2 * TT + CAP, :].rearrange("(a p) d -> p a d", p=P),
                          actT[:].rearrange("p k t -> p (k t)")[:, 0:4 * D].rearrange("p (a d) -> p a d", a=4)).then_inc(S["ginit"], 16)
            act.dma_start(Y_s[0:P, 0:64], actT[:, 0, 0:64]).then_inc(S["ystore"], 16)
            E.next("lbd")
            E.step(A(lbe[:, 0:8], lbe[:, 0:8], ACT.Exp), "lbx")
            E.wait("ginit", 16)
            E.wait("ystore", 16)
            for l in range(L):
                nt2 = NT if l == 0 else SEQ // P
                E.wait("x_in", 32)

                def squares(tiles, ts, jb):
                    for i in range(tiles):
                        if l:
                            E.wait("comb_p" if i % 2 else "comb", i // 2 + 1)
                        E.step(A(jb, x_sb[:, ts[i], :], ACT.Square, accum_out=ss[:, i:i + 1]), "sqs")
                squares(NT, range(NT), junk2 if l else junk[:, 0, :])

                def ht_evac(n, mixed):
                    for _ in range(n):
                        for kk in range(2):
                            g_ = E.n.get("ht", 0)
                            i = htile[0]
                            E.next("ht")
                            if mixed:
                                dst = actT[:].rearrange("p k (s t) -> p (k s) t", s=2)[:, 8 * kk:8 * kk + 8, 64 * i:64 * i + 64]
                                src = ps[2 + g_ % 2][:].rearrange("p (a t) -> p a t", t=64)
                            else:
                                dst = actT[:, 4 * kk:4 * kk + 4, i * P:(i + 1) * P]
                                src = ps[2 + g_ % 2][:].rearrange("p (a t) -> p a t", t=P)
                            E.step(copy(dst, src), "ht_ev")
                        htile[0] += 1
                htile = [0]
                if l:
                    bias(1, 5, 6)
                ht_evac(NT, True)
                norm_gain(l, "norm2_g")
                def qk_out(j):
                    g_ = E.n.get("qkt", 0)
                    E.next("qkt")
                    E.step(copy(qT[:, :, j * P:(j + 1) * P], ps[g_ % 2][:].rearrange("p (c t) -> p c t", c=4)), "astep")
                    E.step(copy(kT[:, j * P:(j + 1) * P], ps[2 + g_ % 2][:, 0:P]), "qkt_ev")
                for gi, (kind, a) in enumerate(PROJ):
                    g_ = E.n.get("proj", 0)
                    b = ps[4 + g_ % 4]
                    E.next("proj")
                    if kind == "q":
                        E.step(A(q_t[:, a, :], b[:], ACT.Sigmoid), "sgm")
                    elif kind == "f":
                        d, c = a
                        E.step(A(f_t[d][:, c * 512:(c + 1) * 512], b[:], ACT.Sigmoid), "astep")
                        E.step(A(KG[d][:, c * 512:(c + 1) * 512], b[:], ACT.Sigmoid, scale=-1.0), "sgm")
                    elif kind == "g":
                        E.step(A(g_a[:, a, :], b[:, 0:256], ACT.Sigmoid), "sgm")
                    elif kind == "v":
                        E.step(copy(v_a[:, a, :], b[:, 0:256]), "proj_x")
                    elif kind == "b":
                        E.lag("zbuf", 3 * (l + 1))
                        E.step(copy(Z[0][:, a, :, 8:8 + SEQ], b[:].rearrange("p (s t) -> p s t", s=2)), "bpool")
                    elif kind == "cq":
                        E.step(copy(qkv[:, a, 0:512], b[:]), "proj_x")
                    elif kind == "ck":
                        E.step(copy(qkv[:, a, 512:768], b[:, 0:256]), "proj_x")
                    if gi in QK_TURN:
                        qk_out(QK_TURN[gi])
                if l == 0:
                    bias(1, 0, 2)
                units = [(j, h) for j in range(nt2) for h in range(8)]
                for u in range(len(units) + 2):
                    if u < len(units):
                        j, h = units[u]
                        nk = TT if j < SEQ // P else CTX
                        g_ = E.n.get("sexp", 0)
                        E.next("scmax")
                        E.lag("ptr", g_ - 3)
                        E.step(A(Pb[:, g_ % 4, 0:nk], ps[g_ % 3][:, 0:nk], ACT.Exp, bias=nmx[:, u:u + 1], scale=HD ** -0.5,
                                 accum_out=rsum[:, u:u + 1]), "sexp")
                    if u >= 2:
                        j, h = units[u - 2]
                        nk = TT if j < SEQ // P else CTX
                        g_ = E.n.get("pt_ev", 0)
                        E.next("ptr")
                        E.lag("pv", g_ - 1)
                        E.step(copy(PT[:, g_ % 2, 0:nk], ps[3 + g_ % 2][:, 0:nk]), "pt_ev")
                E.wait("pv", E.n["pt_ev"])
                E.next("lvup0")
                for v, w in enumerate(LEVELS):
                    if v:
                        E.next("lvdn")
                        E.next("lvup")
                    else:
                        E.next("lvdn")
                    if v >= 2:
                        E.wait("lvmm", 32 * l + 4 * v)
                    Qo, Ko = (pair_buf[:, v % 2, a, :].rearrange("p (n a w) -> p n a w", a=2, w=w) for a in range(2))
                    qf, qb, kf, kb = (z.rearrange("p (n a w) -> p n a w", a=2, w=w) for z in (*QF, *KG))
                    for o, i_ in ((Qo[:, :, 1, :], qf[:, :, 1, :]), (Qo[:, :, 0, :], qb[:, :, 0, :]),
                                  (Ko[:, :, 0, :], kf[:, :, 0, :]), (Ko[:, :, 1, :], kb[:, :, 1, :])):
                        copy(o, i_).then_inc(S["lvcp"], 1)
                E.up("lvdn")
                E.up("lvup")
                for b in range(4):
                    E.next("kgt")
                    E.step(copy(kg_tok[:, b // 2, b % 2], ps[b][:].rearrange("p (j k) -> p j k", j=NT)), "kgt_ev")
                for j in range(nt2):
                    E.next("omm")
                    E.step(copy(osb[:, j, :], ps[j][:, 0:256]), "o_ev")
                for j in range(nt2):
                    E.next("otr")
                    dst = actT[:, 0:2, :]
                    if l == 0:
                        s_, i0 = j // 2, 2 * (j % 2)
                        dst = dst.rearrange("p c (i s t) -> p c i s t", i=4, s=2)[:, :, i0:i0 + 2, s_, :]
                        src = ps[4 + j][:, 0:256].rearrange("p (c i t) -> p c i t", c=2, i=2)
                    else:
                        dst = dst[:, :, j * P:(j + 1) * P]
                        src = ps[4 + j][:, 0:256].rearrange("p (c t) -> p c t", c=2)
                    E.step(copy(dst, src), "omix")
                for i in range(nt2):
                    E.next("xdone")
                    E.step(A(junk2, x_sb[:, (i if l == 0 else 2 * i), :], ACT.Square, accum_out=ss[:, i:i + 1]), "sqs")
                htile = [0]
                ht_evac(nt2, False)
                E.next("lg")
                E.step(A(rtmp[:, 0:nt2 * NE], ps[4][:, 0:nt2 * NE], ACT.Sigmoid), "sig")
                GB, UB, AB, X0, X1, D0, D1 = 0, 1, 2, 3, 4, 5, 6
                b17, b16 = (NE + 1) * l, NE * l
                E.wait("scat", 16 * 2 * (NT if l == 0 else NT + SEQ // P))
                if l == 0:
                    bias(1, 2, 5)
                    norm_gain(1, "norm1_g")
                    gains(1)
                act.wait_ge(S["xtr"], b17 + 1)
                copy(xeT[:, 4:8, :], ps[X1][:].rearrange("p (k s) -> p k s", k=4)).then_inc(S["xe_a"], 1)
                if l == 0:
                    act.sem_inc(S["y_a"], 1)
                else:
                    act.sem_inc(S["y_a"], 1)
                with act.Fori(0, NE // 2) as i:
                    for u in range(2):
                        act.wait_ge(S["moe_used"], i * 6 + (3 * b16 + 3 * u + 1))
                        A(sgl, ps[GB][:], ACT.Silu).then_inc(S["silu"], 1)
                        act.wait_ge(S["xtr"], i * 2 + (b17 + u + 2))
                        copy(xeT[:, 4:8, :], ps[X1][:].rearrange("p (k s) -> p k s", k=4)).then_inc(S["xe_a"], 1)
                        act.wait_ge(S["moe_used"], i * 6 + (3 * b16 + 3 * u + 3))
                        act.wait_ge(S["ystore"], i * 32 + 16 * (b16 + u + 1))
                        copy(y_e[:, 0:512], ps[D0][:]).then_inc(S["y_a"], 1)
                        act.wait_ge(S["y_a"], i * 2 + (b17 + u + 2))
                        act.wait_ge(S["y_d"], i * 2 + (b17 + u + 2))
                        at = act.value_load(offs[0:1, bass.ds(i * 2 + u, 1)], min_val=0, max_val=2 * TT)
                        act.dma_start(Y_s[bass.ds(at, P), :], y_e).then_inc(S["ystore"], 16)
                with long_lists(act, l):
                    O, nj = LONG[l], tiles_of(l)
                    with act.Fori(0, NE) as e:
                        for j in range(nj):
                            act.wait_ge(O["gu"], e * nj + (j + 1))
                            A(sgl, ps[GB][:], ACT.Silu).then_inc(O["silu"], 1)
                for i in range(nt2):
                    act.wait_ge(gats[i], 32 * (l + 1))
                    A(yg[:, i, 0, :], yg[:, i, 0, :], ACT.Copy, scale=wts[:, 0, i:i + 1]).then_inc(S["comb_a"], 1)

        @block.vector
        def _(dve):
            E = Eng(dve)
            v = nc.vector

            def st(ins):
                E.step(ins, "vstep")

            def tt(o, a, b, op, name="vstep"):
                E.step(v.tensor_tensor(o, a, b, op), name)
            def conditioning(a, c, name="vstep"):
                E.step(v.tensor_copy(cmix[:, :, 64 * a:64 * a + 64], cond[:, c, :].unsqueeze(2).broadcast_to([P, KD, 64])), name)

            def mod_out(l, s):
                seg, half = s // 2, s % 2
                if s == 0:
                    E.wait("modb", 32 + 16 * l)
                if (l, s) == (1, 4):
                    E.wait("modb", 64)
                if (l, s) == (1, 10):
                    E.wait("modb", 80)
                if (l, s) == (1, 2):
                    E.wait("gnb", 64)
                if s == 8:
                    E.wait("gnb", 32 + 64 * l)
                E.wait("slab_used", used(("m", l, s)))
                dst = mod[:, seg, 512 * half:512 * half + 512]
                tt(dst, ps[mod_bank(l, s)][:], dst, ALU.add, "mod_ev")
                if seg in (1, 4):
                    gain = gn[:, 0, 512 * half:512 * half + 512] if (l, seg) == (0, 1) else gn_half[half]
                    st(v.scalar_tensor_tensor(out=dst, in0=dst, scalar=1.0, in1=gain, op0=ALU.add, op1=ALU.mult))
                if (l, s) == (1, 3):
                    conditioning(1, 0, "condm")

            E.next("condx")
            conditioning(0, 0)
            conditioning(1, 1, "condm")
            E.wait("consts", NCONST)
            st(v.tensor_copy(masks[:].rearrange("p a b -> p (a b)"), masks_f))
            tt(lbe[:, 8:12], lbr[:, 0, :], lbr[:, 1, :], ALU.max)
            tt(lbe[:, 0:4], lbr[:, 0, :], lbe[:, 8:12], ALU.subtract)
            tt(lbe[:, 4:8], lbr[:, 1, :], lbe[:, 8:12], ALU.subtract, "lbd")
            E.next("lbx")
            tt(lbe[:, 8:12], lbe[:, 0:4], lbe[:, 4:8], ALU.add)
            st(v.reciprocal(lbe[:, 12:16], lbe[:, 8:12]))
            tt(lbe[:, 0:4], lbe[:, 0:4], lbe[:, 12:16], ALU.mult)
            tt(lbe[:, 4:8], lbe[:, 4:8], lbe[:, 12:16], ALU.mult)
            tt(lb[:, 0, :], lbe[:, 0:4], lbe[:, 0:4], ALU.subtract)
            tt(lb[:, 1, :], lbe[:, 0:4], lbe[:, 4:8], ALU.add)
            tt(lb[:, 1, :], lb[:, 1, :], lbe[:, 0:4], ALU.subtract)
            st(v.tensor_scalar(lb[:], lb[:], 1e-30, None, ALU.max))
            st(v.tensor_scalar(oml[:], lb[:], -1.0, 1.0, ALU.mult, ALU.add))
            for l in range(L):
                nt2 = NT if l == 0 else SEQ // P
                if l == 0:
                    for s in range(4):
                        mod_out(0, s)

                def norm_rows(n, ts, seg):
                    E.next("sqs", n)
                    E.step(v.tensor_scalar(ss[:, 0:n], ss[:, 0:n], 1.0 / D, EPS, ALU.mult, ALU.add), "rstd_d")
                    E.next("rstd_p")
                    for i in range(n):
                        st(v.scalar_tensor_tensor(out=rows[:, i, :], in0=x_sb[:, ts[i], :], scalar=rstd[:, i:i + 1],
                                                  in1=mod[:, seg + 1, :], op0=ALU.mult, op1=ALU.mult))
                        tt(rows[:, i, :], rows[:, i, :], mod[:, seg, :], ALU.add, "rows_d")
                norm_rows(NT, range(NT), 0)
                mod_out(l, 4 if l == 0 else 7)
                E.wait("gains", 16 * NGAIN * (l + 1))
                def qk_stats():
                    tt(sqk, qkv[:, :, 0:QK], qkv[:, :, 0:QK], ALU.mult)
                    st(v.tensor_reduce(ssq, sqk.rearrange("p j (h d) -> p j h d", d=HD), AX, ALU.add))
                    E.step(v.tensor_scalar(ssq, ssq, 1.0 / HD, EPS, ALU.mult, ALU.add), "kq_d")

                def qk_made(j):
                    qk = qkv[:, j, 0:QK].rearrange("p (h d) -> p h d", d=HD)
                    tt(qk, qk, rsq[:, j, :].unsqueeze(2).broadcast_to([P, 10, HD]), ALU.mult)
                    gq, gk = (gain_qk[:, a, :].unsqueeze(1) for a in range(2))
                    oq = qkr[:, j % 2, 0:512].rearrange("p (c g d) -> p g c d", g=2, d=HD)
                    ok = qkr[:, j % 2, 512:QK].rearrange("p (h d) -> p h d", d=HD)
                    if j >= 2:
                        E.wait("qkt", NT * l + j - 1)
                    if j >= SEQ // P:
                        for g2 in range(2):
                            tt(oq[:, g2], qk[:, 4 * g2:4 * g2 + 4, :], gq.broadcast_to([P, 4, HD]), ALU.mult)
                        tt(ok, qk[:, 8:10, :], gk.broadcast_to([P, 2, HD]), ALU.mult, "qk_d2")
                    else:
                        tt(qk[:, 0:8, :], qk[:, 0:8, :], gq.broadcast_to([P, 8, HD]), ALU.mult)
                        tt(qk[:, 8:10, :], qk[:, 8:10, :], gk.broadcast_to([P, 2, HD]), ALU.mult)
                        qp = qkv[:, j, 0:QK].rearrange("p (h e b) -> p h e b", e=HD // 2, b=2)
                        sw = swp[:, j % 2, :].rearrange("p (h e b) -> p h e b", e=HD // 2, b=2)
                        rs = rope[:, j, 1, :].rearrange("p (e b) -> p e b", b=2)
                        for b in range(2):
                            tt(sw[:, :, :, b], qp[:, :, :, 1 - b], rs[:, :, b].unsqueeze(1).broadcast_to([P, 10, HD // 2]), ALU.mult)
                        tt(qk, qk, rope[:, j, 0, :].unsqueeze(1).broadcast_to([P, 10, HD]), ALU.mult)
                        s3 = swp[:, j % 2, :].rearrange("p (h d) -> p h d", d=HD)
                        tt(oq, qk[:, 0:8, :].rearrange("p (g c) d -> p g c d", g=2),
                           s3[:, 0:8, :].rearrange("p (g c) d -> p g c d", g=2), ALU.add)
                        tt(ok, qk[:, 8:10, :], s3[:, 8:10, :], ALU.add, "qk_d2")

                for gi, (kind, a) in enumerate(PROJ):
                    g_ = E.n.get("proj", 0)
                    b = ps[4 + g_ % 4]
                    E.next("proj")
                    if kind == "q":
                        E.next("sgm")
                        tt(q_t[:, a, :], q_t[:, a, :], b[:], ALU.mult, "proj_d")
                    elif kind == "f":
                        d, c = a
                        E.next("sgm")
                        o_ = oml[:, l, 2 * d + c:2 * d + c + 1]
                        l_ = lb[:, l, 2 * d + c:2 * d + c + 1]
                        fs, ks = f_t[d][:, c * 512:(c + 1) * 512], KG[d][:, c * 512:(c + 1) * 512]
                        st(v.tensor_scalar(fs, fs, o_, l_, ALU.mult, ALU.add))
                        E.step(v.tensor_scalar(ks, ks, o_, None, ALU.mult), "proj_d")
                    elif kind == "g":
                        E.next("sgm")
                        tt(g_a[:, a, :], g_a[:, a, :], b[:, 0:256], ALU.mult)
                        gv = g_a[:, a, :].rearrange("p (h d) -> p h d", h=4)
                        tt(gv, gv, gain_o[:].unsqueeze(1).broadcast_to([P, 4, HD]), ALU.mult, "proj_d")
                    elif kind == "b":
                        E.next("bpool")
                        dve.sem_inc(S["proj_d"], 1)
                        E.up("proj_d")
                    else:
                        E.next("proj_x")
                        dve.sem_inc(S["proj_d"], 1)
                        E.up("proj_d")
                    if gi == 2 * NT - 1:
                        qk_stats()
                    if gi in QK_NORM:
                        if gi == min(QK_NORM):
                            E.next("qk_p")
                        qk_made(QK_NORM[gi])

                def mixcols(k, a, j):
                    o = actT[a:a + 64, k, :]
                    if l == 0:
                        return o.rearrange("p (i s t) -> p i s t", i=4, s=2)[:, 2 * (j % 2):2 * (j % 2) + 2, j // 2, :]
                    return o[:, j * P:(j + 1) * P]
                units = [(j, h) for j in range(nt2) for h in range(8)]
                for u in range(len(units) + 3):
                    if u < len(units):
                        j, h = units[u]
                        nk = TT if j < SEQ // P else CTX
                        g_ = E.n.get("sc", 0)
                        E.next("sc")
                        st(v.reduce_max(mx[:, u:u + 1], ps[g_ % 3][:, 0:nk], AX))
                        E.step(v.tensor_scalar(nmx[:, u:u + 1], mx[:, u:u + 1], -HD ** -0.5, None, ALU.mult), "scmax")
                    if 1 <= u <= len(units):
                        j, h = units[u - 1]
                        nk = TT if j < SEQ // P else CTX
                        g_ = E.n.get("sexp", 0)
                        E.next("sexp")
                        st(v.reciprocal(rinv[:, u - 1:u], rsum[:, u - 1:u]))
                        E.step(v.tensor_scalar(Pb[:, g_ % 4, 0:nk], Pb[:, g_ % 4, 0:nk], rinv[:, u - 1:u], None, ALU.mult), "pnorm")
                    if u - 1 in AMONG[l]:
                        mod_out(l, AMONG[l][u - 1])
                    if u >= 3:
                        j, h = units[u - 3]
                        g_ = E.n.get("pv", 0)
                        E.next("pv")
                        src = ps[5 + g_ % 2][0:64, 0:P]
                        if l == 0:
                            src = src.rearrange("p (i t) -> p i t", i=2)
                        E.step(v.tensor_copy(mixcols(4 + h // 2, 64 * (h % 2), j), src), "pv_ev")
                for c in range(2):
                    E.next("ymm")
                    if l == 0:
                        dst = actT[:, 2 + c, :].rearrange("p (i s t) -> p s i t", i=4, s=2)
                        src = ps[7][:].rearrange("p (s i t) -> p s i t", s=2, i=4)
                    else:
                        dst, src = actT[:, 2 + c, 0:SEQ], ps[7][:, 0:SEQ]
                    E.step(v.tensor_scalar(dst, src, pool_sc[:, c:c + 1], None, ALU.mult), "ymix")
                qflat = q_t.rearrange("p c t -> p (c t)")
                tt(ksum, KG[0], KG[1], ALU.add)
                tt(QF[0], qflat, f_t[0], ALU.mult)
                tt(QF[1], qflat, f_t[1], ALU.mult, "lvdn")
                dve.sem_inc(S["lvup0"], 1)
                dve.sem_inc(S["tot0"], 1)
                def bank_scores(b):
                    J, a = b // 2, b % 2
                    return (A_s.rearrange("p j (c a) t -> p j c a t", a=2)[:, 2 * J:2 * J + 2, :, a, :])
                b4 = lambda m_: m_.unsqueeze(1).unsqueeze(1).broadcast_to([P, 2, 2, P])
                for b in range(4):
                    E.next("lvmm")
                    E.step(v.tensor_tensor(bank_scores(b), ps[b][:].rearrange("p (j c t) -> p j c t", j=2, c=2),
                                           b4(ident[:]), ALU.mult), "lvA")
                tcur, toff = f_t[0], 0
                for lv, w in enumerate(LEVELS):
                    nb = 1024 // (2 * w)
                    E.next("lvcp", 4)
                    q = QF[0].rearrange("p (n a w) -> p n a w", a=2, w=w)
                    k = KG[0].rearrange("p (n a w) -> p n a w", a=2, w=w)
                    t = tcur.rearrange("p (n a) -> p n a", a=2)
                    tt(q[:, :, 1, :], q[:, :, 1, :], t[:, :, 0:1].broadcast_to([P, nb, w]), ALU.mult)
                    tt(k[:, :, 0, :], k[:, :, 0, :], t[:, :, 1:2].broadcast_to([P, nb, w]), ALU.mult)
                    tn = tots[0][:, toff:toff + nb]
                    tt(tn, t[:, :, 0], t[:, :, 1], ALU.mult, "lvdn")
                    tcur, toff = tn, toff + nb
                    for b in range(4):
                        E.next("lvmm")
                        E.step(v.copy_predicated(bank_scores(b), b4(masks[:, lv, :]),
                                                 ps[4 * ((lv + 1) % 2) + b][:].rearrange("p (j c t) -> p j c t", j=2, c=2)), "lvA")
                E.wait("lvup", len(LEVELS) * (l + 1))
                E.wait("kgt_ev", 4 * (l + 1))
                for d in range(2):
                    st(v.memset(S_st[:, d, :, ORDER[d][0], :], 0.0))
                for s in range(3):
                    E.next("umm")
                    tt(U_m[:, s, :].rearrange("p (a v) -> p a v", a=4), ps[4 + s][:].rearrange("p (a v) -> p a v", a=4),
                       headsep[:].unsqueeze(1).broadcast_to([P, 4, P]), ALU.mult)
                    for d in range(2):
                        for c in range(2):
                            j, jn = ORDER[d][s], ORDER[d][s + 1]
                            tot = tots[d][:, toff - nb + 4 * c + j:toff - nb + 4 * c + j + 1]
                            E.step(v.scalar_tensor_tensor(out=S_st[:, d, c, jn, :], in0=S_st[:, d, c, j, :], scalar=tot,
                                                          in1=U_m[:, s, (2 * d + c) * P:(2 * d + c + 1) * P],
                                                          op0=ALU.mult, op1=ALU.add), "vstep")
                dve.sem_inc(S["stv"], 1)
                for s in IN_STATES[l]:
                    mod_out(l, s)
                for j in range(nt2):
                    E.next("o_ev")
                    tt(osq[:, j, :], osb[:, j, :], osb[:, j, :], ALU.mult)
                    st(v.tensor_reduce(ssq[:, j, 0:4], osq[:, j, :].rearrange("p (h d) -> p h d", d=HD), AX, ALU.add))
                    E.step(v.tensor_scalar(ssq[:, j, 0:4], ssq[:, j, 0:4], 1.0 / HD, EPS, ALU.mult, ALU.add), "ogn")
                for j in range(nt2):
                    E.next("rd_p")
                    o3 = osb[:, j, :].rearrange("p (h d) -> p h d", d=HD)
                    tt(o3, o3, rsq[:, j, 0:4].unsqueeze(2).broadcast_to([P, 4, HD]), ALU.mult)
                    tt(osb[:, j, :], osb[:, j, :], g_a[:, j, :], ALU.mult, "o_fin")
                if l:
                    for t_ in range(SEQ // P):
                        st(v.tensor_copy(x_sb[64:128, 2 * t_, :], x_sb[0:64, 2 * t_ + 1, :]))
                for s in range(NWO):
                    for i in range(nt2):
                        g_ = E.n.get("wo", 0)
                        E.next("wo")
                        cs = slice(512 * s, 512 * s + 512)
                        tt(wtmp, ps[g_ % 4][:], mod[:, 2, cs], ALU.mult, "wo_ev")
                        xt = x_sb[:, (i if l == 0 else 2 * i), cs]
                        tt(xt, xt, wtmp, ALU.add, "xdone" if s == NWO - 1 else "vstep")
                norm_rows(nt2, [i if l == 0 else 2 * i for i in range(nt2)], 3)
                mod_out(l, 11)
                R = cut(rtmp, 0)
                n16, n4 = nt2 * NE, nt2 * NG
                scs = R(64)[:, 0:n16]
                sel, t1, t2, oh1, oh2, msl = (R(64)[:, 0:n16] for _ in range(6))
                ohb = rtmp[:, OH0:OH0 + n16]
                m1, m2, gs, t4, ohg, tm = (rsm[:, 16 * a:16 * a + n4] for a in range(6))
                w1, w2, d1 = (wts[:, a, 0:nt2] for a in range(3))
                r3 = lambda a, n: a.rearrange("p (g e) -> p g e", e=n)
                bc = lambda a, g_, n: a.unsqueeze(2).broadcast_to([P, g_, n])
                E.next("sig")
                tt(r3(sel, NE), r3(scs, NE), rb[:].unsqueeze(1).broadcast_to([P, nt2, NE]), ALU.add)

                def first_max(dst, src, groups, n, top, tmp, red):
                    st(v.tensor_reduce(top, r3(src, n), AX, ALU.max))
                    tt(r3(tmp, n), r3(src, n), bc(top, groups, n), ALU.is_equal)
                    tt(r3(tmp, n), r3(tmp, n), rconst[:, 0:n].unsqueeze(1).broadcast_to([P, groups, n]) if n == NE else
                       rconst[:, NE - n:NE].unsqueeze(1).broadcast_to([P, groups, n]), ALU.mult)
                    st(v.tensor_reduce(red, r3(tmp, n), AX, ALU.max))
                    tt(r3(dst, n), r3(tmp, n), bc(red, groups, n), ALU.is_equal)
                first_max(t2, sel, n4, EG, m1, t1, tm)
                st(v.scalar_tensor_tensor(out=t1, in0=t2, scalar=NEG, in1=sel, op0=ALU.mult, op1=ALU.add))
                st(v.tensor_reduce(m2, r3(t1, EG), AX, ALU.max))
                tt(gs, m1, m2, ALU.add)
                first_max(ohg, gs, nt2, NG, m1[:, 0:nt2], t4, tm[:, 0:nt2])
                st(v.memset(msl, -1e4))
                st(v.copy_predicated(r3(msl, EG), bc(ohg.bitcast(i32), n4, EG), r3(sel, EG)))
                first_max(oh1, msl, nt2, NE, m1[:, 0:nt2], t1, tm[:, 0:nt2])
                st(v.scalar_tensor_tensor(out=msl, in0=oh1, scalar=NEG, in1=msl, op0=ALU.mult, op1=ALU.add))
                first_max(oh2, msl, nt2, NE, m1[:, 0:nt2], t1, tm[:, 0:nt2])
                tt(ohb, oh1, oh2, ALU.add, "ohs")
                if l == 0:
                    mod_out(1, 0)
                for w_, o_ in ((w1, oh1), (w2, oh2)):
                    tt(t1, scs, o_, ALU.mult)
                    st(v.tensor_reduce(w_, r3(t1, NE), AX, ALU.add))
                tt(d1, w1, w2, ALU.add)
                st(v.reciprocal(d1, d1))
                tt(w1, w1, d1, ALU.mult)
                tt(w2, w2, d1, ALU.mult)
                E.next("posm")
                pos, cnt = t2, rsm[:, 0:NE]
                st(v.tensor_copy(pos, ps[5][:, 0:n16]))
                st(v.tensor_copy(cnt, ps[5][:, n16:n16 + NE]))
                ca, cb = rsm[:, 16:16 + 18], rsm[:, 48:48 + 18]
                st(v.memset(rsm[:, 16:96], 0.0))
                st(v.tensor_copy(ca[:, 1:NE], cnt[:, 0:NE - 1]))
                for sh in (1, 2, 4, 8):
                    st(v.tensor_copy(cb[:, 0:NE], ca[:, 0:NE]))
                    tt(cb[:, sh:NE], ca[:, sh:NE], ca[:, 0:NE - sh], ALU.add)
                    ca, cb = cb, ca
                off = ca[:, 0:NE]
                tt(r3(t1, NE), r3(pos, NE), off.unsqueeze(1).broadcast_to([P, nt2, NE]), ALU.add)
                for a, o_ in enumerate((oh1, oh2)):
                    tt(sel, t1, o_, ALU.mult)
                    st(v.tensor_reduce(m16[:, 0:nt2], r3(sel, NE), AX, ALU.add))
                    st(v.tensor_copy(idx[:, a, 0:nt2], m16[:, 0:nt2]))
                st(v.memset(ca[:, NE:NE + 2], 2.0 * nt2 * P))
                st(v.tensor_reduce(m16[:, 0:1], cnt, AX, ALU.max))
                st(v.tensor_copy(offs[:, NE + 2:NE + 3], m16[:, 0:1]))
                E.step(v.tensor_copy(offs[:, 0:NE + 2], ca[:, 0:NE + 2]), "slots_d")
                GB, UB, AB, X0, X1, D0, D1 = 0, 1, 2, 3, 4, 5, 6
                b17, b16 = (NE + 1) * l, NE * l
                if l == 0:
                    mod_out(1, 1)
                dve.wait_ge(S["xtr"], b17 + 1)
                v.tensor_copy(xeT[:, 0:4, :], ps[X0][:].rearrange("p (k s) -> p k s", k=4)).then_inc(S["xe_d"], 1)
                dve.sem_inc(S["y_d"], 1)
                with dve.Fori(0, NE // 2) as i:
                    for u in range(2):
                        dve.wait_ge(S["moe_used"], i * 6 + (3 * b16 + 3 * u + 2))
                        dve.wait_ge(S["silu"], i * 2 + (b16 + u + 1))
                        v.tensor_tensor(act_e, sgl, ps[UB][:], ALU.mult).then_inc(S["a_d"], 1)
                        dve.wait_ge(S["xtr"], i * 2 + (b17 + u + 2))
                        v.tensor_copy(xeT[:, 0:4, :], ps[X0][:].rearrange("p (k s) -> p k s", k=4)).then_inc(S["xe_d"], 1)
                        dve.wait_ge(S["atr"], i * 2 + (b16 + u + 1))
                        v.tensor_copy(aT, ps[AB][:].rearrange("p (k s) -> p k s", k=KF)).then_inc(S["aT_d"], 1)
                        dve.wait_ge(S["moe_used"], i * 6 + (3 * b16 + 3 * u + 3))
                        dve.wait_ge(S["ystore"], i * 32 + 16 * (b16 + u + 1))
                        v.tensor_copy(y_e[:, 512:1024], ps[D1][:]).then_inc(S["y_d"], 1)
                with long_lists(dve, l):
                    O, nj = LONG[l], tiles_of(l)
                    with dve.Fori(0, NE) as e:
                        for j in range(nj):
                            dve.wait_ge(O["xT"], e * nj + (j + 1))
                            for a in range(2):
                                v.tensor_copy(xeT[:, 4 * a:4 * a + 4, :], ps[X0 + a][:].rearrange("p (k s) -> p k s", k=4)).then_inc(O["xe"], 1)
                            dve.wait_ge(O["silu"], e * nj + (j + 1))
                            v.tensor_tensor(act_e, sgl, ps[UB][:], ALU.mult).then_inc(O["a"], 1)
                            dve.wait_ge(O["aT"], e * nj + (j + 1))
                            v.tensor_copy(aT, ps[AB][:].rearrange("p (k s) -> p k s", k=KF)).then_inc(O["aTe"], 1)
                            dve.wait_ge(O["y"], e * nj + (j + 1))
                            v.tensor_copy(y_e[:, 0:512], ps[D0][:]).then_inc(O["yh"], 1)
                            v.tensor_copy(y_e[:, 512:1024], ps[D1][:]).then_inc(O["ye"], 1)
                            dve.wait_ge(O["store"], e * (16 * nj) + 16 * (j + 1))
                for i in range(nt2):
                    if l == 0 and i < 3:
                        mod_out(1, 2 + i)
                    E.next("comb_a")
                    dve.wait_ge(gats[i], 32 * (l + 1))
                    E.step(v.scalar_tensor_tensor(out=yg[:, i, 0, :], in0=yg[:, i, 1, :], scalar=wts[:, 1, i:i + 1], in1=yg[:, i, 0, :],
                                                  op0=ALU.mult, op1=ALU.add), "comb_v" if i % 2 else "vstep")
                    if i % 2 == 0:
                        tt(yg[:, i, 0, :], yg[:, i, 0, :], mod[:, 5, :], ALU.mult)
                        xt = x_sb[:, (i if l == 0 else 2 * i), :]
                        tt(xt, xt, yg[:, i, 0, :], ALU.add, "comb")
                if l == 0:
                    for s in (5, 6):
                        mod_out(1, s)


def shape_constants(seq, ne, cap):
    import numpy as np
    p = np.arange(128)
    ident = np.eye(128, dtype=np.float32)
    before = (p[:, None] < p[None, :]).astype(np.float32)
    headsep = ((p[:, None] // 64) == (p[None, :] // 64)).astype(np.float32)
    masks = np.stack([((p[:, None] // w) ^ (p[None, :] // w)) == 1 for w in (1, 2, 4, 8, 16, 32, 64)], 1).astype(np.float32)
    t = np.arange(seq)
    inv = np.float32(10000.0) ** (-np.arange(16, dtype=np.float32) / np.float32(16))
    ang = np.concatenate([(t // 64).astype(np.float32)[:, None] * inv, (t % 64).astype(np.float32)[:, None] * inv], -1)
    cos, sin = np.repeat(np.cos(ang), 2, 1), np.repeat(np.sin(ang), 2, 1)
    sin[:, 0::2] *= -1
    rope = np.stack([cos, sin], 1).reshape(seq // 128, 128, 2, 64).transpose(1, 0, 2, 3).astype(np.float32)
    invcnt = np.zeros((128, 2, seq), np.float32)
    for g, w in enumerate((2, 4, 8, 16)):
        cnt = np.minimum(t + w // 2, seq) - np.maximum(t - w // 2, 0)
        invcnt[64 * (g % 2):64 * (g % 2) + 64, g // 2] = np.float32(1) / cnt.astype(np.float32)
    router = np.broadcast_to(np.concatenate([np.arange(ne, 0, -1), cap * np.arange(ne)]).astype(np.float32), (128, 2 * ne))
    return {"k_ident": ident, "k_before": before, "k_headsep": headsep, "k_masks": masks, "k_rope": rope,
            "k_invcnt": invcnt, "k_router": router}


def kernel(**inputs):
    import numpy as _np
    import concourse.bacc as _bacc
    from concourse import mybir as _mybir
    from concourse.bass_utils import run_bass_kernel_spmd as _run

    nc = _bacc.Bacc("TRN2", target_bir_lowering=False, num_devices=1)
    named = dict(inputs)
    seq = inputs["x"].shape[1]
    lbs, psc = _np.asarray(named.pop("hgrn_lb")), _np.asarray(named.pop("pool_scale"))
    named["hgrn_lb_cols"] = lbs.reshape(lbs.shape[0], -1, 128).transpose(0, 2, 1)
    named["pool_scale_cols"] = psc.reshape(psc.shape[0], -1, 128).transpose(0, 2, 1)
    named.update(shape_constants(seq, inputs["router_w"].shape[1], seq + inputs["ctx"].shape[1]))
    arrays, T = {}, {}
    for name, a in named.items():
        a = _np.ascontiguousarray(a)
        arrays["in_" + name] = a
        T[name] = nc.dram_tensor("in_" + name, a.shape, _mybir.dt.from_np(a.dtype), kind="ExternalInput").ap()
    T["out"] = nc.dram_tensor("out_latent", inputs["x"].shape, _mybir.dt.float32, kind="ExternalOutput").ap()
    build(nc, T)
    r = _run(nc, [arrays], core_ids=[0])
    return r.results[0]["out_latent"]
```

```python
def build(nc, T):
    import concourse.bass as bass
    from concourse import mybir
    from concourse.alu_op_type import AluOpType as ALU
    from contextlib import ExitStack

    f32, f32r, i32, u32, u8 = mybir.dt.float32, mybir.dt.float32r, mybir.dt.int32, mybir.dt.uint32, mybir.dt.uint8
    ACT, AX = mybir.ActivationFunctionType, mybir.AxisListType.X

    P = 128
    D = T["x"].shape[-1]
    SEQ, CTX = T["x"].shape[1], T["ctx"].shape[1]
    L = T["w_mod"].shape[0]
    KD = D // P
    HD = 64
    TT = SEQ + CTX
    NT = TT // P
    NE = T["router_w"].shape[1]
    NG = 4
    EG = NE // NG
    FE = T["moe_w_gate"].shape[-1]
    KF = FE // P
    CAP = TT
    EPS = 1e-6
    LEVELS = [1, 2, 4, 8, 16, 32, 64]
    SLAB = KD * 512
    NMOD, NWO = 6 * D // 512, D // 512
    QK = 640
    NEG = -1e30

    ctx = ExitStack()
    with ctx:
        def sb(name, shape, dt=f32):
            return ctx.enter_context(nc.sbuf_tensor(name, shape, dt))

        def sem(name):
            return ctx.enter_context(nc.semaphore(name))

        x_sb = sb("x_sb", [P, NT, D])
        mod = sb("mod", [P, 6, D])
        ident = sb("ident", [P, P])
        before = sb("before", [P, P])
        ones = sb("ones", [P, P])
        headsep = sb("headsep", [P, P])
        masks = sb("masks", [P, len(LEVELS), P], u8)
        rope = sb("rope", [P, SEQ // P, 2, HD])
        invcnt = sb("invcnt", [P, 2, SEQ])
        gain_qk = sb("gain_qk", [P, 2, HD])
        cmix = sb("cmix", [P, KD, P])
        gain_o = sb("gain_o", [P, HD])
        pool_bd = sb("pool_bd", [P, 2, P])
        pool_sc = sb("pool_sc", [P, 2])
        rw = sb("rw", [P, KD, NE])
        rb = sb("rb", [P, NE])
        small = sb("small", [P, 864])
        idx = sb("idx", [P, 2, NT], u32)
        offs = sb("offs", [P, NE + 4], i32)

        rconst = sb("rconst", [P, 2 * NE])[:]
        with ExitStack() as turn:
            tsb = lambda name, shape, dt=f32: turn.enter_context(nc.sbuf_tensor(name, shape, dt))
            ring = tsb("ring", [P, 2, SLAB])
            actT = tsb("actT", [P, KD, TT])
            rows = tsb("rows", [P, NT, D])
            arena = tsb("arena", [P, 22528])
        split = sb("split", [P, 4, 2, SLAB // 2], f32r)
        PLACE = [2, 0, 1, 3]
        sb("over_arena", [P, 16384])
        xs = sb("xs", [P, 2, KD, P], f32r)
        acs = sb("acs", [P, 2, KF, P], f32r)

        ps = [ctx.enter_context(nc.psum_tensor(f"bank{i}", [P, 512], f32)) for i in range(8)]

        X_s = nc.dram_tensor("expert_in", [2 * TT + CAP, D], f32).ap()
        Y_s = nc.dram_tensor("expert_out", [2 * TT + CAP, D], f32).ap()

        def cut(tensor, start):
            at = [start]

            def take(n):
                at[0] += n
                return tensor[:, at[0] - n:at[0]]
            return take

        take = cut(arena, 0)
        q_t = take(1024).rearrange("p (c t) -> p c t", c=2)
        f_t = [take(1024), take(1024)]
        v_a = take(1024).rearrange("p (j c) -> p j c", j=NT)
        g_a = take(1024).rearrange("p (j c) -> p j c", j=NT)
        qkv = take(3072).rearrange("p (j c) -> p j c", j=NT)
        dpool = take(1024).rearrange("p (c t) -> p c t", c=2)
        hg0 = 9 * 1024
        KG = [take(1024), take(1024)]
        QF = [take(1024), take(1024)]
        qk_same = take(1024)
        tots = [take(1024), take(1024)]
        KP = [take(1024).rearrange("p (c t) -> p c t", c=2) for _ in range(2)]
        QP = [take(2048).rearrange("p (c a t) -> p c a t", c=2, a=2) for _ in range(2)]
        take = cut(arena, hg0 + 7 * 1024)
        kg_tok = take(2048).rearrange("p (d c j k) -> p d c j k", d=2, c=2, j=NT)
        osb = take(1024).rearrange("p (j c) -> p j c", j=NT)
        osq = take(1024).rearrange("p (j c) -> p j c", j=NT)
        S_st = take(2048).rearrange("p (d c j v) -> p d c j v", d=2, c=2, j=NT)
        U_m = arena[:, hg0:hg0 + 1536].rearrange("p (s n) -> p s n", s=3)
        take = cut(arena, hg0 + 2048)
        qkr = take(2 * QK).rearrange("p (b c) -> p b c", b=2)
        swp = take(2 * QK).rearrange("p (b c) -> p b c", b=2)
        sqk = take(4 * QK).rearrange("p (j c) -> p j c", j=NT)
        qT = take(2048).rearrange("p (c t) -> p c t", c=4)
        kT = take(512)
        Pb = take(2048).rearrange("p (b k) -> p b k", b=4)
        PT = take(1024).rearrange("p (b k) -> p b k", b=2)
        take = cut(arena, 0)
        gn = take(2 * D).rearrange("p (a n) -> p a n", a=2)
        take(KD * P)
        junk = take(2 * D).rearrange("p (a n) -> p a n", a=2)
        ZW = 272
        take = cut(rows[:].rearrange("p a b -> p (a b)"), 0)
        Z = [take(4 * ZW).rearrange("p (c s t) -> p c s t", c=2, s=2) for _ in range(3)]
        A_s = rows[:].rearrange("p j (h t) -> p j h t", t=P)[:, :, 0:4, :]
        gn_half_1 = arena[:, 21504:22016]
        gn_half = [arena[:, 22016:22528], rows[:].rearrange("p a b -> p (a b)")[:, 3584:4096]]
        masks_f = arena[:, 8192:8192 + len(LEVELS) * P]
        zeros = arena[:, 19456:19456 + D]
        take = cut(arena, 0)
        raw = [take(SLAB) for _ in range(3)]
        xe = take(2 * D).rearrange("p (b n) -> p b n", b=2)
        sgl = take(FE)
        act_e = take(FE)
        y_e = take(D)
        take = cut(arena, 16384 + 3072)
        xeT = take(KD * P).rearrange("p (k s) -> p k s", k=KD)
        aT = take(KF * P).rearrange("p (k s) -> p k s", k=KF)
        wtmp, junk2 = sgl, y_e
        yg = arena[:, 0:4 * 2 * D].rearrange("p (i c n) -> p i c n", i=4, c=2)

        take = cut(small, 0)
        cond = take(2 * KD).rearrange("p (a k) -> p a k", a=2)
        ss = take(NT)
        rstd = take(NT)
        mhalf = take(64)
        ssq = take(NT * 10).rearrange("p (j h) -> p j h", j=NT)
        rsq = take(NT * 10).rearrange("p (j h) -> p j h", j=NT)
        lbr = take(8).rearrange("p (l c) -> p l c", l=2)
        lbe = take(16)
        lb = take(8).rearrange("p (l c) -> p l c", l=2)
        oml = take(8).rearrange("p (l c) -> p l c", l=2)
        rsm = take(96)
        wts = take(12).rearrange("p (a i) -> p a i", a=3)
        m16 = take(16)
        rtmp = small[:, 352:864]
        mx, nmx, rsum, rinv = (rtmp[:, 32 * a:32 * a + 32] for a in range(4))

        OH0 = 448
        LONG_FROM = P
        POOLED = [1, 2]
        UNITS = 6 * NE
        ORDER = [[2, 3, 0, 1], [3, 2, 1, 0]]
        def proj_groups(l):
            lat = range(tiles_of(l))
            return ([("cq", j) for j in lat] + [("ck", j) for j in range(NT)]
                    + [("q", 0), ("q", 1), ("f", (0, 0)), ("f", (0, 1)), ("f", (1, 0)), ("f", (1, 1))] + [("v", j) for j in range(NT)]
                    + [("b", 0), ("b", 1)] + [("g", j) for j in lat])

        def tiles_of(l):
            return NT if l == 0 else SEQ // P

        PROJ = [proj_groups(l) for l in range(L)]
        QK_NORM = [{8: 0, 11: 1, 14: 2, 16: 3}, {6: 0, 8: 1, 10: 2, 12: 3}]
        QK_TURN = [{12: 0, 15: 1, 18: 2, 21: 3}, {9: 0, 11: 1, 13: 2, 15: 3}]
        NCONST, NGAIN = 16 * 8, 8
        m_ = lambda l, a: [("m", l, s) for s in a]
        w_ = lambda k, l, a: [(k, l, s) for s in a]
        IN_ORDER = (3, 4, 0, 1, 2)
        RING = (m_(0, range(5)) + w_("i", 0, IN_ORDER) + m_(0, range(5, 11)) + w_("o", 0, range(NWO)) + m_(0, [11]) + m_(1, [0, 1, 2])
                + m_(1, range(3, 8)) + w_("i", 1, IN_ORDER) + m_(1, [8, 9]) + w_("o", 1, range(NWO)) + m_(1, [10, 11]))
        RING_LOOP = [RING.index(("m", 1, 3)), len(RING)]
        AMONG = [{5: 5, 11: 6, 17: 7, 24: 8}, {8: 8}]
        AFTER_ATTN = [9, 9]
        IN_STATES = [[10], []]
        BEHIND_OUT = [11, 10]
        ROUTER_MODS = [[(1, 0), (1, 1), (1, 2)], [(1, 11)]]

        def wanted_half(l, z, w, a):
            if l == 0:
                return z.rearrange("p (n a w) -> p n a w", a=2, w=w)[:, :, a, :]
            return z.rearrange("p (c t) -> p c t", c=2)[:, :, 0:SEQ].rearrange("p c (n a w) -> p c n a w", a=2, w=w)[:, :, :, a, :]

        def wanted_q(l, z, tot, w, a, b):
            if l == 0:
                nb = 1024 // (2 * w)
                return wanted_half(l, z, w, a), tot.rearrange("p (n a) -> p n a", a=2)[:, :, b:b + 1].broadcast_to([P, nb, w])
            nb = SEQ // (2 * w)
            t = tot.rearrange("p (c n) -> p c n", c=2)[:, :, 0:2 * nb].rearrange("p c (n a) -> p c n a", a=2)[:, :, :, b:b + 1]
            return wanted_half(l, z, w, a), t.broadcast_to([P, 2, nb, w])

        def lane(l, z, w, a):
            return z[:, :, 0:tiles_of(l) * P].rearrange("p c (n a w) -> p c n a w", a=2, w=w)[:, :, :, a, :]

        def used(key):
            return RING.index(key) + 1

        def mod_bank(l, s):
            return 6 + s % 2 if (l, s) in [(0, a) for a in range(5)] + [(1, a) for a in range(3, 8)] else 7

        def mod_free(l, s):
            m = NMOD * l + s
            return m - 1 if mod_bank(l, s) != mod_bank(*divmod(m - 1, NMOD)) else m
        PH = [2 * NT, 6 * NT]

        names = """consts ident_in lb_in gn_in x_in cond_in gains mod_ev condm wl0 slab_used ht ht_ev sqs rstd_d rstd_p
        rows_d proj proj_d sgm kq_d qk_p qkt qkt_ev sc scmax sexp pnorm ptr pt_ev pv pv_ev zbuf bpool dp ymm
        ymix hq zeroed dg dg_ev lvcp lvup lvdn lvmm lvA kgt kgt_ev umm stv omm o_ev ogn rd_p otr omix wo
        wo_ev lg sig ohs posm slots_d scat xl0 xl1 xtr x_round x_rest silu a_d atr a_round a_rest w_round
        w_rest y_d y_a ystore moe_used comb out_s vstep astep pstep lbx lbd memz ginit xdone proj_x condx
        o_fin qk_d2 modb gnb comb_a comb_v comb_p xtr2 wl1""".split()
        S = {n: sem("s_" + n) for n in names}
        gats = [sem(f"s_gathered{i}") for i in range(NT)]
        LONG = [{n: sem(f"s_long{l}_{n}") for n in "x xT w xe gu silu a aT aTe y yh ye store".split()} for l in range(L)]
        ml = [sem(f"s_expert_slab{i}") for i in range(6)]

        class Eng:
            def __init__(self, eng):
                self.e, self.n = eng, {}

            def up(self, name, k=1):
                self.n[name] = self.n.get(name, 0) + k
                return self.n[name]

            def wait(self, name, value):
                self.e.wait_ge(S[name], value)

            def next(self, name, k=1):
                self.e.wait_ge(S[name], self.up(name, k))

            def lag(self, name, value):
                if value > 0:
                    self.e.wait_ge(S[name], value)

            def step(self, ins, name):
                ins.then_inc(S[name], 1)
                self.e.wait_ge(S[name], self.up(name))

        block = ctx.enter_context(nc.Block())

        def w_view(w, cols):
            return w[:, cols].rearrange("(p k) n -> p k n", k=KD)

        def long_lists(eng, l):
            n_max = eng.value_load(offs[0:1, NE + 2:NE + 3], min_val=0, max_val=TT)
            return eng.If(n_max > LONG_FROM)

        @block.sync
        def _(sp):
            E = Eng(sp)
            n = [0]

            def slabs(upto):
                while n[0] < upto:
                    kind, l, c = RING[n[0]]
                    width = 256 if (kind, c) == ("i", 4) else 512
                    cols = slice(512 * c, 512 * c + width)
                    if kind == "o":
                        src = T["w_out"][l][:, cols].rearrange("(k p) n -> p k n", p=P)
                    else:
                        src = w_view(T["w_mod" if kind == "m" else "w_in"][l], cols)
                    E.lag("slab_used", n[0] - 1)
                    if n[0] in (RING_LOOP[0], RING_LOOP[0] + 1):
                        E.wait("moe_used", 4 + UNITS - (2 if n[0] % 2 == 0 else 1))
                    sp.dma_start(ring[:, n[0] % 2, :].rearrange("p (k n) -> p k n", k=KD)[:, :, 0:width], src).then_inc(S[f"wl{n[0] % 2}"], 16)
                    n[0] += 1

            sp.dma_start(cond[:, 0, :], T["c"][0].rearrange("(p k) -> p k", k=KD)).then_inc(S["cond_in"], 16)
            sp.dma_start(cond[:, 1, :], T["c_ctx"].rearrange("(p k) -> p k", k=KD)).then_inc(S["cond_in"], 16)
            slabs(2)
            for a, src in enumerate((T["x"][0], T["ctx"][0])):
                sp.dma_start(x_sb[64 * a:64 * a + 64, :, :], src.rearrange("(i p) d -> p i d", p=64)).then_inc(S["x_in"], 16)
                slabs(3 + a)
            for l in range(L):
                slabs(used(("o", l, NWO - 1)))
                wg, wu, wd = T["moe_w_gate"][l], T["moe_w_up"][l], T["moe_w_down"][l]

                def expert_slab(e, m):
                    k = m // 2
                    w = (wg, wu, wd)[k]
                    kk = KF if k == 2 else KD
                    src = w[e] if isinstance(e, int) else w[bass.ds(e, 1)].rearrange("o a b -> (o a) b")
                    src = src.rearrange("(p k) n -> p (k n)", k=kk)
                    h = slice(m % 2 * (SLAB // 2), (m % 2 + 1) * (SLAB // 2))
                    sp.dma_start(raw[k][:, h], src[:, h]).then_inc(ml[m], 16)

                def expert_rows(e, u):
                    at = sp.value_load(offs[0:1, e:e + 1] if isinstance(e, int) else offs[0:1, bass.ds(e, 1)],
                                       min_val=0, max_val=2 * TT)
                    sp.dma_start(xe[:, u, :], X_s[bass.ds(at, P), :]).then_inc(S[f"xl{u}"], 16)

                slabs(used(("m", 0, 11)) if l == 0 else RING_LOOP[1])
                E.wait("slab_used", used(("o", l, NWO - 1)))
                for m in range(6):
                    expert_slab(0, m)
                slabs(RING_LOOP[l])
                def next_slabs(i, u, ms):
                    for m in ms:
                        sp.wait_ge(S["w_rest"], i * 12 + (UNITS * l + 6 * u + m + 1))
                        expert_slab(i * 2 + (u + 1), m)

                def next_expert(i, u, ms=range(6)):
                    next_slabs(i, u, ms)
                    sp.wait_ge(S["xtr2"], i * 2 + ((NE + 1) * l + u + 1))
                    expert_rows(i * 2 + (2 + u), u)
                next_slabs(0, 0, range(POOLED[l]))
                E.next("scat", 16 * 2 * (NT if l == 0 else SEQ // P))
                E.next("slots_d", 1)
                for u in range(2):
                    expert_rows(u, u)
                next_expert(0, 0, range(POOLED[l], 6))
                next_expert(0, 1)
                with sp.Fori(1, NE // 2 - 1) as i:
                    for u in range(2):
                        next_expert(i, u)
                next_expert(NE // 2 - 1, 0)
                if l == 0:
                    slabs(RING_LOOP[0] + 2)
                E.wait("moe_used", (UNITS + 4) * (l + 1))
                E.wait("ystore", 16 * (NE * (l + 1) + 1))
                with long_lists(sp, l):
                    O, nj = LONG[l], tiles_of(l)
                    with sp.Fori(0, NE) as e:
                        for k in range(3):
                            w, kk = (wg, wu, wd)[k], KF if k == 2 else KD
                            src = w[bass.ds(e, 1)].rearrange("o a b -> (o a) b").rearrange("(p k) n -> p (k n)", k=kk)
                            sp.dma_start(raw[k], src).then_inc(O["w"], 16)
                        at = sp.value_load(offs[0:1, bass.ds(e, 1)], min_val=0, max_val=2 * nj * P)
                        for j in range(nj):
                            sp.dma_start(xe[:, 0, :], X_s[bass.ds(at + j * P, P), :]).then_inc(O["x"], 16)
                            sp.wait_ge(O["yh"], e * nj + (j + 1))
                            sp.wait_ge(O["ye"], e * nj + (j + 1))
                            sp.dma_start(Y_s[bass.ds(at + j * P, P), :], y_e).then_inc(O["store"], 16)
            for i in range(SEQ // P):
                E.wait("comb" if i % 2 else "comb_p", NT // 2 + 1)
                sp.dma_start(T["out"][0, i * P:(i + 1) * P, :], x_sb[:, 2 * i, :]).then_inc(S["out_s"], 16)
            E.wait("out_s", 16 * (SEQ // P))

        @block.gpsimd
        def _(pool):
            E = Eng(pool)
            g = nc.gpsimd

            def powr(dst, src, sem_out):
                E.step(g.tensor_tensor(dst, src, mhalf[:, 0:src.shape[-1]] if len(src.shape) == 2 else
                                       mhalf[:, 0:src.shape[1] * src.shape[2]].rearrange("p (a b) -> p a b", a=src.shape[1]),
                                       ALU.pow), sem_out)

            E.step(g.memset(mhalf, -0.5), "pstep")
            g.memset(pool_bd[:], 0.0).then_inc(S["memz"], 1)
            g.memset(ones[:], 1.0).then_inc(S["memz"], 1)
            g.memset(zeros, 0.0).then_inc(S["memz"], 1)
            E.wait("memz", 3)
            g.dma_start(Y_s[0:P, 0:64], ones[:, 0:64]).then_inc(S["ystore"], 16)
            for l in range(L):
                nt2 = NT if l == 0 else SEQ // P
                E.next("rstd_d")
                powr(rstd[:, 0:NT], ss[:, 0:NT], "rstd_p")
                M = 8
                E.wait("ht", PH[l])
                for z in Z:
                    E.step(g.memset(z[:, :, :, :], 0.0), "zbuf")
                E.next("kq_d")
                powr(rsq, ssq, "qk_p")
                E.next("bpool", 2)
                n_ = ZW - 1
                E.step(g.tensor_tensor(Z[1][:, :, :, 0:n_], Z[0][:, :, :, 0:n_], Z[0][:, :, :, 1:n_ + 1], ALU.add), "pstep")
                x0 = lambda p0, c: Z[0][p0:p0 + 64, c, :, M:M + SEQ]
                dv = lambda p0, c: dpool[p0:p0 + 64, c, :].rearrange("p (s t) -> p s t", s=2)
                ic = lambda p0, c: invcnt[p0:p0 + 64, c, :].unsqueeze(1).broadcast_to([64, 2, SEQ])

                def finish(zsum, p0, c, half):
                    E.step(g.tensor_tensor(dv(p0, c), zsum[p0:p0 + 64, c, :, M - half:M - half + SEQ], ic(p0, c), ALU.mult), "pstep")
                    E.step(g.tensor_tensor(dv(p0, c), dv(p0, c), x0(p0, c), ALU.subtract), "dp")
                finish(Z[1], 0, 0, 1)
                n_ -= 2
                E.step(g.tensor_tensor(Z[2][:, :, :, 0:n_], Z[1][:, :, :, 0:n_], Z[1][:, :, :, 2:n_ + 2], ALU.add), "pstep")
                finish(Z[2], 64, 0, 2)
                n_ -= 4
                E.step(g.tensor_tensor(Z[1][:, 1, :, 0:n_], Z[2][:, 1, :, 0:n_], Z[2][:, 1, :, 4:n_ + 4], ALU.add), "pstep")
                finish(Z[1], 0, 1, 4)
                n_ -= 8
                E.step(g.tensor_tensor(Z[2][64:128, 1, :, 0:n_], Z[1][64:128, 1, :, 0:n_], Z[1][64:128, 1, :, 8:n_ + 8], ALU.add), "pstep")
                finish(Z[2], 64, 1, 8)
                E.wait("proj_d", sum(len(PROJ[i]) for i in range(l + 1)))
                E.wait("qkt", NT * (l + 1))
                q_flat = q_t.rearrange("p c t -> p (c t)")
                for d in range(2):
                    E.step(g.tensor_tensor(QF[d], q_flat, f_t[d], ALU.mult), "pstep")
                E.step(g.tensor_tensor(qk_same, KG[0], KG[1], ALU.add), "pstep")
                E.step(g.tensor_tensor(qk_same, qk_same, q_flat, ALU.mult), "hq")
                E.next("pv_ev", 8 * nt2)
                for b in range(2):
                    E.step(g.memset(QP[b][64:128, :, 0, :], 0.0), "zeroed")
                    E.step(g.memset(QP[b][0:64, :, 1, :], 0.0), "zeroed")
                tcur = f_t[1]
                toff = 0
                for w in LEVELS:
                    E.next("lvcp", 2)
                    k = KG[1].rearrange("p (n a w) -> p n a w", a=2, w=w)
                    t = tcur.rearrange("p (n a) -> p n a", a=2)
                    nb = 1024 // (2 * w)
                    q, tq = wanted_q(l, QF[1], tcur, w, 0, 1)
                    E.step(g.tensor_tensor(q, q, tq, ALU.mult), "lvup")
                    E.next("lvcp", 1)
                    E.step(g.tensor_tensor(k[:, :, 1, :], k[:, :, 1, :], t[:, :, 0:1].broadcast_to([P, nb, w]), ALU.mult), "lvup")
                    tn = tots[1][:, toff:toff + nb]
                    E.step(g.tensor_tensor(tn, t[:, :, 0], t[:, :, 1], ALU.mult), "lvup")
                    E.up("lvcp", 3)
                    tcur = tn
                    toff += nb
                for j in range(nt2):
                    E.next("ogn")
                    powr(rsq[:, j, 0:4], ssq[:, j, 0:4], "rd_p")
                E.next("rstd_d")
                powr(rstd[:, 0:nt2], ss[:, 0:nt2], "rstd_p")
                for m in range(POOLED[l]):
                    E.wait("w_round", UNITS * l + m + 1)
                    E.step(g.tensor_tensor(split[:, PLACE[m], 1, :], raw[0][:, m * (SLAB // 2):(m + 1) * (SLAB // 2)],
                                           split[:, PLACE[m], 0, :].bitcast(f32), ALU.subtract), "w_rest")
                E.up("w_rest", UNITS - POOLED[l])
                E.next("slots_d")
                if l == 0:
                    E.wait("ginit", 16)
                tiles = range(NT) if l == 0 else range(SEQ // P)
                for i in tiles:
                    for c in range(2):
                        g.indirect_dma_start(out=X_s, out_offset=bass.IndirectOffsetOnAxis(ap=idx[:, c, i:i + 1], axis=0),
                                             in_=rows[:, i, :], in_offset=None).then_inc(S["scat"], 16)
                with pool.Fori(0, NE) as e:
                    pool.wait_ge(S["y_a"], e + ((NE + 1) * l + 2))
                    pool.wait_ge(S["y_d"], e + ((NE + 1) * l + 2))
                    at = pool.value_load(offs[0:1, bass.ds(e, 1)], min_val=0, max_val=2 * TT)
                    pool.dma_start(Y_s[bass.ds(at, P), :], y_e).then_inc(S["ystore"], 16)
                E.wait("ystore", 16 * (NE * (l + 1) + 1))
                with long_lists(pool, l):
                    pool.wait_ge(LONG[l]["store"], 16 * NE * tiles_of(l))
                for i in tiles:
                    for c in range(2):
                        g.indirect_dma_start(out=yg[:, i, c, :], out_offset=None, in_=Y_s[0:2 * TT, :],
                                             in_offset=bass.IndirectOffsetOnAxis(ap=idx[:, c, i:i + 1], axis=0)
                                             ).then_inc(gats[i], 16)
                for i in tiles:
                    if i % 2 == 0:
                        E.n["comb_v"] = E.n.get("comb_v", 0) + 1
                        E.wait("comb_v", E.n["comb_v"])
                        E.step(g.tensor_tensor(yg[:, i, 0, :], yg[:, i, 0, :], mod[:, 5, :], ALU.mult), "pstep")
                        xt = x_sb[:, (i if l == 0 else 2 * i), :]
                        g.tensor_tensor(xt, xt, yg[:, i, 0, :], ALU.add).then_inc(S["comb_p"], 1)

        @block.tensor
        def _(pe):
            E = Eng(pe)
            mm, tr = nc.tensor.matmul, nc.tensor.transpose
            n = [0]

            def slab_in(key):
                assert RING[n[0]] == key
                s = n[0] % 2
                pe.wait_ge(S[f"wl{s}"], 16 * (n[0] // 2 + 1))
                n[0] += 1
                return ring[:, s, :].rearrange("p (k n) -> p k n", k=KD)

            def rows_transposed(i):
                for kk in range(2):
                    g_ = E.n.get("ht", 0)
                    E.lag("ht_ev", g_ - 1)
                    for k in range(4):
                        last = tr(ps[2 + g_ % 2][:, k * P:(k + 1) * P], rows[:, i, 4 * kk + k::KD], ident[:])
                    last.then_inc(S["ht"], 1)
                    E.up("ht")

            def mod_slab(l, s):
                if (l, s) in ((0, 0), (1, 4)):
                    E.next("condm")
                E.lag("mod_ev", mod_free(l, s))
                w = slab_in(("m", l, s))
                for k in range(KD):
                    last = mm(ps[mod_bank(l, s)][:], cmix[:, k, :], w[:, k, :], start=(k == 0), stop=(k == KD - 1))
                last.then_inc(S["slab_used"], 1)

            for l in range(L):
                nt2 = NT if l == 0 else SEQ // P
                for s in (range(5) if l == 0 else [7]):
                    mod_slab(l, s)
                if l == 0:
                    E.wait("ident_in", 16)
                for i in range(NT):
                    E.next("rows_d")
                    rows_transposed(i)
                E.wait("ht_ev", E.n["ht"])

                def proj(out, k, lhsT, rhs):
                    return mm(out, lhsT, rhs, start=(k == 0), stop=(k == KD - 1))

                def group():
                    b = 4 + E.n.get("proj", 0) % 4
                    E.lag("proj_d", E.n.get("proj", 0) - 3)
                    E.up("proj")
                    return ps[b]
                def qk_turned(j):
                    E.next("qk_d2")
                    g_ = E.n.get("qkt", 0)
                    E.lag("qkt_ev", g_ - 1)
                    for c in range(4 if j < nt2 else 0):
                        tr(ps[g_ % 2][:, c * P:(c + 1) * P], qkr[:, j % 2, c * P:(c + 1) * P], ident[:])
                    tr(ps[2 + g_ % 2][:, 0:P], qkr[:, j % 2, 4 * P:5 * P], ident[:]).then_inc(S["qkt"], 1)
                    E.up("qkt")

                E.wait("mod_ev", NMOD * l + (5 if l == 0 else 8))
                if l == 0:
                    E.wait("consts", NCONST)
                    E.wait("memz", 3)
                gi = 0
                for s in IN_ORDER:
                    tc, tk = [((0, 128, 256, 384), None), ((0, 128), (256, 512)), ((256, 384), (0, 256)),
                              ((), (0, 512)), ((), (0, 256))][s]
                    w = slab_in(("i", l, s))
                    jobs = [(c, None) for c in tc] + [(None, j) for j in (range(NT if s in (1, 4) else nt2) if tk else ())]
                    nq = nt2 * P if s == 2 else TT
                    for c, j in jobs:
                        b = group()
                        for k in range(KD):
                            if j is None:
                                nn = nt2 * P if s == 0 and c < 256 else nq
                                last = proj(b[:, 0:nn], k, w[:, k, c:c + 128], actT[:, k, 0:nn])
                            else:
                                last = proj(b[:, 0:tk[1] - tk[0]], k, actT[:, k, j * P:(j + 1) * P], w[:, k, tk[0]:tk[1]])
                        last.then_inc(S["proj"], 1)
                        if (c, j) == jobs[-1]:
                            pe.wait_ge(S["proj"], E.n["proj"])
                            pe.sem_inc(S["slab_used"], 1)
                        if gi in QK_TURN[l]:
                            qk_turned(QK_TURN[l][gi])
                        gi += 1
                E.wait("qkt_ev", E.n["qkt"])
                E.wait("proj_d", E.n["proj"])
                units = [(j, h) for j in range(nt2) for h in range(8)]

                def scores(u):
                    j, h = units[u]
                    a = 64 * (h // 4)
                    g_ = E.n.get("sc", 0)
                    E.lag("sexp", g_ - 2)
                    keys = slice(0, TT) if j < SEQ // P else slice(SEQ, TT)
                    nk = keys.stop - keys.start
                    mm(ps[g_ % 3][:, 0:nk], qT[a:a + 64, h % 4, j * P:(j + 1) * P], kT[a:a + 64, keys],
                       start=True, stop=True).then_inc(S["sc"], 1)
                    E.up("sc")

                def values(u):
                    j, h = units[u]
                    kt = range(NT) if j < SEQ // P else range(SEQ // P, NT)
                    E.next("pnorm")
                    g_ = E.n.get("ptr", 0)
                    E.lag("pt_ev", g_ - 1)
                    for m, _ in enumerate(kt):
                        last = tr(ps[3 + g_ % 2][:, m * P:(m + 1) * P], Pb[:, g_ % 4, m * P:(m + 1) * P], ident[:])
                    last.then_inc(S["ptr"], 1)
                    E.up("ptr")
                    return g_, kt

                def outv(u, g_, kt):
                    j, h = units[u]
                    E.next("pt_ev")
                    E.lag("pv_ev", g_ - 1)
                    for m, t_ in enumerate(kt):
                        last = mm(ps[5 + g_ % 2][0:64, 0:P], qkv[:, t_, QK + 64 * (h // 4):QK + 64 * (h // 4) + 64],
                                  PT[:, g_ % 2, m * P:(m + 1) * P], start=(m == 0), stop=(m == len(kt) - 1))
                    last.then_inc(S["pv"], 1)
                    E.up("pv")
                for u in range(3):
                    scores(u)
                turned = {}
                for u in range(len(units) + 2):
                    if 1 <= u and u + 2 < len(units):
                        scores(u + 2)
                    if u >= 2:
                        outv(u - 2, *turned.pop(u - 2))
                    if u in AMONG[l]:
                        mod_slab(l, AMONG[l][u])
                    if u < len(units):
                        turned[u] = values(u)
                E.wait("pv_ev", E.n["pv"])
                E.wait("mod_ev", NMOD * l + max(AMONG[l].values()) + 1)
                E.next("dp", 4)
                for c in range(2):
                    mm(ps[7][:, 0:nt2 * P], pool_bd[:, c, :], dpool[:, c, 0:nt2 * P], start=True, stop=True).then_inc(S["ymm"], 1)
                    E.next("ymix")
                E.next("hq")
                for j in range(nt2):
                    for c in range(2):
                        last = mm(ps[4][:, (2 * j + c) * 2:(2 * j + c) * 2 + 2], qk_same[:, c * TT + j * P:c * TT + (j + 1) * P],
                                  headsep[:, 0::HD], start=True, stop=True)
                last.then_inc(S["dg"], 1)
                mod_slab(l, AFTER_ATTN[l])
                for v, w in enumerate(LEVELS):
                    E.next("lvcp", 6)
                    if v < 2:
                        E.next("zeroed", 2)
                    if v == 1:
                        E.next("dg_ev")
                        E.wait("mod_ev", NMOD * l + AFTER_ATTN[l] + 1)
                    for j in range(nt2):
                        E.lag("lvA", E.n.get("lvmm", 0) + 1 - 2 * nt2)
                        for c in range(2):
                            last = mm(ps[4 * (v % 2) + j][:, c * 2 * P:(c + 1) * 2 * P].rearrange("p (a t) -> p a t", a=2),
                                      KP[v % 2][:, c, j * P:(j + 1) * P], QP[v % 2][:, c, :, j * P:(j + 1) * P], start=True, stop=True)
                        last.then_inc(S["lvmm"], 1)
                        E.up("lvmm")
                E.wait("lvA", E.n["lvmm"] - nt2)
                E.next("lvdn", 3 * len(LEVELS))
                E.next("lvup", 3 * len(LEVELS))
                for d in range(2):
                    for c in range(2):
                        for j in range(NT):
                            last = tr(ps[4 + 2 * d + c][:, j * P:(j + 1) * P], KG[d][:, c * 512 + j * P:c * 512 + (j + 1) * P], ident[:])
                        last.then_inc(S["kgt"], 1)
                E.next("kgt_ev", 4)
                E.wait("lvA", E.n["lvmm"])
                order = ORDER
                for s in range(3):
                    for d in range(2):
                        for c in range(2):
                            j = order[d][s]
                            last = mm(ps[s][:, (2 * d + c) * P:(2 * d + c + 1) * P], kg_tok[:, d, c, j, :],
                                      v_a[:, j, c * P:(c + 1) * P], start=True, stop=True)
                    last.then_inc(S["umm"], 1)
                for s in IN_STATES[l]:
                    mod_slab(l, s)
                E.next("stv")
                for j in range(nt2):
                    for c in range(2):
                        for a in range(2):
                            o, hc = ps[j][:, (2 * c + a) * HD:(2 * c + a + 1) * HD], slice(a * HD, (a + 1) * HD)
                            for d in range(2):
                                mm(o, QF[d][:, c * 512 + j * P:c * 512 + (j + 1) * P], S_st[:, d, c, j, hc], start=(d == 0), stop=False)
                            last = mm(o, A_s[:, j, 2 * c + a, :], v_a[:, j, (2 * c + a) * HD:(2 * c + a + 1) * HD], start=False, stop=True)
                    last.then_inc(S["omm"], 1)
                for j in range(nt2):
                    E.next("o_fin")
                    for c in range(2):
                        last = tr(ps[4 + j][:, c * P:(c + 1) * P], osb[:, j, c * P:(c + 1) * P], ident[:])
                    last.then_inc(S["otr"], 1)
                E.next("omix", nt2)
                for s in range(NWO):
                    w = slab_in(("o", l, s))
                    for i in range(nt2):
                        g_ = E.n.get("wo", 0)
                        E.lag("wo_ev", g_ - 3)
                        for k in range(KD):
                            last = mm(ps[g_ % 4][:], actT[:, k, i * P:(i + 1) * P], w[:, k, :], start=(k == 0), stop=(k == KD - 1))
                        last.then_inc(S["wo"], 1)
                        E.up("wo")
                    pe.wait_ge(S["wo"], E.n["wo"])
                    pe.sem_inc(S["slab_used"], 1)
                mod_slab(l, BEHIND_OUT[l])
                E.wait("wo_ev", E.n["wo"])

                def logits(i):
                    E.wait("ht_ev", E.n["ht"] - 2 * (nt2 - 1 - i) if i == nt2 - 1 else E.n["ht"] - 2)
                    for k in range(KD):
                        last = mm(ps[4][:, i * NE:(i + 1) * NE], actT[:, k, i * P:(i + 1) * P], rw[:, k, :],
                                  start=(k == 0), stop=(k == KD - 1))
                    return last
                for i in range(nt2):
                    E.next("rows_d")
                    rows_transposed(i)
                    if i:
                        logits(i - 1)
                logits(nt2 - 1).then_inc(S["lg"], 1)
                pe.sem_inc(S["moe_used"], 4)
                mod_slab(*ROUTER_MODS[l][0])
                E.next("ohs")
                oh = rtmp[:, OH0:OH0 + nt2 * NE].rearrange("p (i e) -> p i e", e=NE)
                for i in range(nt2 + 1):
                    for j in range(min(i + 1, nt2)):
                        lhs = before if j == i else ones
                        last = mm(ps[5][:, i * NE:(i + 1) * NE], lhs[:], oh[:, j, :], start=(j == 0), stop=(j == min(i, nt2 - 1)))
                last.then_inc(S["posm"], 1)
                for m in ROUTER_MODS[l][1:]:
                    mod_slab(*m)
                E.next("slots_d")
                GB, UB, AB, X0, X1, D0, D1 = 0, 1, 2, 3, 4, 5, 6
                b17 = (NE + 1) * l
                b16 = NE * l

                def x_transposed(u, h):
                    for k in range(4 * h, 4 * h + 4):
                        last = tr(ps[X0 + h][:, (k % 4) * P:(k % 4 + 1) * P], xe[:, u, k::KD], ident[:])
                    last.then_inc(S["xtr2" if h else "xtr"], 1)
                pe.wait_ge(S["xl0"], 16 * (9 * l + 1))
                x_transposed(0, 0)
                x_transposed(0, 1)

                def half_slab(i, u, m, banks, act2, kk):
                    pe.wait_ge(S["w_rest"], i * 12 + (UNITS * l + 6 * u + m + 1))
                    w = split[:, PLACE[(6 * u + m) % 4]].rearrange("p a (k n) -> p a k n", k=kk // 2)
                    for h, bank in enumerate(banks):
                        for k in range(kk // 2):
                            ka = m % 2 * (kk // 2) + k
                            for a, b in ((0, 0), (0, 1), (1, 0)):
                                last = mm(ps[bank][:], act2[:, a, ka, :], w[:, b, k, 512 * h:512 * h + 512],
                                          start=(ka == 0 and a + b == 0), stop=(ka == kk - 1 and a == 1))
                    last.then_inc(S["moe_used"], 1)
                with pe.Fori(0, NE // 2) as i:
                    for u in range(2):
                        pe.wait_ge(S["x_rest"], i * 4 + (2 * b17 + 2 * u + 2))
                        for m in range(4):
                            half_slab(i, u, m, (GB,) if m < 2 else (UB,), xs, KD)
                        if u == 0:
                            pe.wait_ge(S["xl1"], i * 16 + 16 * (8 * l + 1))
                        else:
                            pe.wait_ge(S["xl0"], i * 16 + 16 * (9 * l + 2))
                        x_transposed(1 - u, 0)
                        pe.wait_ge(S["a_d"], i * 2 + (b16 + u + 1))
                        for k in range(KF):
                            last = tr(ps[AB][:, k * P:(k + 1) * P], act_e[:, k::KF], ident[:])
                        last.then_inc(S["atr"], 1)
                        x_transposed(1 - u, 1)
                        pe.wait_ge(S["a_rest"], i * 2 + (b16 + u + 1))
                        pe.wait_ge(S["y_d"], i * 2 + (b17 + u + 1))
                        pe.wait_ge(S["y_a"], i * 2 + (b17 + u + 1))
                        for m in (4, 5):
                            half_slab(i, u, m, (D0, D1), acs, KF)
                E.wait("y_d", b17 + NE + 1)
                E.wait("y_a", b17 + NE + 1)
                E.wait("x_rest", 2 * (b17 + NE + 1))
                with long_lists(pe, l):
                    O, nj = LONG[l], tiles_of(l)
                    wg, wu = (raw[k].rearrange("p (k n) -> p k n", k=KD) for k in range(2))
                    wd = raw[2].rearrange("p (k n) -> p k n", k=KF)
                    with pe.Fori(0, NE) as e:
                        for j in range(nj):
                            pe.wait_ge(O["x"], e * (16 * nj) + 16 * (j + 1))
                            for k in range(KD):
                                last = tr(ps[X0 + k // 4][:, (k % 4) * P:(k % 4 + 1) * P], xe[:, 0, k::KD], ident[:])
                            last.then_inc(O["xT"], 1)
                            pe.wait_ge(O["xe"], e * (2 * nj) + 2 * (j + 1))
                            pe.wait_ge(O["w"], e * 48 + 48)
                            for bank, w in ((GB, wg), (UB, wu)):
                                for k in range(KD):
                                    last = mm(ps[bank][:], xeT[:, k, :], w[:, k, :], start=(k == 0), stop=(k == KD - 1))
                            last.then_inc(O["gu"], 1)
                            pe.wait_ge(O["a"], e * nj + (j + 1))
                            for k in range(KF):
                                last = tr(ps[AB][:, k * P:(k + 1) * P], act_e[:, k::KF], ident[:])
                            last.then_inc(O["aT"], 1)
                            pe.wait_ge(O["aTe"], e * nj + (j + 1))
                            for h in range(2):
                                for k in range(KF):
                                    last = mm(ps[D0 + h][:], aT[:, k, :], wd[:, k, h * 512:(h + 1) * 512], start=(k == 0), stop=(k == KF - 1))
                            last.then_inc(O["y"], 1)
                            pe.wait_ge(O["yh"], e * nj + (j + 1))
                            pe.wait_ge(O["ye"], e * nj + (j + 1))
                if l == 0:
                    E.wait("mod_ev", NMOD + 3)
                    for s in range(3, 7):
                        mod_slab(1, s)

        @block.scalar
        def _(act):
            E = Eng(act)
            A = nc.scalar.activation

            def copy(o, i):
                return A(o, i, ACT.Copy)

            def bias(l, a, b):
                act.dma_start(mod[:, a:b, :].rearrange("p a n -> p (a n)"),
                              T["b_mod"][l:l + 1, a * D:b * D].broadcast_to([P, (b - a) * D])).then_inc(S["modb"], 16)

            def norm_gain(l, name, halves=(0, 1)):
                for h in halves:
                    dst = gn_half_1 if (name, h) == ("norm1_g", 1) else gn_half[h]
                    act.dma_start(dst, T[name][l:l + 1, 512 * h:512 * h + 512].broadcast_to([P, 512])).then_inc(S["gnb"], 16)

            def gains(l):
                act.dma_start(gain_qk[:, 0, :], T["q_norm_g"][l:l + 1, :].broadcast_to([P, HD])).then_inc(S["gains"], 16)
                act.dma_start(gain_qk[:, 1, :], T["k_norm_g"][l:l + 1, :].broadcast_to([P, HD])).then_inc(S["gains"], 16)
                act.dma_start(gain_o[:], T["hgrn_norm_g"][l:l + 1, :].broadcast_to([P, HD])).then_inc(S["gains"], 16)
                for gi in range(4):
                    a = 64 * (gi % 2)
                    act.dma_start(pool_bd[a:a + 64, gi // 2, a:a + 64], T["pool_w"][l, gi]).then_inc(S["gains"], 16)
                act.dma_start(pool_sc[:], T["pool_scale_cols"][l]).then_inc(S["gains"], 16)

            E.wait("cond_in", 32)
            E.step(A(cond[:], cond[:], ACT.Silu), "condx")
            for l_ in range(2):
                act.dma_start(lbr[:, l_, :], T["hgrn_lb_cols"][l_]).then_inc(S["lb_in"], 16)
            bias(0, 0, 2)
            E.next("lbd")
            E.step(A(lbe[:, 0:8], lbe[:, 0:8], ACT.Exp), "lbx")
            E.wait("wl0", 32)
            act.dma_start(gn[:, 0, :], T["norm1_g"][0:1, :].broadcast_to([P, D])).then_inc(S["gn_in"], 16)
            E.wait("x_in", 32)
            act.dma_start(ident[:], T["k_ident"]).then_inc(S["ident_in"], 16)

            def head_constants():
                bias(0, 2, 6)
                act.dma_start(before[:], T["k_before"]).then_inc(S["consts"], 16)
                act.dma_start(headsep[:], T["k_headsep"]).then_inc(S["consts"], 16)
                act.dma_start(masks_f, T["k_masks"].rearrange("p a b -> p (a b)")).then_inc(S["consts"], 16)
                act.dma_start(rope[:], T["k_rope"]).then_inc(S["consts"], 16)
                act.dma_start(invcnt[:], T["k_invcnt"]).then_inc(S["consts"], 16)
                act.dma_start(rw[:], T["router_w"].rearrange("(p k) e -> p k e", k=KD)).then_inc(S["consts"], 16)
                act.dma_start(rb[:], T["router_b"].rearrange("(a e) -> a e", a=1).broadcast_to([P, NE])).then_inc(S["consts"], 16)
                act.dma_start(rconst, T["k_router"]).then_inc(S["consts"], 16)
                E.wait("memz", 3)
                gains(0)
            for l in range(L):
                nt2 = NT if l == 0 else SEQ // P
                E.wait("x_in", 32)

                def squares(tiles, ts, jb):
                    for i in range(tiles):
                        if l:
                            E.wait("comb" if i % 2 else "comb_p", i // 2 + 1)
                        E.step(A(jb, x_sb[:, ts[i], :], ACT.Square, accum_out=ss[:, i:i + 1]), "sqs")
                squares(NT, range(NT), junk2 if l else junk[:, 0, :])
                if l == 0:
                    E.wait("mod_ev", 1)
                    head_constants()

                def ht_evac(n, mixed):
                    for _ in range(n):
                        for kk in range(2):
                            g_ = E.n.get("ht", 0)
                            i = htile[0]
                            E.next("ht")
                            if mixed:
                                dst = actT[:].rearrange("p k (s t) -> p (k s) t", s=2)[:, 8 * kk:8 * kk + 8, 64 * i:64 * i + 64]
                                src = ps[2 + g_ % 2][:].rearrange("p (a t) -> p a t", t=64)
                            else:
                                dst = actT[:, 4 * kk:4 * kk + 4, i * P:(i + 1) * P]
                                src = ps[2 + g_ % 2][:].rearrange("p (a t) -> p a t", t=P)
                            E.step(copy(dst, src), "ht_ev")
                        htile[0] += 1
                htile = [0]
                if l:
                    bias(1, 5, 6)
                ht_evac(NT, True)
                norm_gain(l, "norm2_g")
                if l == 0:
                    act.dma_start(X_s[2 * TT:2 * TT + CAP, :].rearrange("(a p) d -> p a d", p=P),
                                  zeros.unsqueeze(1).broadcast_to([P, CAP // P, D])).then_inc(S["ginit"], 16)
                def qk_out(j):
                    g_ = E.n.get("qkt", 0)
                    E.next("qkt")
                    if j < nt2:
                        E.step(copy(qT[:, :, j * P:(j + 1) * P], ps[g_ % 2][:].rearrange("p (c t) -> p c t", c=4)), "astep")
                    E.step(copy(kT[:, j * P:(j + 1) * P], ps[2 + g_ % 2][:, 0:P]), "qkt_ev")
                for gi, (kind, a) in enumerate(PROJ[l]):
                    g_ = E.n.get("proj", 0)
                    b = ps[4 + g_ % 4]
                    E.next("proj")
                    if kind == "q":
                        E.step(A(q_t[:, a, 0:nt2 * P], b[:, 0:nt2 * P], ACT.Sigmoid), "sgm")
                    elif kind == "f":
                        d, c = a
                        E.step(A(f_t[d][:, c * 512:(c + 1) * 512], b[:], ACT.Sigmoid), "astep")
                        E.step(A(KG[d][:, c * 512:(c + 1) * 512], b[:], ACT.Sigmoid, scale=-1.0), "sgm")
                    elif kind == "g":
                        E.step(A(g_a[:, a, :], b[:, 0:256], ACT.Sigmoid), "sgm")
                    elif kind == "v":
                        E.step(copy(v_a[:, a, :], b[:, 0:256]), "proj_x")
                    elif kind == "b":
                        E.lag("zbuf", 3 * (l + 1))
                        ns = nt2 * P // SEQ
                        E.step(copy(Z[0][:, a, 0:ns, 8:8 + SEQ], b[:, 0:nt2 * P].rearrange("p (s t) -> p s t", s=ns)), "bpool")
                    elif kind == "cq":
                        E.step(copy(qkv[:, a, 0:512], b[:]), "proj_x")
                    elif kind == "ck":
                        E.step(copy(qkv[:, a, 512:768], b[:, 0:256]), "proj_x")
                    if gi in QK_TURN[l]:
                        qk_out(QK_TURN[l][gi])
                if l == 0:
                    bias(1, 0, 2)
                    E.wait("ginit", 16)
                units = [(j, h) for j in range(nt2) for h in range(8)]
                for u in range(len(units) + 2):
                    if u < len(units):
                        j, h = units[u]
                        nk = TT if j < SEQ // P else CTX
                        g_ = E.n.get("sexp", 0)
                        E.next("scmax")
                        E.lag("ptr", g_ - 3)
                        E.step(A(Pb[:, g_ % 4, 0:nk], ps[g_ % 3][:, 0:nk], ACT.Exp, bias=nmx[:, u:u + 1], scale=HD ** -0.5,
                                 accum_out=rsum[:, u:u + 1]), "sexp")
                    if u >= 2:
                        j, h = units[u - 2]
                        nk = TT if j < SEQ // P else CTX
                        g_ = E.n.get("pt_ev", 0)
                        E.next("ptr")
                        E.lag("pv", g_ - 1)
                        E.step(copy(PT[:, g_ % 2, 0:nk], ps[3 + g_ % 2][:, 0:nk]), "pt_ev")
                E.wait("pv", E.n["pt_ev"])
                E.next("hq")
                for v, w in enumerate(LEVELS):
                    if v >= 2:
                        E.wait("lvmm", len(LEVELS) * NT * l + nt2 * (v - 1))
                    for z, done in ((1, "lvup"), (0, "lvdn")):
                        qf, kg = (y.rearrange("p (c t) -> p c t", c=2) for y in (QF[z], KG[z]))
                        for a in range(2):
                            if v and a == 0:
                                E.wait(done, 3 * (len(LEVELS) * l + v - 1) + 1)
                            hs = slice(64 * a, 64 * a + 64)
                            copy(lane(l, QP[v % 2][hs, :, a, :], w, 1 - z), lane(l, qf[hs], w, 1 - z)).then_inc(S["lvcp"], 1)
                        if v:
                            E.wait(done, 3 * (len(LEVELS) * l + v - 1) + 2)
                        copy(lane(l, KP[v % 2], w, z), lane(l, kg, w, z)).then_inc(S["lvcp"], 1)
                for b in range(4):
                    E.next("kgt")
                    E.step(copy(kg_tok[:, b // 2, b % 2], ps[4 + b][:].rearrange("p (j k) -> p j k", j=NT)), "kgt_ev")
                for j in range(nt2):
                    E.next("omm")
                    E.step(copy(osb[:, j, :], ps[j][:, 0:256]), "o_ev")
                for j in range(nt2):
                    E.next("otr")
                    dst = actT[:, 0:2, :]
                    if l == 0:
                        s_, i0 = j // 2, 2 * (j % 2)
                        dst = dst.rearrange("p c (i s t) -> p c i s t", i=4, s=2)[:, :, i0:i0 + 2, s_, :]
                        src = ps[4 + j][:, 0:256].rearrange("p (c i t) -> p c i t", c=2, i=2)
                    else:
                        dst = dst[:, :, j * P:(j + 1) * P]
                        src = ps[4 + j][:, 0:256].rearrange("p (c t) -> p c t", c=2)
                    E.step(copy(dst, src), "omix")
                for i in range(nt2):
                    E.next("xdone")
                    E.step(A(junk2, x_sb[:, (i if l == 0 else 2 * i), :], ACT.Square, accum_out=ss[:, i:i + 1]), "sqs")
                htile = [0]
                ht_evac(nt2, False)
                if l == 0:
                    norm_gain(1, "norm1_g", (0,))
                E.next("lg")
                E.step(A(rtmp[:, 0:nt2 * NE], ps[4][:, 0:nt2 * NE], ACT.Sigmoid), "sig")
                GB, UB, AB, X0, X1, D0, D1 = 0, 1, 2, 3, 4, 5, 6
                b17, b16 = (NE + 1) * l, NE * l

                def w_rounded(i, u, m):
                    act.wait_ge(ml[m], i * 32 + 16 * (b16 + u + 1))
                    act.wait_ge(S["moe_used"], i * 12 + ((UNITS + 4) * l + 6 * u + m + 1))
                    copy(split[:, PLACE[(6 * u + m) % 4], 0, :], raw[m // 2][:, m % 2 * (SLAB // 2):(m % 2 + 1) * (SLAB // 2)]
                         ).then_inc(S["w_round"], 1)
                def x_rounded(i, u, h):
                    act.wait_ge(S["xtr2" if h else "xtr"], i * 2 + (b17 + u + 1))
                    copy(xs[:, 0, 4 * h:4 * h + 4, :], ps[X0 + h][:].rearrange("p (k s) -> p k s", k=4)).then_inc(S["x_round"], 1)

                def expert_act(i, u, more):
                    for m in (3, 4):
                        w_rounded(i, u, m)
                    act.wait_ge(S["moe_used"], i * 12 + ((UNITS + 4) * l + 6 * u + 6))
                    A(sgl, ps[GB][:], ACT.Silu).then_inc(S["silu"], 1)
                    w_rounded(i, u, 5)
                    x_rounded(i, u + 1, 0)
                    act.wait_ge(S["atr"], i * 2 + (b16 + u + 1))
                    copy(acs[:, 0], ps[AB][:].rearrange("p (k s) -> p k s", k=KF)).then_inc(S["a_round"], 1)
                    x_rounded(i, u + 1, 1)
                    if more:
                        for m in range(3):
                            w_rounded(i, u + 1, m)
                    act.wait_ge(S["moe_used"], i * 12 + ((UNITS + 4) * l + 6 * u + 10))
                    act.wait_ge(S["ystore"], i * 32 + 16 * (b16 + u + 1))
                    copy(y_e[:, 0:512], ps[D0][:]).then_inc(S["y_a"], 1)
                w_rounded(0, 0, 0)
                E.wait("slab_used", RING_LOOP[l] - 1)
                w_rounded(0, 0, 1)
                for h in range(2):
                    x_rounded(0, 0, h)
                E.wait("slab_used", RING_LOOP[l])
                w_rounded(0, 0, 2)
                act.sem_inc(S["y_a"], 1)
                E.wait("scat", 16 * 2 * (NT if l == 0 else NT + SEQ // P))
                if l == 0:
                    bias(1, 2, 5)
                    E.wait("gnb", 48)
                    norm_gain(1, "norm1_g", (1,))
                    gains(1)
                with act.Fori(0, NE // 2 - 1) as i:
                    for u in range(2):
                        expert_act(i, u, True)
                for u in range(2):
                    expert_act(NE // 2 - 1, u, u == 0)
                with long_lists(act, l):
                    O, nj = LONG[l], tiles_of(l)
                    with act.Fori(0, NE) as e:
                        for j in range(nj):
                            act.wait_ge(O["gu"], e * nj + (j + 1))
                            A(sgl, ps[GB][:], ACT.Silu).then_inc(O["silu"], 1)
                for i in range(nt2):
                    act.wait_ge(gats[i], 32 * (l + 1))
                    A(yg[:, i, 0, :], yg[:, i, 0, :], ACT.Copy, scale=wts[:, 0, i:i + 1]).then_inc(S["comb_a"], 1)

        @block.vector
        def _(dve):
            E = Eng(dve)
            v = nc.vector

            def st(ins):
                E.step(ins, "vstep")

            def tt(o, a, b, op, name="vstep"):
                E.step(v.tensor_tensor(o, a, b, op), name)
            def conditioning(a, c, name="vstep"):
                E.step(v.tensor_copy(cmix[:, :, 64 * a:64 * a + 64], cond[:, c, :].unsqueeze(2).broadcast_to([P, KD, 64])), name)

            def mod_out(l, s):
                seg, half = s // 2, s % 2
                biases = {(0, 0): 1, (0, 4): 2, (1, 0): 3, (1, 4): 4, (1, 10): 5}
                if (l, s) in biases:
                    E.wait("modb", 16 * biases[l, s])
                if (l, s) == (0, 2):
                    E.wait("gn_in", 16)
                if (l, s) in ((1, 2), (1, 3)):
                    E.wait("gnb", 16 * (s + 1))
                if s == 8:
                    E.wait("gnb", 32 + 64 * l)
                E.wait("slab_used", used(("m", l, s)))
                dst = mod[:, seg, 512 * half:512 * half + 512]
                tt(dst, ps[mod_bank(l, s)][:], dst, ALU.add, "mod_ev")
                if seg in (1, 4):
                    gain = gn[:, 0, 512 * half:512 * half + 512] if (l, seg) == (0, 1) else \
                        gn_half_1 if (l, s) == (1, 3) else gn_half[half]
                    st(v.scalar_tensor_tensor(out=dst, in0=dst, scalar=1.0, in1=gain, op0=ALU.add, op1=ALU.mult))
                if (l, s) == (1, 3):
                    conditioning(1, 0, "condm")

            E.next("condx")
            conditioning(0, 0)
            conditioning(1, 1, "condm")
            E.wait("lb_in", 32)
            tt(lbe[:, 8:12], lbr[:, 0, :], lbr[:, 1, :], ALU.max)
            tt(lbe[:, 0:4], lbr[:, 0, :], lbe[:, 8:12], ALU.subtract)
            tt(lbe[:, 4:8], lbr[:, 1, :], lbe[:, 8:12], ALU.subtract, "lbd")
            E.next("lbx")
            tt(lbe[:, 8:12], lbe[:, 0:4], lbe[:, 4:8], ALU.add)
            st(v.reciprocal(lbe[:, 12:16], lbe[:, 8:12]))
            tt(lbe[:, 0:4], lbe[:, 0:4], lbe[:, 12:16], ALU.mult)
            tt(lbe[:, 4:8], lbe[:, 4:8], lbe[:, 12:16], ALU.mult)
            tt(lb[:, 0, :], lbe[:, 0:4], lbe[:, 0:4], ALU.subtract)
            tt(lb[:, 1, :], lbe[:, 0:4], lbe[:, 4:8], ALU.add)
            tt(lb[:, 1, :], lb[:, 1, :], lbe[:, 0:4], ALU.subtract)
            st(v.tensor_scalar(lb[:], lb[:], 1e-30, None, ALU.max))
            st(v.tensor_scalar(oml[:], lb[:], -1.0, 1.0, ALU.mult, ALU.add))
            for l in range(L):
                nt2 = NT if l == 0 else SEQ // P
                if l == 0:
                    for s in range(4):
                        mod_out(0, s)

                def norm_rows(n, ts, seg):
                    E.next("sqs", n)
                    E.step(v.tensor_scalar(ss[:, 0:n], ss[:, 0:n], 1.0 / D, EPS, ALU.mult, ALU.add), "rstd_d")
                    E.next("rstd_p")
                    for i in range(n):
                        st(v.scalar_tensor_tensor(out=rows[:, i, :], in0=x_sb[:, ts[i], :], scalar=rstd[:, i:i + 1],
                                                  in1=mod[:, seg + 1, :], op0=ALU.mult, op1=ALU.mult))
                        tt(rows[:, i, :], rows[:, i, :], mod[:, seg, :], ALU.add, "rows_d")
                norm_rows(NT, range(NT), 0)
                if l == 0:
                    E.wait("consts", NCONST)
                    st(v.tensor_copy(masks[:].rearrange("p a b -> p (a b)"), masks_f))
                mod_out(l, 4 if l == 0 else 7)
                E.wait("gains", 16 * NGAIN * (l + 1))
                def qk_stats():
                    tt(sqk, qkv[:, :, 0:QK], qkv[:, :, 0:QK], ALU.mult)
                    st(v.tensor_reduce(ssq, sqk.rearrange("p j (h d) -> p j h d", d=HD), AX, ALU.add))
                    E.step(v.tensor_scalar(ssq, ssq, 1.0 / HD, EPS, ALU.mult, ALU.add), "kq_d")

                def qk_made(j):
                    qk = qkv[:, j, 0:QK].rearrange("p (h d) -> p h d", d=HD)
                    tt(qk, qk, rsq[:, j, :].unsqueeze(2).broadcast_to([P, 10, HD]), ALU.mult)
                    gq, gk = (gain_qk[:, a, :].unsqueeze(1) for a in range(2))
                    oq = qkr[:, j % 2, 0:512].rearrange("p (c g d) -> p g c d", g=2, d=HD)
                    ok = qkr[:, j % 2, 512:QK].rearrange("p (h d) -> p h d", d=HD)
                    if j >= 2:
                        E.wait("qkt", NT * l + j - 1)
                    if j >= SEQ // P:
                        for g2 in range(2 if l == 0 else 0):
                            tt(oq[:, g2], qk[:, 4 * g2:4 * g2 + 4, :], gq.broadcast_to([P, 4, HD]), ALU.mult)
                        tt(ok, qk[:, 8:10, :], gk.broadcast_to([P, 2, HD]), ALU.mult, "qk_d2")
                    else:
                        tt(qk[:, 0:8, :], qk[:, 0:8, :], gq.broadcast_to([P, 8, HD]), ALU.mult)
                        tt(qk[:, 8:10, :], qk[:, 8:10, :], gk.broadcast_to([P, 2, HD]), ALU.mult)
                        qp = qkv[:, j, 0:QK].rearrange("p (h e b) -> p h e b", e=HD // 2, b=2)
                        sw = swp[:, j % 2, :].rearrange("p (h e b) -> p h e b", e=HD // 2, b=2)
                        rs = rope[:, j, 1, :].rearrange("p (e b) -> p e b", b=2)
                        for b in range(2):
                            tt(sw[:, :, :, b], qp[:, :, :, 1 - b], rs[:, :, b].unsqueeze(1).broadcast_to([P, 10, HD // 2]), ALU.mult)
                        tt(qk, qk, rope[:, j, 0, :].unsqueeze(1).broadcast_to([P, 10, HD]), ALU.mult)
                        s3 = swp[:, j % 2, :].rearrange("p (h d) -> p h d", d=HD)
                        tt(oq, qk[:, 0:8, :].rearrange("p (g c) d -> p g c d", g=2),
                           s3[:, 0:8, :].rearrange("p (g c) d -> p g c d", g=2), ALU.add)
                        tt(ok, qk[:, 8:10, :], s3[:, 8:10, :], ALU.add, "qk_d2")

                for gi, (kind, a) in enumerate(PROJ[l]):
                    g_ = E.n.get("proj", 0)
                    b = ps[4 + g_ % 4]
                    E.next("proj")
                    if kind == "q":
                        E.next("sgm")
                        qz = q_t[:, a, 0:nt2 * P]
                        tt(qz, qz, b[:, 0:nt2 * P], ALU.mult, "proj_d")
                    elif kind == "f":
                        d, c = a
                        E.next("sgm")
                        o_ = oml[:, l, 2 * d + c:2 * d + c + 1]
                        l_ = lb[:, l, 2 * d + c:2 * d + c + 1]
                        fs, ks = f_t[d][:, c * 512:(c + 1) * 512], KG[d][:, c * 512:(c + 1) * 512]
                        st(v.tensor_scalar(fs, fs, o_, l_, ALU.mult, ALU.add))
                        E.step(v.tensor_scalar(ks, ks, o_, None, ALU.mult), "proj_d")
                    elif kind == "g":
                        E.next("sgm")
                        tt(g_a[:, a, :], g_a[:, a, :], b[:, 0:256], ALU.mult)
                        gv = g_a[:, a, :].rearrange("p (h d) -> p h d", h=4)
                        tt(gv, gv, gain_o[:].unsqueeze(1).broadcast_to([P, 4, HD]), ALU.mult, "proj_d")
                    elif kind == "b":
                        E.next("bpool")
                        dve.sem_inc(S["proj_d"], 1)
                        E.up("proj_d")
                    else:
                        E.next("proj_x")
                        dve.sem_inc(S["proj_d"], 1)
                        E.up("proj_d")
                    if (kind, a) == ("ck", NT - 1):
                        qk_stats()
                    if gi in QK_NORM[l]:
                        if gi == min(QK_NORM[l]):
                            E.next("qk_p")
                        qk_made(QK_NORM[l][gi])

                def mixcols(k, a, j):
                    o = actT[a:a + 64, k, :]
                    if l == 0:
                        return o.rearrange("p (i s t) -> p i s t", i=4, s=2)[:, 2 * (j % 2):2 * (j % 2) + 2, j // 2, :]
                    return o[:, j * P:(j + 1) * P]
                units = [(j, h) for j in range(nt2) for h in range(8)]
                for u in range(len(units) + 3):
                    if u < len(units):
                        j, h = units[u]
                        nk = TT if j < SEQ // P else CTX
                        g_ = E.n.get("sc", 0)
                        E.next("sc")
                        st(v.reduce_max(mx[:, u:u + 1], ps[g_ % 3][:, 0:nk], AX))
                        E.step(v.tensor_scalar(nmx[:, u:u + 1], mx[:, u:u + 1], -HD ** -0.5, None, ALU.mult), "scmax")
                    if 1 <= u <= len(units):
                        j, h = units[u - 1]
                        nk = TT if j < SEQ // P else CTX
                        g_ = E.n.get("sexp", 0)
                        E.next("sexp")
                        st(v.reciprocal(rinv[:, u - 1:u], rsum[:, u - 1:u]))
                        E.step(v.tensor_scalar(Pb[:, g_ % 4, 0:nk], Pb[:, g_ % 4, 0:nk], rinv[:, u - 1:u], None, ALU.mult), "pnorm")
                    if u - 1 in AMONG[l]:
                        mod_out(l, AMONG[l][u - 1])
                    if u >= 3:
                        j, h = units[u - 3]
                        g_ = E.n.get("pv", 0)
                        E.next("pv")
                        src = ps[5 + g_ % 2][0:64, 0:P]
                        if l == 0:
                            src = src.rearrange("p (i t) -> p i t", i=2)
                        E.step(v.tensor_copy(mixcols(4 + h // 2, 64 * (h % 2), j), src), "pv_ev")
                for c in range(2):
                    E.next("ymm")
                    if l == 0:
                        dst = actT[:, 2 + c, :].rearrange("p (i s t) -> p s i t", i=4, s=2)
                        src = ps[7][:].rearrange("p (s i t) -> p s i t", s=2, i=4)
                    else:
                        dst, src = actT[:, 2 + c, 0:SEQ], ps[7][:, 0:SEQ]
                    E.step(v.tensor_scalar(dst, src, pool_sc[:, c:c + 1], None, ALU.mult), "ymix")
                E.next("dg")
                E.next("hq")
                E.step(v.tensor_tensor(A_s[:, 0:nt2], ident[:].unsqueeze(1).unsqueeze(1).broadcast_to([P, nt2, 4, P]),
                                       ps[4][:, 0:4 * nt2].rearrange("p (j h) -> p j h", h=4).unsqueeze(3).broadcast_to([P, nt2, 4, P]),
                                       ALU.mult), "dg_ev")
                tcur, toff = f_t[0], 0
                for lv, w in enumerate(LEVELS):
                    nb = 1024 // (2 * w)
                    E.next("lvcp", 5)
                    q, tq = wanted_q(l, QF[0], tcur, w, 1, 0)
                    k = KG[0].rearrange("p (n a w) -> p n a w", a=2, w=w)
                    t = tcur.rearrange("p (n a) -> p n a", a=2)
                    tt(q, q, tq, ALU.mult, "lvdn")
                    E.next("lvcp", 1)
                    tt(k[:, :, 0, :], k[:, :, 0, :], t[:, :, 1:2].broadcast_to([P, nb, w]), ALU.mult, "lvdn")
                    tn = tots[0][:, toff:toff + nb]
                    tt(tn, t[:, :, 0], t[:, :, 1], ALU.mult, "lvdn")
                    tcur, toff = tn, toff + nb
                    if lv == 0:
                        mod_out(l, AFTER_ATTN[l])
                    for j in range(nt2):
                        E.next("lvmm")
                        E.step(v.copy_predicated(A_s[:, j], masks[:, lv, :].unsqueeze(1).broadcast_to([P, 4, P]),
                                                 ps[4 * (lv % 2) + j][:].rearrange("p (h t) -> p h t", h=4)), "lvA")
                E.wait("lvup", 3 * len(LEVELS) * (l + 1))
                E.wait("kgt_ev", 4 * (l + 1))
                for d in range(2):
                    st(v.memset(S_st[:, d, :, ORDER[d][0], :], 0.0))
                for s in range(3):
                    E.next("umm")
                    tt(U_m[:, s, :].rearrange("p (a v) -> p a v", a=4), ps[s][:].rearrange("p (a v) -> p a v", a=4),
                       headsep[:].unsqueeze(1).broadcast_to([P, 4, P]), ALU.mult)
                    for d in range(2):
                        for c in range(2):
                            j, jn = ORDER[d][s], ORDER[d][s + 1]
                            tot = tots[d][:, toff - nb + 4 * c + j:toff - nb + 4 * c + j + 1]
                            E.step(v.scalar_tensor_tensor(out=S_st[:, d, c, jn, :], in0=S_st[:, d, c, j, :], scalar=tot,
                                                          in1=U_m[:, s, (2 * d + c) * P:(2 * d + c + 1) * P],
                                                          op0=ALU.mult, op1=ALU.add), "vstep")
                dve.sem_inc(S["stv"], 1)
                for s in IN_STATES[l]:
                    mod_out(l, s)
                for j in range(nt2):
                    E.next("o_ev")
                    tt(osq[:, j, :], osb[:, j, :], osb[:, j, :], ALU.mult)
                    st(v.tensor_reduce(ssq[:, j, 0:4], osq[:, j, :].rearrange("p (h d) -> p h d", d=HD), AX, ALU.add))
                    E.step(v.tensor_scalar(ssq[:, j, 0:4], ssq[:, j, 0:4], 1.0 / HD, EPS, ALU.mult, ALU.add), "ogn")
                for j in range(nt2):
                    E.next("rd_p")
                    o3 = osb[:, j, :].rearrange("p (h d) -> p h d", d=HD)
                    tt(o3, o3, rsq[:, j, 0:4].unsqueeze(2).broadcast_to([P, 4, HD]), ALU.mult)
                    tt(osb[:, j, :], osb[:, j, :], g_a[:, j, :], ALU.mult, "o_fin")
                if l:
                    for t_ in range(SEQ // P):
                        st(v.tensor_copy(x_sb[64:128, 2 * t_, :], x_sb[0:64, 2 * t_ + 1, :]))
                for s in range(NWO):
                    for i in range(nt2):
                        g_ = E.n.get("wo", 0)
                        E.next("wo")
                        cs = slice(512 * s, 512 * s + 512)
                        tt(wtmp, ps[g_ % 4][:], mod[:, 2, cs], ALU.mult, "wo_ev")
                        xt = x_sb[:, (i if l == 0 else 2 * i), cs]
                        tt(xt, xt, wtmp, ALU.add, "xdone" if s == NWO - 1 else "vstep")
                norm_rows(nt2, [i if l == 0 else 2 * i for i in range(nt2)], 3)
                mod_out(l, BEHIND_OUT[l])
                R = cut(rtmp, 0)
                n16, n4 = nt2 * NE, nt2 * NG
                scs = R(64)[:, 0:n16]
                sel, t1, t2, oh1, oh2, msl = (R(64)[:, 0:n16] for _ in range(6))
                ohb = rtmp[:, OH0:OH0 + n16]
                m1, m2, gs, t4, ohg, tm = (rsm[:, 16 * a:16 * a + n4] for a in range(6))
                w1, w2, d1 = (wts[:, a, 0:nt2] for a in range(3))
                r3 = lambda a, n: a.rearrange("p (g e) -> p g e", e=n)
                bc = lambda a, g_, n: a.unsqueeze(2).broadcast_to([P, g_, n])
                E.next("sig")
                tt(r3(sel, NE), r3(scs, NE), rb[:].unsqueeze(1).broadcast_to([P, nt2, NE]), ALU.add)

                def first_max(dst, src, groups, n, top, tmp, red):
                    st(v.tensor_reduce(top, r3(src, n), AX, ALU.max))
                    tt(r3(tmp, n), r3(src, n), bc(top, groups, n), ALU.is_equal)
                    tt(r3(tmp, n), r3(tmp, n), rconst[:, 0:n].unsqueeze(1).broadcast_to([P, groups, n]) if n == NE else
                       rconst[:, NE - n:NE].unsqueeze(1).broadcast_to([P, groups, n]), ALU.mult)
                    st(v.tensor_reduce(red, r3(tmp, n), AX, ALU.max))
                    tt(r3(dst, n), r3(tmp, n), bc(red, groups, n), ALU.is_equal)
                first_max(t2, sel, n4, EG, m1, t1, tm)
                st(v.scalar_tensor_tensor(out=t1, in0=t2, scalar=NEG, in1=sel, op0=ALU.mult, op1=ALU.add))
                st(v.tensor_reduce(m2, r3(t1, EG), AX, ALU.max))
                tt(gs, m1, m2, ALU.add)
                first_max(ohg, gs, nt2, NG, m1[:, 0:nt2], t4, tm[:, 0:nt2])
                st(v.memset(msl, -1e4))
                st(v.copy_predicated(r3(msl, EG), bc(ohg.bitcast(i32), n4, EG), r3(sel, EG)))
                first_max(oh1, msl, nt2, NE, m1[:, 0:nt2], t1, tm[:, 0:nt2])
                st(v.scalar_tensor_tensor(out=msl, in0=oh1, scalar=NEG, in1=msl, op0=ALU.mult, op1=ALU.add))
                first_max(oh2, msl, nt2, NE, m1[:, 0:nt2], t1, tm[:, 0:nt2])
                tt(ohb, oh1, oh2, ALU.add, "ohs")
                mod_out(*ROUTER_MODS[l][0])
                for w_, o_ in ((w1, oh1), (w2, oh2)):
                    tt(t1, scs, o_, ALU.mult)
                    st(v.tensor_reduce(w_, r3(t1, NE), AX, ALU.add))
                tt(d1, w1, w2, ALU.add)
                st(v.reciprocal(d1, d1))
                tt(w1, w1, d1, ALU.mult)
                tt(w2, w2, d1, ALU.mult)
                E.next("posm")
                pos, cnt = t2, rsm[:, 0:NE]
                st(v.tensor_copy(pos, ps[5][:, 0:n16]))
                st(v.tensor_copy(cnt, ps[5][:, n16:n16 + NE]))
                ca, cb = rsm[:, 16:16 + 18], rsm[:, 48:48 + 18]
                st(v.memset(rsm[:, 16:96], 0.0))
                st(v.tensor_copy(ca[:, 1:NE], cnt[:, 0:NE - 1]))
                for sh in (1, 2, 4, 8):
                    st(v.tensor_copy(cb[:, 0:NE], ca[:, 0:NE]))
                    tt(cb[:, sh:NE], ca[:, sh:NE], ca[:, 0:NE - sh], ALU.add)
                    ca, cb = cb, ca
                off = ca[:, 0:NE]
                tt(r3(t1, NE), r3(pos, NE), off.unsqueeze(1).broadcast_to([P, nt2, NE]), ALU.add)
                for a, o_ in enumerate((oh1, oh2)):
                    tt(sel, t1, o_, ALU.mult)
                    st(v.tensor_reduce(m16[:, 0:nt2], r3(sel, NE), AX, ALU.add))
                    st(v.tensor_copy(idx[:, a, 0:nt2], m16[:, 0:nt2]))
                st(v.memset(ca[:, NE:NE + 2], 2.0 * nt2 * P))
                st(v.tensor_reduce(m16[:, 0:1], cnt, AX, ALU.max))
                st(v.tensor_copy(offs[:, NE + 2:NE + 3], m16[:, 0:1]))
                E.step(v.tensor_copy(offs[:, 0:NE + 2], ca[:, 0:NE + 2]), "slots_d")
                GB, UB, AB, X0, X1, D0, D1 = 0, 1, 2, 3, 4, 5, 6
                b17, b16 = (NE + 1) * l, NE * l
                for m in ROUTER_MODS[l][1:]:
                    mod_out(*m)
                def w_rest(i, u, m):
                    dve.wait_ge(S["w_round"], i * 12 + (UNITS * l + 6 * u + m + 1))
                    pl = PLACE[(6 * u + m) % 4]
                    v.tensor_tensor(split[:, pl, 1, :], raw[m // 2][:, m % 2 * (SLAB // 2):(m % 2 + 1) * (SLAB // 2)],
                                    split[:, pl, 0, :].bitcast(f32), ALU.subtract).then_inc(S["w_rest"], 1)

                def x_rest(i, u, h):
                    dve.wait_ge(S["x_round"], i * 4 + (2 * b17 + 2 * u + h + 1))
                    v.tensor_tensor(xs[:, 1, 4 * h:4 * h + 4, :], ps[X0 + h][:].rearrange("p (k s) -> p k s", k=4),
                                    xs[:, 0, 4 * h:4 * h + 4, :].bitcast(f32), ALU.subtract).then_inc(S["x_rest"], 1)

                def expert_dve(i, u, more):
                    for m in (3, 4, 5):
                        w_rest(i, u, m)
                    dve.wait_ge(S["moe_used"], i * 12 + ((UNITS + 4) * l + 6 * u + 8))
                    dve.wait_ge(S["silu"], i * 2 + (b16 + u + 1))
                    v.tensor_tensor(act_e, sgl, ps[UB][:], ALU.mult).then_inc(S["a_d"], 1)
                    x_rest(i, u + 1, 0)
                    dve.wait_ge(S["a_round"], i * 2 + (b16 + u + 1))
                    v.tensor_tensor(acs[:, 1], ps[AB][:].rearrange("p (k s) -> p k s", k=KF), acs[:, 0].bitcast(f32),
                                    ALU.subtract).then_inc(S["a_rest"], 1)
                    x_rest(i, u + 1, 1)
                    if more:
                        for m in range(3):
                            w_rest(i, u + 1, m)
                    dve.wait_ge(S["moe_used"], i * 12 + ((UNITS + 4) * l + 6 * u + 10))
                    dve.wait_ge(S["ystore"], i * 32 + 16 * (b16 + u + 1))
                    v.tensor_copy(y_e[:, 512:1024], ps[D1][:]).then_inc(S["y_d"], 1)
                E.wait("w_rest", UNITS * l + POOLED[l])
                for m in range(POOLED[l], 2):
                    w_rest(0, 0, m)
                for h in range(2):
                    x_rest(0, 0, h)
                w_rest(0, 0, 2)
                dve.sem_inc(S["y_d"], 1)
                with dve.Fori(0, NE // 2 - 1) as i:
                    for u in range(2):
                        expert_dve(i, u, True)
                for u in range(2):
                    expert_dve(NE // 2 - 1, u, u == 0)
                with long_lists(dve, l):
                    O, nj = LONG[l], tiles_of(l)
                    with dve.Fori(0, NE) as e:
                        for j in range(nj):
                            dve.wait_ge(O["xT"], e * nj + (j + 1))
                            for a in range(2):
                                v.tensor_copy(xeT[:, 4 * a:4 * a + 4, :], ps[X0 + a][:].rearrange("p (k s) -> p k s", k=4)).then_inc(O["xe"], 1)
                            dve.wait_ge(O["silu"], e * nj + (j + 1))
                            v.tensor_tensor(act_e, sgl, ps[UB][:], ALU.mult).then_inc(O["a"], 1)
                            dve.wait_ge(O["aT"], e * nj + (j + 1))
                            v.tensor_copy(aT, ps[AB][:].rearrange("p (k s) -> p k s", k=KF)).then_inc(O["aTe"], 1)
                            dve.wait_ge(O["y"], e * nj + (j + 1))
                            v.tensor_copy(y_e[:, 0:512], ps[D0][:]).then_inc(O["yh"], 1)
                            v.tensor_copy(y_e[:, 512:1024], ps[D1][:]).then_inc(O["ye"], 1)
                            dve.wait_ge(O["store"], e * (16 * nj) + 16 * (j + 1))
                for i in range(nt2):
                    if l == 0 and i < 3:
                        mod_out(1, 3 + i)
                    E.next("comb_a")
                    dve.wait_ge(gats[i], 32 * (l + 1))
                    E.step(v.scalar_tensor_tensor(out=yg[:, i, 0, :], in0=yg[:, i, 1, :], scalar=wts[:, 1, i:i + 1], in1=yg[:, i, 0, :],
                                                  op0=ALU.mult, op1=ALU.add), "vstep" if i % 2 else "comb_v")
                    if i % 2:
                        tt(yg[:, i, 0, :], yg[:, i, 0, :], mod[:, 5, :], ALU.mult)
                        xt = x_sb[:, (i if l == 0 else 2 * i), :]
                        tt(xt, xt, yg[:, i, 0, :], ALU.add, "comb")
                if l == 0:
                    mod_out(1, 6)


def shape_constants(seq, ne, cap):
    import numpy as np
    p = np.arange(128)
    ident = np.eye(128, dtype=np.float32)
    before = (p[:, None] < p[None, :]).astype(np.float32)
    headsep = ((p[:, None] // 64) == (p[None, :] // 64)).astype(np.float32)
    masks = np.stack([((p[:, None] // w) ^ (p[None, :] // w)) == 1 for w in (1, 2, 4, 8, 16, 32, 64)], 1).astype(np.float32)
    t = np.arange(seq)
    inv = np.float32(10000.0) ** (-np.arange(16, dtype=np.float32) / np.float32(16))
    ang = np.concatenate([(t // 64).astype(np.float32)[:, None] * inv, (t % 64).astype(np.float32)[:, None] * inv], -1)
    cos, sin = np.repeat(np.cos(ang), 2, 1), np.repeat(np.sin(ang), 2, 1)
    sin[:, 0::2] *= -1
    rope = np.stack([cos, sin], 1).reshape(seq // 128, 128, 2, 64).transpose(1, 0, 2, 3).astype(np.float32)
    invcnt = np.zeros((128, 2, seq), np.float32)
    for g, w in enumerate((2, 4, 8, 16)):
        cnt = np.minimum(t + w // 2, seq) - np.maximum(t - w // 2, 0)
        invcnt[64 * (g % 2):64 * (g % 2) + 64, g // 2] = np.float32(1) / cnt.astype(np.float32)
    router = np.broadcast_to(np.concatenate([np.arange(ne, 0, -1), cap * np.arange(ne)]).astype(np.float32), (128, 2 * ne))
    return {"k_ident": ident, "k_before": before, "k_headsep": headsep, "k_masks": masks, "k_rope": rope,
            "k_invcnt": invcnt, "k_router": router}


def kernel(**inputs):
    import numpy as _np
    import concourse.bacc as _bacc
    from concourse import mybir as _mybir
    from concourse.bass_utils import run_bass_kernel_spmd as _run

    nc = _bacc.Bacc("TRN2", target_bir_lowering=False, num_devices=1)
    named = dict(inputs)
    seq = inputs["x"].shape[1]
    lbs, psc = _np.asarray(named.pop("hgrn_lb")), _np.asarray(named.pop("pool_scale"))
    named["hgrn_lb_cols"] = lbs.reshape(lbs.shape[0], -1, 128).transpose(0, 2, 1)
    named["pool_scale_cols"] = psc.reshape(psc.shape[0], -1, 128).transpose(0, 2, 1)
    named.update(shape_constants(seq, inputs["router_w"].shape[1], seq + inputs["ctx"].shape[1]))
    arrays, T = {}, {}
    for name, a in named.items():
        a = _np.ascontiguousarray(a)
        arrays["in_" + name] = a
        T[name] = nc.dram_tensor("in_" + name, a.shape, _mybir.dt.from_np(a.dtype), kind="ExternalInput").ap()
    T["out"] = nc.dram_tensor("out_latent", inputs["x"].shape, _mybir.dt.float32, kind="ExternalOutput").ap()
    build(nc, T)
    r = _run(nc, [arrays], core_ids=[0])
    return r.results[0]["out_latent"]
```
